# Optimizing a Trainium2 kernel written in Bass

```python
import math
import jax
import jax.numpy as jnp
from jax import lax
import numpy as np

D_MODEL = 2048
BATCH = 1
SEQ = 256
DEPTH = 1

D_MIX = D_MODEL
NSA_HEADS = 16
NSA_KV = 4
NSA_REP = NSA_HEADS // NSA_KV
HEAD_DIM = 64
D_NSA = NSA_HEADS * HEAD_DIM
D_KV = NSA_KV * HEAD_DIM
CMP_STRIDE = 16
CMP_BLOCK = 2 * CMP_STRIDE
CMP_HIDDEN = 2 * HEAD_DIM
SLC_BLOCK = 64
SLC_TOPN = 16
WINDOW = 512
Q_BLOCK = 128
N_BRANCH = 3
SG_HEADS = 8
D_SG = D_MIX - D_NSA
SG_DIM = D_SG // SG_HEADS
SG_CHUNK = 128
REL_BUCKETS = 32
REL_MAX_DIST = 1024
PEER_HEADS = 8
PEER_NKEYS = 128
PEER_EXPERTS = PEER_NKEYS * PEER_NKEYS
PEER_QDIM = 256
PEER_HALF = PEER_QDIM // 2
PEER_TOPK = 16
PEER_TOKEN_BLOCK = 128
D_IN = D_NSA + 6 * D_KV + N_BRANCH * NSA_HEADS + 2 * D_SG
EPS = 1e-6
NEG = -1e30
BIG = 1e30

kernel_name = 'hymba_nsa_gmlp_peer_layer'

def gelu(x):
    return jax.nn.gelu(x, approximate=False)

def rmsnorm(x, g):
    xf = x.astype(jnp.float32)
    y = xf * lax.rsqrt(jnp.mean(xf * xf, axis=-1, keepdims=True) + EPS)
    return (y * g.astype(jnp.float32)).astype(x.dtype)

def layernorm(x, g, b):
    xf = x.astype(jnp.float32)
    mu = jnp.mean(xf, axis=-1, keepdims=True)
    var = jnp.mean(jnp.square(xf - mu), axis=-1, keepdims=True)
    y = (xf - mu) * lax.rsqrt(var + EPS)
    return (y * g.astype(jnp.float32) + b.astype(jnp.float32)).astype(x.dtype)

def rel_bucket(dist):
    n = jnp.maximum(dist, 0)
    max_exact = REL_BUCKETS // 2
    nf = jnp.maximum(n, 1).astype(jnp.float32)
    large = max_exact + (jnp.log(nf / max_exact) / math.log(REL_MAX_DIST / max_exact)
                         * (REL_BUCKETS - max_exact)).astype(jnp.int32)
    large = jnp.minimum(large, REL_BUCKETS - 1)
    return jnp.where(n < max_exact, n, large)

def compress(k, pe, w1, w2):
    b_, t_, g_, dh = k.shape
    ch = k.reshape(b_, t_ // CMP_STRIDE, CMP_STRIDE, g_, dh)
    blocks = jnp.concatenate([ch[:, :-1], ch[:, 1:]], axis=2) + pe
    nc = blocks.shape[1]
    flat = blocks.transpose(0, 1, 3, 2, 4).reshape(b_, nc, g_, CMP_BLOCK * dh)
    hid = gelu(jnp.einsum('bngf,gfh->bngh', flat, w1))
    return jnp.einsum('bngh,ghd->bngd', hid, w2)

def nsa_attention(q, kc, vc, ks, vs, kw, vw, gate, rel_table):
    b_, t_ = q.shape[:2]
    n_qb = t_ // Q_BLOCK
    n_cmp = kc.shape[1]
    n_slc = t_ // SLC_BLOCK
    top_n = min(SLC_TOPN, n_slc)
    cmp_start = jnp.arange(n_cmp) * CMP_STRIDE
    cmp_end = cmp_start + CMP_BLOCK - 1
    slc_start = jnp.arange(n_slc) * SLC_BLOCK
    overlap = ((cmp_start[:, None] < slc_start[None, :] + SLC_BLOCK)
               & (cmp_start[:, None] + CMP_BLOCK > slc_start[None, :])).astype(jnp.float32)
    ks_blk = ks.reshape(b_, n_slc, SLC_BLOCK, NSA_KV, HEAD_DIM).transpose(0, 3, 1, 2, 4)
    vs_blk = vs.reshape(b_, n_slc, SLC_BLOCK, NSA_KV, HEAD_DIM).transpose(0, 3, 1, 2, 4)
    kw_pad = jnp.pad(kw, ((0, 0), (WINDOW, 0), (0, 0), (0, 0)))
    vw_pad = jnp.pad(vw, ((0, 0), (WINDOW, 0), (0, 0), (0, 0)))
    tab = rel_table.astype(jnp.float32)
    tab_g = tab.reshape(REL_BUCKETS, NSA_KV, NSA_REP).transpose(1, 0, 2)
    bidx = jnp.arange(b_)[:, None, None, None]
    gidx = jnp.arange(NSA_KV)[None, :, None, None]
    gidx5 = jnp.arange(NSA_KV)[None, :, None, None, None]
    slc_j = jnp.arange(n_slc)

    q_blocks = q.reshape(b_, n_qb, Q_BLOCK, NSA_KV, NSA_REP, HEAD_DIM).transpose(1, 0, 2, 3, 4, 5)
    g_blocks = gate.reshape(b_, n_qb, Q_BLOCK, NSA_KV, NSA_REP, N_BRANCH).transpose(1, 0, 2, 3, 4, 5)

    def head_bias(dist):
        bb = tab[rel_bucket(dist)].transpose(2, 0, 1)
        return bb.reshape(NSA_KV, NSA_REP, dist.shape[0], dist.shape[1])

    def one_block(args):
        qb, gb, i = args
        t = i * Q_BLOCK + jnp.arange(Q_BLOCK)
        dist_c = t[:, None] - cmp_end[None, :]
        mask_c = dist_c >= 0
        s_c = jnp.einsum('bqgrd,bngd->bgrqn', qb, kc).astype(jnp.float32) + head_bias(dist_c)
        p_c = jax.nn.softmax(jnp.where(mask_c, s_c, NEG), axis=-1) * mask_c
        o_c = jnp.einsum('bgrqn,bngd->bqgrd', p_c.astype(vc.dtype), vc)
        imp = jnp.einsum('bgrqn,ns->bgqs', p_c, overlap)
        cur = t // SLC_BLOCK
        forced = (slc_j[None, :] == 0) | (slc_j[None, :] == cur[:, None]) | (slc_j[None, :] == cur[:, None] - 1)
        future = slc_start[None, :] > t[:, None]
        imp = jnp.where(future, NEG, jnp.where(forced, BIG, imp))
        _, sel = lax.top_k(imp, top_n)
        k_sel = ks_blk[bidx, gidx, sel]
        v_sel = vs_blk[bidx, gidx, sel]
        pos_s = sel[..., None] * SLC_BLOCK + jnp.arange(SLC_BLOCK)
        dist_s = t[:, None, None] - pos_s
        mask_s = dist_s >= 0
        bias_s = tab_g[gidx5, rel_bucket(dist_s)].transpose(0, 1, 2, 5, 3, 4)
        s_s = jnp.einsum('bqgrd,bgqnsd->bgqrns', qb, k_sel).astype(jnp.float32) + bias_s
        s_s = jnp.where(mask_s[:, :, :, None], s_s, NEG)
        s_s = s_s.reshape(b_, NSA_KV, Q_BLOCK, NSA_REP, top_n * SLC_BLOCK)
        p_s = jax.nn.softmax(s_s, axis=-1)
        o_s = jnp.einsum('bgqrk,bgqkd->bqgrd', p_s.astype(vs.dtype),
                         v_sel.reshape(b_, NSA_KV, Q_BLOCK, top_n * SLC_BLOCK, HEAD_DIM))
        kw_b = lax.dynamic_slice_in_dim(kw_pad, i * Q_BLOCK, Q_BLOCK + WINDOW, axis=1)
        vw_b = lax.dynamic_slice_in_dim(vw_pad, i * Q_BLOCK, Q_BLOCK + WINDOW, axis=1)
        pos_w = i * Q_BLOCK - WINDOW + jnp.arange(Q_BLOCK + WINDOW)
        dist_w = t[:, None] - pos_w[None, :]
        mask_w = (dist_w >= 0) & (dist_w < WINDOW) & (pos_w[None, :] >= 0)
        s_w = jnp.einsum('bqgrd,bkgd->bgrqk', qb, kw_b).astype(jnp.float32) + head_bias(dist_w)
        p_w = jax.nn.softmax(jnp.where(mask_w, s_w, NEG), axis=-1)
        o_w = jnp.einsum('bgrqk,bkgd->bqgrd', p_w.astype(vw.dtype), vw_b)
        return gb[..., 0:1] * o_c + gb[..., 1:2] * o_s + gb[..., 2:3] * o_w

    o = lax.map(one_block, (q_blocks, g_blocks, jnp.arange(n_qb)))
    return o.transpose(1, 0, 2, 3, 4, 5).reshape(b_, t_, D_NSA)

def spatial_gating(u, v, ln_g, ln_b, w_s, b_s):
    b_, t_ = v.shape[:2]
    u = gelu(u)
    v = layernorm(gelu(v), ln_g, ln_b)
    vc = v.reshape(b_, t_ // SG_CHUNK, SG_CHUNK, SG_HEADS, SG_DIM)
    causal = jnp.tril(jnp.ones((SG_CHUNK, SG_CHUNK), dtype=bool))
    w = jnp.where(causal, w_s, 0.0)
    mixed = jnp.einsum('hts,bnshc->bnthc', w, vc) + b_s.T[None, None, :, :, None]
    return (u * mixed.reshape(b_, t_, SG_HEADS, SG_DIM)).reshape(b_, t_, SG_HEADS * SG_DIM)

def peer(h, w_query, sub_keys, expert_u, expert_v):
    b_, t_, d_ = h.shape
    q = jnp.einsum('btd,dq->btq', h, w_query).reshape(b_, t_, PEER_HEADS, 2, PEER_HALF)
    s = jnp.einsum('bthpc,pkc->bthpk', q, sub_keys).astype(jnp.float32)
    s1, i1 = lax.top_k(s[..., 0, :], PEER_TOPK)
    s2, i2 = lax.top_k(s[..., 1, :], PEER_TOPK)
    cand = (s1[..., :, None] + s2[..., None, :]).reshape(b_, t_, PEER_HEADS, PEER_TOPK * PEER_TOPK)
    cand_id = (i1[..., :, None] * PEER_NKEYS + i2[..., None, :]).reshape(b_, t_, PEER_HEADS, PEER_TOPK * PEER_TOPK)
    top_s, pos = lax.top_k(cand, PEER_TOPK)
    ids = jnp.take_along_axis(cand_id, pos, axis=-1)
    g = jax.nn.softmax(top_s, axis=-1).astype(h.dtype)
    n_blk = (b_ * t_) // PEER_TOKEN_BLOCK
    hb = h.reshape(n_blk, PEER_TOKEN_BLOCK, d_)
    idb = ids.reshape(n_blk, PEER_TOKEN_BLOCK, PEER_HEADS * PEER_TOPK)
    gb = g.reshape(n_blk, PEER_TOKEN_BLOCK, PEER_HEADS * PEER_TOPK)

    def one(args):
        hx, e, ge = args
        a = gelu(jnp.einsum('nd,nkd->nk', hx, expert_u[e])) * ge
        return jnp.einsum('nk,nkd->nd', a, expert_v[e])

    y = lax.map(one, (hb, idb, gb))
    return y.reshape(b_, t_, d_)

def setup_inputs(seed: int = 0) -> dict:
    key = jax.random.key(seed)
    ks = jax.random.split(key, 24)
    f32 = jnp.float32
    nrm = lambda k, shape, scale: jax.random.normal(k, shape, f32) * scale
    gain = lambda k, shape: 1.0 + 0.02 * jax.random.normal(k, shape, f32)
    return {
        'x': nrm(ks[0], (BATCH, SEQ, D_MODEL), 1.0),
        'attn_norm_g': gain(ks[1], (D_MODEL,)),
        'w_in': nrm(ks[2], (D_MODEL, D_IN), D_MODEL ** -0.5),
        'q_norm_g': gain(ks[3], (HEAD_DIM,)),
        'k_norm_g': gain(ks[4], (N_BRANCH, HEAD_DIM)),
        'cmp_pe_k': nrm(ks[5], (CMP_BLOCK, NSA_KV, HEAD_DIM), 0.1),
        'cmp_w1_k': nrm(ks[6], (NSA_KV, CMP_BLOCK * HEAD_DIM, CMP_HIDDEN), (CMP_BLOCK * HEAD_DIM) ** -0.5),
        'cmp_w2_k': nrm(ks[7], (NSA_KV, CMP_HIDDEN, HEAD_DIM), CMP_HIDDEN ** -0.5),
        'cmp_pe_v': nrm(ks[8], (CMP_BLOCK, NSA_KV, HEAD_DIM), 0.1),
        'cmp_w1_v': nrm(ks[9], (NSA_KV, CMP_BLOCK * HEAD_DIM, CMP_HIDDEN), (CMP_BLOCK * HEAD_DIM) ** -0.5),
        'cmp_w2_v': nrm(ks[10], (NSA_KV, CMP_HIDDEN, HEAD_DIM), CMP_HIDDEN ** -0.5),
        'rel_bias': nrm(ks[11], (REL_BUCKETS, NSA_HEADS), 0.2),
        'sg_ln_g': gain(ks[12], (SG_HEADS, SG_DIM)),
        'sg_ln_b': nrm(ks[13], (SG_HEADS, SG_DIM), 0.02),
        'sg_w': nrm(ks[14], (SG_HEADS, SG_CHUNK, SG_CHUNK), SG_CHUNK ** -0.5),
        'sg_b': gain(ks[15], (SG_HEADS, SG_CHUNK)),
        'out_norm_nsa': gain(ks[16], (D_NSA,)),
        'out_norm_sg': gain(ks[17], (D_SG,)),
        'w_out': nrm(ks[18], (D_MIX, D_MODEL), D_MIX ** -0.5),
        'ffn_norm_g': gain(ks[19], (D_MODEL,)),
        'peer_w_query': nrm(ks[20], (D_MODEL, PEER_HEADS * PEER_QDIM), D_MODEL ** -0.5),
        'peer_sub_keys': nrm(ks[21], (2, PEER_NKEYS, PEER_HALF), PEER_HALF ** -0.5),
        'peer_u': nrm(ks[22], (PEER_EXPERTS, D_MODEL), D_MODEL ** -0.5),
        'peer_v': nrm(ks[23], (PEER_EXPERTS, D_MODEL), 0.5),
    }

def reference(x, attn_norm_g, w_in, q_norm_g, k_norm_g, cmp_pe_k, cmp_w1_k, cmp_w2_k,
              cmp_pe_v, cmp_w1_v, cmp_w2_v, rel_bias, sg_ln_g, sg_ln_b, sg_w, sg_b,
              out_norm_nsa, out_norm_sg, w_out, ffn_norm_g, peer_w_query, peer_sub_keys,
              peer_u, peer_v):
    b_, t_, _ = x.shape
    for _layer in range(DEPTH):
        h = rmsnorm(x, attn_norm_g)
        proj = jnp.einsum('btd,de->bte', h, w_in)
        cuts = []
        acc = 0
        for size in (D_NSA, D_KV, D_KV, D_KV, D_KV, D_KV, D_KV, N_BRANCH * NSA_HEADS, D_SG):
            acc += size
            cuts.append(acc)
        q, kc, vc, ks_, vs_, kw, vw, gl, u, v = jnp.split(proj, cuts, axis=-1)
        kv_shape = (b_, t_, NSA_KV, HEAD_DIM)
        q = rmsnorm(q.reshape(b_, t_, NSA_HEADS, HEAD_DIM), q_norm_g) * (HEAD_DIM ** -0.5)
        kc = rmsnorm(compress(kc.reshape(kv_shape), cmp_pe_k, cmp_w1_k, cmp_w2_k), k_norm_g[0])
        vc = compress(vc.reshape(kv_shape), cmp_pe_v, cmp_w1_v, cmp_w2_v)
        ks_ = rmsnorm(ks_.reshape(kv_shape), k_norm_g[1])
        vs_ = vs_.reshape(kv_shape)
        kw = rmsnorm(kw.reshape(kv_shape), k_norm_g[2])
        vw = vw.reshape(kv_shape)
        gate = jax.nn.sigmoid(gl.astype(jnp.float32)).reshape(b_, t_, NSA_HEADS, N_BRANCH).astype(x.dtype)
        o_nsa = nsa_attention(q, kc, vc, ks_, vs_, kw, vw, gate, rel_bias)
        o_sg = spatial_gating(u.reshape(b_, t_, SG_HEADS, SG_DIM), v.reshape(b_, t_, SG_HEADS, SG_DIM),
                              sg_ln_g, sg_ln_b, sg_w, sg_b)
        mix = jnp.concatenate([rmsnorm(o_nsa, out_norm_nsa), rmsnorm(o_sg, out_norm_sg)], axis=-1)
        x = x + jnp.einsum('btm,md->btd', mix, w_out)
        x = x + peer(rmsnorm(x, ffn_norm_g), peer_w_query, peer_sub_keys, peer_u, peer_v)
    return x


_drawn_inputs = setup_inputs


def setup_inputs(seed=0):
    import zlib

    import numpy as np

    out = dict(_drawn_inputs(seed))
    spreads = {}
    factors = {'q_norm_g': 3.16,
     'k_norm_g': 3.714,
     'sg_ln_g': 91.812,
     'sg_ln_b': 89.454,
     'sg_b': 61.911,
     'out_norm_nsa': 30.416,
     'out_norm_sg': 30.562,
     'ffn_norm_g': 16.643}
    for name, (base, spread) in spreads.items():
        noise = np.random.default_rng([zlib.crc32(name.encode()), seed]).standard_normal(out[name].shape)
        drawn = base * np.exp(spread * noise) if base else spread * noise
        out[name] = jnp.asarray(drawn.astype(out[name].dtype))
    for name, factor in factors.items():
        out[name] = (out[name] * factor).astype(out[name].dtype)
    return out
```

```python
from contextlib import ExitStack

import concourse.bass as bass
from concourse import mybir

ALU = mybir.AluOpType
ACT = mybir.ActivationFunctionType
F32 = mybir.dt.float32
U32 = mybir.dt.uint32
AX = mybir.AxisListType

P = 128
D = 2048
T = 256
TB = T // P
DC = D // P
HEADS, KV, HD = 16, 4, 64
D_NSA, D_KV, D_SG = HEADS * HD, KV * HD, 1024
SG_HEADS = 8
CMP_STRIDE = 16
CMP_BLOCK = 32
NCMP = T // CMP_STRIDE - 1
BUCKETS = 32
REP = HEADS // KV
GATES = 3 * HEADS
PEER_HEADS, TOPK, KEYS = 8, 16, 128
EPS = 1e-6
NEG = -1e30

GROUP = 512
QUADS = DC // 4
G_IN = 9
G_CMP = 2
G_OUT = D // GROUP
G_QUERY = PEER_HEADS * 2 * KEYS // GROUP
TILES = QUADS * (G_IN + G_CMP + G_OUT + G_QUERY)
T_CMP = QUADS * G_IN
T_OUT = T_CMP + QUADS * G_CMP
T_QUERY = T_OUT + QUADS * G_OUT
RING = 8
UNITS = TB * PEER_HEADS
ROWS = UNITS * TOPK
VRING = 4

C_KC, C_VC, C_KS, C_VS, C_KW, C_VW, C_Q, C_V, C_U = 0, 256, 512, 768, 1024, 1280, 1536, 2560, 3584
PROJ = 4608

SMALL = {}
_at = 0
for _name, _n in (("attn_g", DC), ("out_g", DC), ("q_g", 1), ("k_g", 3), ("sg_b", SG_HEADS), ("rel", HEADS),
                  ("w2", 2 * KV * HD), ("pe", 2 * 2 * CMP_BLOCK), ("subkeys", 2 * KEYS),
                  ("sg_w", SG_HEADS * P), ("w_gate", DC * GATES)):
    SMALL[_name] = (_at, _n)
    _at += _n
SMALL_N = _at
SPAN = 384
CONST = {}
_at = 0
for _name, _n in (("eye", P), ("iota", P), ("causal", P), ("own", REP), ("seen", 1), ("bucket", SPAN)):
    CONST[_name] = (_at, _n)
    _at += _n
CONST_N = _at


def peer_layer(nc, x, tiles, small_in, const_in, ln_g, ln_b, ffn_g, peer_u, peer_v, bias_rows, out):
    with ExitStack() as ctx:
        base = 16512

        def sb(name, offset, shape, dt=F32):
            return nc.alloc_sbuf_tensor_at(name, shape, dt, offset=base + offset)

        def sem(name):
            return ctx.enter_context(nc.semaphore(name))

        K = 1024
        ring = [sb(f"ring{s}", (s if s < 4 else s + 4) * 8 * K, [P, D]) for s in range(RING)]
        xs = sb("xs", 32 * K, [P, TB, D])
        consts = sb("consts", 48 * K, [P, CONST_N])
        stats = sb("stats", 52 * K, [P, 128])
        kv_pe = sb("kv_pe", 53 * K, [P, 2, 4, T])
        scratch = sb("scratch", 61 * K, [P, 512])
        one_i1 = sb("one_i1", 53 * K, [P, 2, 4, P])
        one_i2 = sb("one_i2", 57 * K, [P, 2, 4, P])
        kT_of = sb("kT_of", 61 * K, [P, 3, T])
        xT = sb("xT", 96 * K, [P, DC, T])
        vc_own = sb("vc_own", 96 * K, [P, KV, REP, HD])
        kcT = sb("kcT", 100 * K, [P, KV, 32])
        pc = sb("pc", 101 * K, [P, HEADS, 32])
        pcT = sb("pcT", 103 * K, [P, KV, P])
        kcs = sb("kcs", 105 * K, [P, KV, HD])
        small = sb("small", 112 * K, [P, SMALL_N])
        gates = sb("gates", 123 * K, [P, TB, GATES])
        sums = sb("sums", 123 * K + 512, [P, TB, 2, HEADS])
        proj = sb("proj", 126 * K, [P, TB, PROJ])
        h0 = sb("h0", 126 * K, [P, TB, D])
        bias = sb("bias", 162 * K, [P, HEADS, T])
        bias_rep = sb("bias_rep", 162 * K, [P, HEADS, SPAN])
        qT = sb("qT", 178 * K, [P, HEADS // 2, T])
        kT = sb("kT", 186 * K, [P, 2, KV, T])
        lnG = sb("lnG", 194 * K, [P, D_SG])
        lnB = sb("lnB", 198 * K, [P, D_SG])
        hid = sb("hid", 202 * K, [P, 2, KV, P])
        biased = sb("biased", 194 * K, [P, 2, 2, T])
        probs = sb("probs", 198 * K, [P, 2, 2, T])
        probsT = sb("probsT", 202 * K, [P, 2, 4, P])
        squares = sb("squares", 194 * K, [P, 1024])
        carried = sb("carried", 52 * K + 512, [P, 2])
        wcomb = sb("wcomb", 124 * K, [P, 2 * 8])
        hn = sb("hn", 126 * K, [P, TB, D])
        scores = sb("scores", 142 * K, [P, UNITS, 2, KEYS])
        ffnG = sb("ffnG", 158 * K, [P, D])
        queryT = sb("queryT", 166 * K, [P, 2, 4, T])
        sc = sb("sc", 178 * K, [P, 2, KEYS])
        sc_rest = sb("sc_rest", 179 * K, [P, 2, KEYS])
        cand = sb("cand", 180 * K, [P, TOPK, TOPK])
        cand_rest = sb("cand_rest", 181 * K, [P, TOPK * TOPK])
        hit = sb("hit", 182 * K, [P, 2, TOPK, TOPK])
        best = sb("best", 184 * K, [P, 2, TOPK])
        best_at = sb("best_at", 184 * K + 128, [P, 2, TOPK], U32)
        best_f = sb("best_f", 184 * K + 256, [P, 2, TOPK])
        pos = sb("pos", 184 * K + 384, [P, TOPK], U32)
        pos2 = sb("pos2", 184 * K + 448, [P, 2, TOPK], U32)
        pos_f = sb("pos_f", 184 * K + 576, [P, 2, TOPK])
        chosen = sb("chosen", 185 * K, [P, 3, TOPK])
        ids = [sb(f"ids{e}", 185 * K + 256 + 64 * e, [P, TOPK], U32) for e in range(2)]
        dots = [sb(f"dots{e}", 185 * K + 384 + 64 * e, [P, TOPK]) for e in range(2)]
        picked = sb("picked", 192 * K, [P, 3, UNITS * TOPK])
        act_in = sb("act_in", 195 * K, [P, UNITS * TOPK])
        soft = sb("soft", 196 * K, [P, UNITS * TOPK])
        spread = sb("spread", 64 * K, [P, T, KEYS])
        wcol = [sb(f"wcol{e}", 197 * K + K * e, [P, T]) for e in range(VRING)]

        bank = ctx.enter_context(nc.psum_tensor("bank", [P, 8, 512], F32))

        def par(name, rows=P):
            a, n = SMALL[name]
            return small[0:rows, a:a + n]

        def con(name, rows=P):
            a, n = CONST[name]
            return consts[0:rows, a:a + n]

        eye = con("eye")

        x_in = sem("x_in")
        small_in_s = sem("small_in")
        rows_ln = sem("rows_ln")
        rows_ffn = sem("rows_ffn")
        tile_in = [sem(f"tile_in{s}") for s in range(RING)]
        tiles_used = sem("tiles_used")
        var_ready = sem("var_ready")
        root_ready = sem("root_ready")
        squares_ready = sem("squares_ready")
        rows_scaled = sem("rows_scaled")
        turned_x = sem("turned_x")
        xT_part = sem("xT_part")
        group_out_act = sem("group_out_act")
        group_out_dve = sem("group_out_dve")
        gates_done = sem("gates_done")
        gates_exp = sem("gates_exp")
        bias_rows_done = sem("bias_rows_done")
        bias_rows_out = sem("bias_rows_out")
        bias_stored = sem("bias_stored")
        bias_in = sem("bias_in")
        kn_ready = sem("kn_ready")
        qn_ready = sem("qn_ready")
        turned_kq = sem("turned_kq")
        kq_out = sem("kq_out")
        gelu_done = sem("gelu_done")
        v_centred = sem("v_centred")
        v_ready = sem("v_ready")
        sgw_ready = sem("sgw_ready")
        mixed_done = sem("mixed_done")
        sg_out = sem("sg_out")
        turned_kv = sem("turned_kv")
        kv_pe_ready = sem("kv_pe_ready")
        hid_done = sem("hid_done")
        hid_zero = sem("hid_zero")
        hid_ready = sem("hid_ready")
        cmp_done = sem("cmp_done")
        kc_ready = sem("kc_ready")
        kc_turned = sem("kc_turned")
        kc_out = sem("kc_out")
        cmp_scored = sem("cmp_scored")
        cmp_shifted = sem("cmp_shifted")
        cmp_exp = sem("cmp_exp")
        cmp_weighed = sem("cmp_weighed")
        cmp_turned = sem("cmp_turned")
        cmp_out = sem("cmp_out")
        scored = sem("scored")
        biased_ready = sem("biased_ready")
        probs_ready = sem("probs_ready")
        probs_turned = sem("probs_turned")
        probsT_ready = sem("probsT_ready")
        valued = sem("valued")
        half_done = sem("half_done")
        half_out = sem("half_out")
        dve_step = sem("dve_step")
        choice_step = sem("choice_step")
        carry_step = sem("carry_step")
        pool_step = sem("pool_step")
        act_step = sem("act_step")
        query_out_act = sem("query_out_act")
        query_out_dve = sem("query_out_dve")
        keyed = sem("keyed")
        keyed_out_act = sem("keyed_out_act")
        keyed_out_dve = sem("keyed_out_dve")
        ids_ready = sem("ids_ready")
        row_in = [sem(f"row_in{s}") for s in range(RING)]
        rows_used = sem("rows_used")
        soft_shifted = sem("soft_shifted")
        soft_exp = sem("soft_exp")
        peer_gelu = sem("peer_gelu")
        weights_ready = sem("weights_ready")
        slots_turned = sem("slots_turned")
        slotsT_ready = sem("slotsT_ready")
        one_i1_ready = sem("one_i1_ready")
        one_i2_ready = sem("one_i2_ready")
        spread_done = sem("spread_done")
        spread_out = sem("spread_out")
        v_in = [sem(f"v_in{s}") for s in range(VRING)]
        v_used = sem("v_used")
        wcol_ready = sem("wcol_ready")
        out_ready = sem("out_ready")
        out_stored = sem("out_stored")

        N_UNITS_ATT = TB * HEADS
        x_rows = x.rearrange("(b p) d -> p b d", p=P)
        out_rows = out.rearrange("(b p) d -> p b d", p=P)
        v_tiles = peer_v.rearrange("(p j) d -> j p d", j=KEYS)

        def cols(c):
            return proj[:, :, c:c + D_KV]

        def tb_cols(b):
            return slice(b * P, (b + 1) * P)

        block = ctx.enter_context(nc.Block())

        @block.sync
        def _(sp):
            sp.dma_start(xs[:], x_rows).then_inc(x_in, 16)
            for s in range(RING):
                sp.dma_start(ring[s][:], tiles[s]).then_inc(tile_in[s], 16)
            whole = TILES // RING
            with sp.Fori(1, whole) as j:
                for s in range(RING):
                    sp.wait_ge(tiles_used, j * RING + (s + 1 - RING))
                    sp.dma_start(ring[s][:], tiles[j * RING + s]).then_inc(tile_in[s], 16)
            for s in range(TILES % RING):
                sp.wait_ge(tiles_used, whole * RING + s + 1 - RING)
                sp.dma_start(ring[s][:], tiles[whole * RING + s]).then_inc(tile_in[s], 16)
            sp.wait_ge(rows_used, ROWS)
            for s in range(VRING):
                sp.dma_start(ring[s][:], v_tiles[s]).then_inc(v_in[s], 16)
            with sp.Fori(1, KEYS // VRING) as j:
                for s in range(VRING):
                    sp.wait_ge(v_used, j * VRING + (s + 1 - VRING))
                    sp.dma_start(ring[s][:], v_tiles[j * VRING + s]).then_inc(v_in[s], 16)
            for b in range(TB):
                sp.wait_ge(out_ready, 4 * (b + 1))
                sp.dma_start(out_rows[:, b], xs[:, b]).then_inc(out_stored, 16)
            sp.wait_ge(out_stored, 16 * TB)

        @block.tensor
        def _(pe):
            def weight_tile(t):
                pe.wait_ge(tile_in[t % RING], 16 * (t // RING + 1))
                return ring[t % RING]

            def turn_rows(src, n, first_turn):
                for b in range(TB):
                    pe.wait_ge(rows_scaled, n + b + 1)
                    for k in range(DC // 4):
                        m = first_turn + b * (DC // 4) + k
                        if m >= 2:
                            pe.wait_ge(xT_part, m - 1)
                        for c in range(4):
                            mm = pe.transpose(bank[:, m % 2, c * P:(c + 1) * P], src(b, 4 * k + c), eye)
                        mm.then_inc(turned_x, 1)

            def product(t, G, q):
                w = weight_tile(t)
                for c in range(4):
                    for b in range(TB):
                        mm = pe.matmul(bank[:, 4 + 2 * (G % 2) + b], xT[:, 4 * q + c, tb_cols(b)],
                                       w[:, c * GROUP:(c + 1) * GROUP],
                                       start=(q == 0 and c == 0), stop=(q == QUADS - 1 and c == 3))
                mm.then_inc(tiles_used, 1)

            pe.wait_ge(small_in_s, 32)
            rel = par("rel", BUCKETS + 1)
            for h in range(HEADS):
                if h >= 2:
                    pe.wait_ge(bias_rows_out, h - 1)
                pe.matmul(bank[:, 2 + h % 2, 0:SPAN], rel[:, h:h + 1].broadcast_to([BUCKETS + 1, P]),
                          con("bucket", BUCKETS + 1), start=True, stop=True).then_inc(bias_rows_done, 1)

            turn_rows(lambda b, c: h0[:, b, c * P:(c + 1) * P], 0, 0)

            pe.wait_ge(xT_part, 8)
            for G in range(G_IN):
                if G >= 2:
                    pe.wait_ge(group_out_act, G - 1)
                    pe.wait_ge(group_out_dve, G - 1)
                for q in range(QUADS):
                    product(QUADS * G + q, G, q)
            w_gate = par("w_gate").rearrange("p (c n) -> p c n", c=DC)
            for b in range(TB):
                for c in range(DC):
                    mm = pe.matmul(bank[:, b, 0:GATES], xT[:, c, tb_cols(b)], w_gate[:, c, :],
                                   start=(c == 0), stop=(c == DC - 1))
                mm.then_inc(gates_done, 1)

            pe.wait_ge(kn_ready, 2)
            pe.wait_ge(bias_rows_out, HEADS)
            for b in range(TB):
                for r, c0 in enumerate((C_KS, C_KW)):
                    for gp in range(2):
                        mm = pe.transpose(bank[:, 2 + b, (2 * r + gp) * P:(2 * r + gp + 1) * P],
                                          proj[:, b, c0 + gp * P:c0 + (gp + 1) * P], eye)
                mm.then_inc(turned_kq, 1)
            pe.wait_ge(group_out_act, G_IN)
            pe.wait_ge(group_out_dve, G_IN)
            for b in range(TB):
                for k in range(4):
                    mm = pe.transpose(bank[:, 4 + b, tb_cols(k)], proj[:, b, k * P:(k + 1) * P], eye)
                mm.then_inc(turned_kv, 1)
            pe.wait_ge(qn_ready, 2)
            for b in range(TB):
                for half in range(2):
                    m = 2 * b + half
                    if m >= 2:
                        pe.wait_ge(kq_out, 8)
                    for k in range(4):
                        pr = 4 * half + k
                        mm = pe.transpose(bank[:, (6, 7, 2, 3)[m], tb_cols(k)],
                                          proj[:, b, C_Q + pr * P:C_Q + (pr + 1) * P], eye)
                    mm.then_inc(turned_kq, 1)

            pe.wait_ge(gates_exp, 2)
            pe.wait_ge(kv_pe_ready, 4)
            for kvgp in range(4):
                for ih in range(2):
                    t = T_CMP + 2 * kvgp + ih
                    w = weight_tile(t)
                    for i in range(CMP_STRIDE):
                        for e in range(2):
                            rows = slice(HD * e, HD * e + HD)
                            start_tok = CMP_STRIDE * ih + i
                            mm = pe.matmul(bank[:, e, kvgp * 16:kvgp * 16 + NCMP], w[rows, i * P:(i + 1) * P],
                                           kv_pe[rows, ih, kvgp, start_tok:start_tok + 16 * (NCMP - 1) + 1:16],
                                           start=(ih == 0 and i == 0), stop=(ih == 1 and i == CMP_STRIDE - 1))
                    mm.then_inc(tiles_used, 1)
            pe.wait_ge(hid_ready, 2)
            pe.wait_ge(kv_pe_ready, 4)
            for kvi in range(2):
                for g in range(KV):
                    w2 = par("w2").rearrange("p (k g d) -> p k g d", k=2, g=KV)
                    mm = pe.matmul(bank[:, 4, (kvi * KV + g) * HD:(kvi * KV + g + 1) * HD], hid[:, kvi, g, :],
                                   w2[:, kvi, g, :], start=True, stop=True)
            mm.then_inc(cmp_done, 1)
            pe.wait_ge(kc_ready, 1)
            for gp in range(2):
                mm = pe.transpose(bank[:, 5, gp * 32:gp * 32 + 32],
                                  kcs[0:32, 2 * gp:2 * gp + 2, :].rearrange("p g d -> p (g d)"), eye[0:32, 0:32])
            mm.then_inc(kc_turned, 1)

            pe.wait_ge(v_ready, 2)
            pe.wait_ge(sgw_ready, 1)
            pe.wait_ge(kq_out, 12)
            pe.wait_ge(hid_ready, 2)
            for h in range(SG_HEADS):
                w_s = par("sg_w").rearrange("p (h t) -> p h t", h=SG_HEADS)
                pe.matmul(bank[:, (0, 1, 2, 3)[h // 2], (h % 2) * T:(h % 2 + 1) * T], w_s[:, h, :],
                          proj[:, :, C_V + h * P:C_V + (h + 1) * P], start=True, stop=True).then_inc(mixed_done, 1)

            pe.wait_ge(sg_out, SG_HEADS)
            pe.wait_ge(kc_out, 1)
            S0, PT0, O_SEL, O_WIN, O_CMP, CMP = 0, 2, 4, 5, 6, 7

            def score(u):
                b, h = divmod(u, HEADS)
                n = (b + 1) * P
                rows = slice(HD * (h % 2), HD * (h % 2) + HD)
                if u >= 2:
                    pe.wait_ge(biased_ready, u - 1)
                pe.matmul(bank[:, S0 + u % 2, 0:2 * n], qT[rows, h // 2, tb_cols(b)],
                          kT[rows, :, h // REP, 0:n], start=True, stop=True).then_inc(scored, 1)

            def turn_probs(u):
                b, h = divmod(u, HEADS)
                pe.wait_ge(probs_ready, 2 * (u + 1))
                if u >= 2:
                    pe.wait_ge(probsT_ready, u - 1)
                for r in range(2):
                    for s in range(b + 1):
                        mm = pe.transpose(bank[:, PT0 + u % 2, tb_cols(r * (b + 1) + s)],
                                          probs[:, u % 2, r, tb_cols(s)], eye)
                mm.then_inc(probs_turned, 1)

            def value(u):
                b, h = divmod(u, HEADS)
                half = u // 8
                pe.wait_ge(probsT_ready, u + 1)
                if h % 8 == 0:
                    if half >= 1:
                        pe.wait_ge(half_out, half)
                    if h == 0:
                        pe.wait_ge(cmp_out, b + 1)
                    for g in range(2):
                        gg = 2 * (half % 2) + g
                        pe.matmul(bank[:, O_CMP, g * T:(g + 1) * T], pcT[:, gg, :],
                                  vc_own[:, gg].rearrange("p r d -> p (r d)"), start=True, stop=True)
                for r, (o, c0) in enumerate(((O_SEL, C_VS), (O_WIN, C_VW))):
                    for s in range(b + 1):
                        v0 = c0 + (h // REP) * HD
                        mm = pe.matmul(bank[:, o, (h % 8) * HD:(h % 8 + 1) * HD],
                                       probsT[:, u % 2, r * (b + 1) + s, :], proj[:, s, v0:v0 + HD],
                                       start=(s == 0), stop=(s == b))
                mm.then_inc(valued, 1)

            for u in range(N_UNITS_ATT + 2):
                if u % HEADS == 0 and u < N_UNITS_ATT:
                    b = u // HEADS
                    if b >= 1:
                        pe.wait_ge(cmp_shifted, b)
                    for odd in range(2):
                        if odd:
                            pe.wait_ge(cmp_scored, 2 * b + 1)
                        rows = slice(HD * odd, HD * odd + HD)
                        for h in range(odd, HEADS, 2):
                            mm = pe.matmul(bank[:, CMP, h * 32:h * 32 + 16], qT[rows, h // 2, tb_cols(b)],
                                           kcT[rows, h // REP, 0:16], start=True, stop=True)
                        mm.then_inc(cmp_scored, 1)
                if u < N_UNITS_ATT:
                    score(u)
                if 1 <= u <= N_UNITS_ATT:
                    turn_probs(u - 1)
                if u % HEADS == 1 and u < N_UNITS_ATT:
                    b = u // HEADS
                    pe.wait_ge(cmp_weighed, b + 1)
                    for g in range(KV):
                        mm = pe.transpose(bank[:, CMP, tb_cols(g)],
                                          pc[:, 4 * g:4 * g + 4, :].rearrange("p h n -> p (h n)"), eye)
                    mm.then_inc(cmp_turned, 1)
                if u >= 2:
                    value(u - 2)

            mix_col = lambda c: (C_Q if c < 8 else C_U - 8 * P) + c * P
            turn_rows(lambda b, c: proj[:, b, mix_col(c):mix_col(c) + P], 2, 8)
            pe.wait_ge(xT_part, 16)
            pe.wait_ge(half_out, 4)
            for k in range(G_OUT):
                G = G_IN + k
                if k >= 2:
                    pe.wait_ge(group_out_dve, G - 1)
                for q in range(QUADS):
                    product(T_OUT + QUADS * k + q, G, q)

            turn_rows(lambda b, c: hn[:, b, c * P:(c + 1) * P], 4, 16)
            pe.wait_ge(xT_part, 24)
            pe.wait_ge(group_out_dve, G_IN + G_OUT)
            subkeys = par("subkeys").rearrange("p (a k) -> p a k", a=2)

            def key_scores(k):
                pe.wait_ge(query_out_act, k + 1)
                pe.wait_ge(query_out_dve, k + 1)
                if k >= 1:
                    pe.wait_ge(keyed_out_act, k)
                    pe.wait_ge(keyed_out_dve, k)
                for b in range(TB):
                    for j in range(4):
                        mm = pe.matmul(bank[:, b, tb_cols(j)], queryT[:, k % 2, j, tb_cols(b)],
                                       subkeys[:, j % 2, :], start=True, stop=True)
                mm.then_inc(keyed, 1)

            for k in range(G_QUERY):
                if k >= 2:
                    pe.wait_ge(query_out_act, k - 1)
                    pe.wait_ge(query_out_dve, k - 1)
                for q in range(QUADS):
                    w = weight_tile(T_QUERY + QUADS * k + q)
                    for c in range(4):
                        for j in range(4):
                            mm = pe.matmul(bank[:, 4 + 2 * (k % 2) + j // 2, (j % 2) * T:(j % 2 + 1) * T],
                                           w[:, c * GROUP + j * P:c * GROUP + (j + 1) * P], xT[:, 4 * q + c, :],
                                           start=(q == 0 and c == 0 and j % 2 == 0),
                                           stop=(q == QUADS - 1 and c == 3), skip_group_check=True)
                    mm.then_inc(tiles_used, 1)
                if k >= 1:
                    key_scores(k - 1)
            key_scores(G_QUERY - 1)

            pe.wait_ge(weights_ready, 1)
            pe.wait_ge(keyed_out_act, G_QUERY)
            pe.wait_ge(keyed_out_dve, G_QUERY)
            for a in range(3):
                for b in range(TB):
                    src = picked[:, a, tb_cols(b)] if a < 2 else soft[:, tb_cols(b)]
                    mm = pe.transpose(bank[:, a // 2, (a % 2) * T + b * P:(a % 2) * T + (b + 1) * P], src, eye)
            mm.then_inc(slots_turned, 1)

            def spread_four(e):
                for j in range(4):
                    mm = pe.matmul(bank[:, 2 + e, tb_cols(j)], one_i1[:, e, j, :], one_i2[:, e, j, :],
                                   start=True, stop=True)
                mm.then_inc(spread_done, 1)

            for e in range(2):
                pe.wait_ge(one_i1_ready, e + 1)
                pe.wait_ge(one_i2_ready, e + 1)
                spread_four(e)
            with pe.Fori(1, T // 8) as i:
                for e in range(2):
                    pe.wait_ge(one_i1_ready, i * 2 + (e + 1))
                    pe.wait_ge(one_i2_ready, i * 2 + (e + 1))
                    pe.wait_ge(spread_out, i * 2 + (e - 1))
                    spread_four(e)

            def experts(s, first, last):
                for c in range(4):
                    for b in range(TB):
                        mm = pe.matmul(bank[:, 4 * b + c], wcol[s][:, tb_cols(b)], ring[s][:, c * 512:(c + 1) * 512],
                                       start=first, stop=last, skip_group_check=True)
                mm.then_inc(v_used, 1)

            pe.wait_ge(spread_out, T // 4)
            pe.wait_ge(slotsT_ready, 2)
            for s in range(VRING):
                pe.wait_ge(v_in[s], 16)
                pe.wait_ge(wcol_ready, s + 1)
                experts(s, s == 0, False)
            with pe.Fori(1, KEYS // VRING - 1) as j:
                for s in range(VRING):
                    pe.wait_ge(v_in[s], j * 16 + 16)
                    pe.wait_ge(wcol_ready, j * VRING + (s + 1))
                    experts(s, False, False)
            for s in range(VRING):
                pe.wait_ge(v_in[s], 16 * (KEYS // VRING))
                pe.wait_ge(wcol_ready, KEYS - VRING + s + 1)
                experts(s, False, s == VRING - 1)

        @block.scalar
        def _(act):
            step = [0]

            def link(ins):
                step[0] += 1
                ins.then_inc(act_step, 1)
                act.wait_ge(act_step, step[0])

            act.dma_start(small[:], small_in).then_inc(small_in_s, 16)
            act.dma_start(consts[:], const_in).then_inc(small_in_s, 16)
            act.dma_start(lnG[:], ln_g.partition_broadcast(P)).then_inc(rows_ln, 16)
            act.dma_start(lnB[:], ln_b.partition_broadcast(P)).then_inc(rows_ln, 16)

            roots = [0]

            def root(cols_):
                roots[0] += 1
                act.wait_ge(var_ready, roots[0])
                act.activation(stats[:, cols_], stats[:, cols_], ACT.Sqrt).then_inc(root_ready, 1)

            act.wait_ge(x_in, 16)
            for b in range(TB):
                act.activation(h0[:, b], xs[:, b], ACT.Square, accum_out=stats[:, b:b + 1]).then_inc(squares_ready, 1)
            root(slice(0, 2))
            for h in range(HEADS):
                act.wait_ge(bias_rows_done, h + 1)
                act.copy(bias_rep[:, h], bank[:, 2 + h % 2, 0:SPAN]).then_inc(bias_rows_out, 1)
            act.wait_ge(bias_rows_out, HEADS)
            act.dma_start(bias_rows.rearrange("p h m -> p (h m)"),
                          bias_rep[:].rearrange("p h m -> p (h m)")).then_inc(bias_stored, 16)
            act.wait_ge(bias_stored, 16)
            act.dma_start(bias[:], bass.AP(bias_rows.tensor, P - 1, [[HEADS * SPAN - 1, P], [SPAN, HEADS], [1, T]]))\
               .then_inc(bias_in, 16)

            def group_out(G):
                act.wait_ge(tiles_used, QUADS * (G + 1))
                act.copy(proj[:, 0, G * GROUP:(G + 1) * GROUP], bank[:, 4 + 2 * (G % 2)]).then_inc(group_out_act, 1)

            for G in range(G_IN):
                group_out(G)
                if G == 3:
                    root(slice(8, 24))
                if G == 5:
                    root(slice(24, 56))
                if G == 6:
                    act.wait_ge(group_out_act, 7)
                    act.wait_ge(group_out_dve, 7)
                    act.activation(proj[:, :, C_V:C_V + D_SG], proj[:, :, C_V:C_V + D_SG], ACT.Gelu)\
                       .then_inc(gelu_done, 1)
            act.wait_ge(group_out_act, 9)
            act.wait_ge(group_out_dve, 9)
            act.activation(proj[:, :, C_U:C_U + D_SG], proj[:, :, C_U:C_U + D_SG], ACT.Gelu).then_inc(gelu_done, 1)
            root(slice(56, 72))
            for b in range(TB):
                act.wait_ge(gates_done, b + 1)
                act.activation(gates[:, b], bank[:, b, 0:GATES], ACT.Exp, scale=-1.0).then_inc(gates_exp, 1)
            act.wait_ge(tiles_used, T_OUT)
            act.wait_ge(hid_zero, 1)
            hid_v = hid[:].rearrange("p k (a e) (r n) -> p e (k a) r n", e=2, n=32)
            for e in range(2):
                for kvgp in range(4):
                    src = bank[:, e, kvgp * 16:kvgp * 16 + NCMP].rearrange("p (o n) -> p o n", o=1)
                    ins = act.activation(hid_v[:, e, kvgp, :, 0:NCMP], src.broadcast_to([P, 4, NCMP]), ACT.Gelu)
                ins.then_inc(hid_ready, 1)
            root(slice(72, 76))

            def cmp_exps(b):
                act.wait_ge(cmp_shifted, b + 1)
                nv = 7 if b == 0 else NCMP
                act.activation(pc[:, :, 0:nv], pc[:, :, 0:nv], ACT.Exp).then_inc(cmp_exp, 1)

            def exps(u):
                b, h = divmod(u, HEADS)
                n = (b + 1) * P
                act.wait_ge(biased_ready, u + 1)
                if u >= 2:
                    act.wait_ge(probs_turned, u - 1)
                for r in range(2):
                    act.activation(probs[:, u % 2, r, 0:n], biased[:, u % 2, r, 0:n], ACT.Exp,
                                   bias=stats[:, 80 + 2 * (u % 2) + r:81 + 2 * (u % 2) + r],
                                   accum_out=sums[:, b, r, h:h + 1]).then_inc(probs_ready, 1)

            def probsT_copy(u):
                b, h = divmod(u, HEADS)
                act.wait_ge(probs_turned, u + 1)
                if u >= 2:
                    act.wait_ge(valued, u - 1)
                n = 2 * (b + 1)
                act.copy(probsT[:, u % 2, 0:n].rearrange("p a t -> p (a t)"), bank[:, 2 + u % 2, 0:n * P])\
                   .then_inc(probsT_ready, 1)

            for u in range(N_UNITS_ATT + 1):
                if u < N_UNITS_ATT:
                    if u % HEADS == 0:
                        cmp_exps(u // HEADS)
                    exps(u)
                if u >= 1:
                    probsT_copy(u - 1)

            for b in range(TB):
                act.wait_ge(half_out, 2 * (b + 1))
                act.wait_ge(sg_out, SG_HEADS)
                for k, c0 in enumerate((C_Q, C_U)):
                    if b or k:
                        act.wait_ge(squares_ready, TB + 2 * b + k)
                    act.activation(squares[:], proj[:, b, c0:c0 + 1024], ACT.Square,
                                   accum_out=stats[:, 84 + 2 * b + k:85 + 2 * b + k]).then_inc(squares_ready, 1)
            root(slice(84, 88))
            act.wait_ge(xT_part, 16)
            act.dma_start(ffnG[:], ffn_g.partition_broadcast(P)).then_inc(rows_ffn, 16)
            for b in range(TB):
                act.wait_ge(group_out_dve, G_IN + G_OUT)
                act.activation(hn[:, b], xs[:, b], ACT.Square, accum_out=stats[:, 88 + b:89 + b])\
                   .then_inc(squares_ready, 1)
            root(slice(88, 90))
            for k in range(G_QUERY):
                act.wait_ge(tiles_used, T_QUERY + QUADS * (k + 1))
                if k >= 2:
                    act.wait_ge(keyed, k - 1)
                act.copy(queryT[:, k % 2, 0:2].rearrange("p j t -> p (j t)"), bank[:, 4 + 2 * (k % 2)])\
                   .then_inc(query_out_act, 1)
                act.wait_ge(keyed, k + 1)
                act.copy(scores[:, 2 * k:2 * k + 2].rearrange("p u a k -> p (u a k)"), bank[:, 0])\
                   .then_inc(keyed_out_act, 1)

            act.wait_ge(soft_shifted, 1)
            act.activation(soft[:], soft[:], ACT.Exp).then_inc(soft_exp, 1)
            act.activation(act_in[:], act_in[:], ACT.Gelu).then_inc(peer_gelu, 1)

            def spread_copy(e, token):
                act.copy(spread[:, bass.ds(token, 4), :].rearrange("p t k -> p (t k)"), bank[:, 2 + e])\
                   .then_inc(spread_out, 1)

            with act.Fori(0, T // 8) as i:
                for e in range(2):
                    act.wait_ge(spread_done, i * 2 + (e + 1))
                    spread_copy(e, i * 8 + 4 * e)

        @block.vector
        def _(dve):
            step = [0]

            def link(ins):
                step[0] = step[0] + 1
                ins.then_inc(dve_step, 1)
                dve.wait_ge(dve_step, step[0])

            choice = [0]

            def link_choice(ins):
                choice[0] += 1
                ins.then_inc(choice_step, 1)
                dve.wait_ge(choice_step, choice[0])

            roots = [0]

            def rstd(c, count):
                roots[0] += 1
                dve.tensor_scalar(stats[:, c], stats[:, c], 1.0 / count, EPS, ALU.mult, ALU.add).then_inc(var_ready, 1)
                dve.wait_ge(root_ready, roots[0])
                link(dve.reciprocal(stats[:, c], stats[:, c]))

            dve.wait_ge(squares_ready, TB)
            rstd(slice(0, 2), D)
            for b in range(TB):
                dve.tensor_scalar(h0[:, b], xs[:, b], stats[:, b:b + 1], None, ALU.mult).then_inc(rows_scaled, 1)

            def take_turned(n, gain):
                for b in range(TB):
                    for k in range(DC // 4):
                        m = n + b * (DC // 4) + k
                        dve.wait_ge(turned_x, m + 1)
                        src = bank[:, m % 2].rearrange("p (c t) -> p c t", c=4)
                        dst = xT[:, 4 * k:4 * k + 4, tb_cols(b)]
                        if gain is None:
                            dve.tensor_copy(dst, src).then_inc(xT_part, 1)
                        else:
                            g = gain[:, 4 * k:4 * k + 4].rearrange("p (c o) -> p c o", o=1).broadcast_to([P, 4, P])
                            dve.tensor_tensor(dst, src, g, ALU.mult).then_inc(xT_part, 1)

            dve.wait_ge(small_in_s, 32)
            take_turned(0, par("attn_g"))

            def group_out(G):
                dve.wait_ge(tiles_used, QUADS * (G + 1))
                dve.tensor_copy(proj[:, 1, G * GROUP:(G + 1) * GROUP], bank[:, 5 + 2 * (G % 2)])\
                   .then_inc(group_out_dve, 1)

            for G in range(3):
                group_out(G)
            dve.wait_ge(group_out_act, 3)
            dve.wait_ge(group_out_dve, 3)
            k_both = lambda b: proj[:, b, C_KS:C_KS + 1024].rearrange("p (r n) -> p r n", r=2)[:, :, 0:D_KV]
            k_stat = lambda b: stats[:, 8 + 8 * b:16 + 8 * b]
            for b in range(TB):
                link(dve.tensor_tensor(scratch[:].rearrange("p (r n) -> p r n", r=2), k_both(b), k_both(b), ALU.mult))
                link(dve.tensor_reduce(k_stat(b), scratch[:].rearrange("p (g d) -> p g d", d=HD), AX.X, ALU.add))
            group_out(3)
            rstd(slice(8, 24), HD)
            for b in range(TB):
                for r in range(2):
                    v = proj[:, b, C_KS + 512 * r:C_KS + 512 * r + D_KV].rearrange("p (g d) -> p g d", d=HD)
                    s = stats[:, 8 + 8 * b + 4 * r:12 + 8 * b + 4 * r].rearrange("p (g o) -> p g o", o=1)
                    ins = dve.tensor_tensor(v, v, s.broadcast_to([P, KV, HD]), ALU.mult)
                ins.then_inc(kn_ready, 1)
            group_out(4)
            dve.wait_ge(group_out_act, 5)
            dve.wait_ge(group_out_dve, 5)
            for b in range(TB):
                for half in range(2):
                    q = proj[:, b, C_Q + 512 * half:C_Q + 512 * half + 512]
                    link(dve.tensor_tensor(scratch[:], q, q, ALU.mult))
                    a = 24 + 16 * b + 8 * half
                    link(dve.tensor_reduce(stats[:, a:a + 8], scratch[:].rearrange("p (g d) -> p g d", d=HD),
                                           AX.X, ALU.add))
            group_out(5)
            rstd(slice(24, 56), HD)
            for b in range(TB):
                v = proj[:, b, C_Q:C_Q + D_NSA].rearrange("p (h d) -> p h d", d=HD)
                s = stats[:, 24 + 16 * b:40 + 16 * b].rearrange("p (h o) -> p h o", o=1)
                dve.tensor_tensor(v, v, s.broadcast_to([P, HEADS, HD]), ALU.mult).then_inc(qn_ready, 1)
            group_out(6)
            dve.wait_ge(gelu_done, 1)
            for b in range(TB):
                v = proj[:, b, C_V:C_V + D_SG].rearrange("p (h c) -> p h c", c=P)
                mean = stats[:, 92 + 8 * b:100 + 8 * b]
                link(dve.tensor_reduce(mean, v, AX.X, ALU.add))
                link(dve.tensor_scalar(mean, mean, 1.0 / P, None, ALU.mult))
                link(dve.tensor_tensor(v, v, mean.rearrange("p (h o) -> p h o", o=1).broadcast_to([P, SG_HEADS, P]),
                                       ALU.subtract))
            group_out(7)
            for b in range(TB):
                for half in range(2):
                    v = proj[:, b, C_V + 512 * half:C_V + 512 * half + 512]
                    link(dve.tensor_tensor(scratch[:], v, v, ALU.mult))
                    a = 56 + 8 * b + 4 * half
                    link(dve.tensor_reduce(stats[:, a:a + 4], scratch[:].rearrange("p (h c) -> p h c", c=P),
                                           AX.X, ALU.add))
            group_out(8)
            rstd(slice(56, 72), P)
            for b in range(TB):
                v = proj[:, b, C_V:C_V + D_SG].rearrange("p (h c) -> p h c", c=P)
                s = stats[:, 56 + 8 * b:64 + 8 * b].rearrange("p (h o) -> p h o", o=1)
                dve.tensor_tensor(v, v, s.broadcast_to([P, SG_HEADS, P]), ALU.mult).then_inc(v_centred, 1)
            dve.wait_ge(gates_exp, TB)
            gates_all = gates[:].rearrange("p b n -> p (b n)")
            link(dve.tensor_scalar(gates_all, gates_all, 1.0, None, ALU.add))
            link(dve.reciprocal(gates_all, gates_all))
            g_cmp = gates[:, 0, 0:GATES:3]
            link(dve.tensor_scalar(g_cmp, g_cmp, con("seen"), None, ALU.mult))

            dve.wait_ge(bias_stored, 16)
            for b in range(TB):
                dve.wait_ge(turned_kq, b + 1)
                for src_half in range(2):
                    for dst_half in range(2):
                        sr, dr = slice(64 * src_half, 64 * src_half + 64), slice(64 * dst_half, 64 * dst_half + 64)
                        src = bank[sr, 2 + b].rearrange("p (r a t) -> p r a t", r=2, a=2)
                        gain = small[sr, SMALL["k_g"][0] + 1:SMALL["k_g"][0] + 3].rearrange("p (r a o) -> p r a o", a=1, o=1)
                        dst = kT[dr, :, src_half::2, tb_cols(b)]
                        dve.tensor_tensor(dst, src, gain.broadcast_to([64, 2, 2, P]), ALU.mult).then_inc(kq_out, 1)
            pe_code = par("pe").rearrange("p (k i) -> p k i", k=4)
            for b in range(TB):
                dve.wait_ge(turned_kv, b + 1)
                for ih in range(2):
                    for k in range(4):
                        src = bank[:, 4 + b, tb_cols(k)].rearrange("p (n i) -> p n i", i=16)
                        dst = kv_pe[:, ih, k, tb_cols(b)].rearrange("p (n i) -> p n i", i=16)
                        code = pe_code[:, k, 16 * ih:16 * ih + 16].rearrange("p (o i) -> p o i", o=1)
                        ins = dve.tensor_tensor(dst, src, code.broadcast_to([P, 8, 16]), ALU.add)
                    ins.then_inc(kv_pe_ready, 1)
            for m in range(4):
                b, half = divmod(m, 2)
                dve.wait_ge(turned_kq, 3 + m)
                src = bank[:, (6, 7, 2, 3)[m]].rearrange("p (a t) -> p a t", a=4)
                dve.tensor_scalar(qT[:, 4 * half:4 * half + 4, tb_cols(b)], src, par("q_g"), HD ** -0.5,
                                  ALU.mult, ALU.mult).then_inc(kq_out, 1)

            dve.wait_ge(cmp_done, 1)
            kc_src = bank[:, 4, 0:D_KV].rearrange("p (g d) -> p g d", d=HD)
            link(dve.tensor_copy(kcs[:], kc_src))
            own = con("own").rearrange("p (r o) -> p r o", o=1).broadcast_to([P, REP, HD])
            for g in range(KV):
                src = bank[:, 4, D_KV + g * HD:D_KV + (g + 1) * HD].rearrange("p (o d) -> p o d", o=1)
                ins = dve.tensor_tensor(vc_own[:, g], src.broadcast_to([P, REP, HD]), own, ALU.mult)
            link(ins)
            sq = scratch[:, 0:D_KV].rearrange("p (g d) -> p g d", d=HD)
            link(dve.tensor_tensor(sq, kcs[:], kcs[:], ALU.mult))
            link(dve.tensor_reduce(stats[:, 72:76], sq, AX.X, ALU.add))
            rstd(slice(72, 76), HD)
            s = stats[:, 72:76].rearrange("p (g o) -> p g o", o=1)
            dve.tensor_tensor(kcs[:], kcs[:], s.broadcast_to([P, KV, HD]), ALU.mult).then_inc(kc_ready, 1)
            dve.wait_ge(kc_turned, 1)
            k0 = SMALL["k_g"][0]
            for src_half in range(2):
                for dst_half in range(2):
                    sr, dr = slice(64 * src_half, 64 * src_half + 64), slice(64 * dst_half, 64 * dst_half + 64)
                    src = bank[sr, 5, 0:64].rearrange("p (a n) -> p a n", a=2)
                    ins = dve.tensor_scalar(kcT[dr, src_half::2, :], src, small[sr, k0:k0 + 1], None, ALU.mult)
            ins.then_inc(kc_out, 1)

            for h in range(SG_HEADS):
                dve.wait_ge(mixed_done, 2 * (h // 2) + 2)
                if h == 0:
                    dve.wait_ge(gelu_done, 2)
                src = bank[:, h // 2, (h % 2) * T:(h % 2 + 1) * T].rearrange("p (b c) -> p b c", b=TB)
                u = proj[:, :, C_U + h * P:C_U + (h + 1) * P]
                a = SMALL["sg_b"][0] + h
                dve.scalar_tensor_tensor(out=u, in0=src, scalar=small[:, a:a + 1], in1=u, op0=ALU.add,
                                         op1=ALU.mult).then_inc(sg_out, 1)

            dve.wait_ge(bias_in, 16)
            link(dve.memset(pc[:], 0.0))

            def cmp_softmax(b):
                nv = 7 if b == 0 else NCMP
                first = P + CMP_BLOCK - 1 if b == 0 else CMP_BLOCK - 1
                p = pc[:, :, 0:nv]
                st = stats[:, 108:124]
                st_o = st.rearrange("p (h o) -> p h o", o=1).broadcast_to([P, HEADS, nv])
                dve.wait_ge(cmp_scored, 2 * b + 2)
                if b:
                    dve.wait_ge(cmp_turned, b)
                src = bank[:, 7].rearrange("p (h n) -> p h n", n=32)[:, :, 0:nv]
                link(dve.tensor_tensor(p, src, bias[:, :, first:first + 16 * (nv - 1) + 1:16], ALU.add))
                link(dve.tensor_reduce(st, p, AX.X, ALU.max))
                dve.tensor_tensor(p, p, st_o, ALU.subtract).then_inc(cmp_shifted, 1)

            def cmp_weigh(b):
                nv = 7 if b == 0 else NCMP
                p = pc[:, :, 0:nv]
                st = stats[:, 108:124]
                st_o = st.rearrange("p (h o) -> p h o", o=1).broadcast_to([P, HEADS, nv])
                dve.wait_ge(cmp_exp, b + 1)
                link(dve.tensor_reduce(st, p, AX.X, ALU.add))
                link(dve.reciprocal(st, st))
                link(dve.tensor_tensor(st, st, gates[:, b, 0:GATES:3], ALU.mult))
                dve.tensor_tensor(p, p, st_o, ALU.mult).then_inc(cmp_weighed, 1)

            def cmp_take(b):
                dve.wait_ge(cmp_turned, b + 1)
                if b:
                    dve.wait_ge(valued, 9)
                dve.tensor_copy(pcT[:].rearrange("p g t -> p (g t)"), bank[:, 7]).then_inc(cmp_out, 1)

            def bias_scores(u):
                b, h = divmod(u, HEADS)
                n = (b + 1) * P
                dve.wait_ge(scored, u + 1)
                if u >= 2:
                    dve.wait_ge(probs_ready, 2 * (u - 1))
                src = bank[:, u % 2, 0:2 * n].rearrange("p (r s) -> p r s", r=2)
                bb = bias[:, h, T - n:T].rearrange("p (o s) -> p o s", o=1).broadcast_to([P, 2, n])
                dst = biased[:, u % 2, :, 0:n]
                link(dve.tensor_tensor(dst, src, bb, ALU.add))
                dve.tensor_reduce(stats[:, 80 + 2 * (u % 2):82 + 2 * (u % 2)], dst, AX.X, ALU.max,
                                  negate=True).then_inc(biased_ready, 1)

            def combine(half):
                b, k = divmod(half, 2)
                dve.wait_ge(valued, 8 * (half + 1))
                hs = slice(8 * k, 8 * k + 8)
                wt = wcomb[:].rearrange("p (r h) -> p r h", r=2)
                link(dve.reciprocal(wt, sums[:, b, :, hs]))
                gt = gates[:, b].rearrange("p (h r) -> p r h", r=3)[:, 1:3, hs]
                link(dve.tensor_tensor(wt, wt, gt, ALU.mult))
                o = proj[:, b, C_Q + 512 * k:C_Q + 512 * k + 512]
                for r, dst in enumerate((o, scratch[:])):
                    src = bank[:, 4 + r].rearrange("p (h d) -> p h d", d=HD)
                    ww = wt[:, r].rearrange("p (h o) -> p h o", o=1).broadcast_to([P, 8, HD])
                    link(dve.tensor_tensor(dst.rearrange("p (h d) -> p h d", d=HD), src, ww, ALU.mult))
                link(dve.tensor_tensor(o, o, scratch[:], ALU.add))
                dve.tensor_tensor(o, o, bank[:, 6], ALU.add).then_inc(half_out, 1)

            for u in range(N_UNITS_ATT):
                if u % HEADS == 0:
                    cmp_softmax(u // HEADS)
                bias_scores(u)
                if u % HEADS == 0:
                    cmp_weigh(u // HEADS)
                if u % HEADS == 1:
                    cmp_take(u // HEADS)
                if u % 8 == 1 and u > 8:
                    combine(u // 8 - 1)
            combine(3)

            dve.wait_ge(squares_ready, TB + 4)
            rstd(slice(84, 88), 1024)
            for b in range(TB):
                for k, c0 in enumerate((C_Q, C_U)):
                    v = proj[:, b, c0:c0 + 1024]
                    ins = dve.tensor_scalar(v, v, stats[:, 84 + 2 * b + k:85 + 2 * b + k], None, ALU.mult)
                    if k == 0:
                        link(ins)
                ins.then_inc(rows_scaled, 1)
            take_turned(8, par("out_g"))
            for k in range(G_OUT):
                G = G_IN + k
                dve.wait_ge(tiles_used, T_OUT + QUADS * (k + 1))
                for b in range(TB):
                    xc = xs[:, b, k * GROUP:(k + 1) * GROUP]
                    ins = dve.tensor_tensor(xc, bank[:, 4 + 2 * (G % 2) + b], xc, ALU.add)
                    if b == 0:
                        link(ins)
                ins.then_inc(group_out_dve, 1)
            dve.wait_ge(squares_ready, TB + 4 + TB)
            rstd(slice(88, 90), D)
            dve.wait_ge(rows_ffn, 16)
            for b in range(TB):
                dve.scalar_tensor_tensor(out=hn[:, b], in0=xs[:, b], scalar=stats[:, 88 + b:89 + b], in1=ffnG[:],
                                         op0=ALU.mult, op1=ALU.mult).then_inc(rows_scaled, 1)
            take_turned(16, None)
            for k in range(G_QUERY):
                dve.wait_ge(tiles_used, T_QUERY + QUADS * (k + 1))
                if k >= 2:
                    dve.wait_ge(keyed, k - 1)
                dve.tensor_copy(queryT[:, k % 2, 2:4].rearrange("p j t -> p (j t)"), bank[:, 5 + 2 * (k % 2)])\
                   .then_inc(query_out_dve, 1)
                dve.wait_ge(keyed, k + 1)
                dve.tensor_copy(scores[:, 8 + 2 * k:10 + 2 * k].rearrange("p u a k -> p (u a k)"), bank[:, 1])\
                   .then_inc(keyed_out_dve, 1)

            dve.wait_ge(keyed_out_act, G_QUERY)
            dve.wait_ge(keyed_out_dve, G_QUERY)

            iota16 = con("iota")[:, 0:TOPK].rearrange("p (a m) -> p a m", a=1)

            def choose(u, e):
                link_choice(dve.tensor_copy(sc[:].rearrange("p a k -> p (a k)"),
                                     scores[:].rearrange("p u a k -> p (u a k)")[:, bass.ds(u * (2 * KEYS), 2 * KEYS)]))
                for a in range(2):
                    link_choice(dve.max(best[:, a, 0:8], sc[:, a]))
                    link_choice(dve.match_replace(sc_rest[:, a], best[:, a, 0:8], sc[:, a], -3.0e38))
                    link_choice(dve.max(best[:, a, 8:16], sc_rest[:, a]))
                    link_choice(dve.max_index(best_at[:, a, 0:8], best[:, a, 0:8], sc[:, a]))
                    link_choice(dve.max_index(best_at[:, a, 8:16], best[:, a, 8:16], sc_rest[:, a]))
                link_choice(dve.tensor_copy(best_f[:], best_at[:]))
                b1 = best[:, 0].rearrange("p (a o) -> p a o", o=1).broadcast_to([P, TOPK, TOPK])
                b2 = best[:, 1].rearrange("p (o b) -> p o b", o=1).broadcast_to([P, TOPK, TOPK])
                link_choice(dve.tensor_tensor(cand[:], b1, b2, ALU.add))
                flat = cand[:].rearrange("p a b -> p (a b)")
                link_choice(dve.max(chosen[:, 2, 0:8], flat))
                link_choice(dve.match_replace(cand_rest[:], chosen[:, 2, 0:8], flat, -3.0e38))
                link_choice(dve.max(chosen[:, 2, 8:16], cand_rest[:]))
                link_choice(dve.max_index(pos[:, 0:8], chosen[:, 2, 0:8], flat))
                link_choice(dve.max_index(pos[:, 8:16], chosen[:, 2, 8:16], cand_rest[:]))
                dve.tensor_scalar(pos2[:, 0], pos[:], 4, None, ALU.logical_shift_right)
                link_choice(dve.tensor_scalar(pos2[:, 1], pos[:], 15, None, ALU.bitwise_and))
                link_choice(dve.tensor_copy(pos_f[:], pos2[:]))
                for a in range(2):
                    at = pos_f[:, a].rearrange("p (j o) -> p j o", o=1).broadcast_to([P, TOPK, TOPK])
                    link_choice(dve.tensor_tensor(hit[:, a], at, iota16.broadcast_to([P, TOPK, TOPK]), ALU.is_equal))
                    val = best_f[:, a].rearrange("p (o m) -> p o m", o=1).broadcast_to([P, TOPK, TOPK])
                    link_choice(dve.tensor_tensor(hit[:, a], hit[:, a], val, ALU.mult))
                link_choice(dve.tensor_reduce(chosen[:, 0:2], hit[:], AX.X, ALU.add))
                dve.scalar_tensor_tensor(out=ids[e][:], in0=chosen[:, 0], scalar=float(KEYS), in1=chosen[:, 1],
                                         op0=ALU.mult, op1=ALU.add).then_inc(ids_ready, 1)
                dve.sem_clear(choice_step)
                choice[0] = 0
                link(dve.tensor_copy(picked[:, :, bass.ds(u * TOPK, TOPK)], chosen[:]))

            def dot_products(u, e, b):
                for k in range(TOPK):
                    s = k % RING
                    dve.wait_ge(row_in[s], u * 32 + 16 * (k // RING + 1))
                    dve.tensor_tensor_reduce(ring[s][:], ring[s][:], hn[:, b], 1.0, 0.0, ALU.mult, ALU.add,
                                             dots[e][:, k:k + 1]).then_inc(rows_used, 1)
                dve.wait_ge(rows_used, u * TOPK + TOPK)
                link(dve.tensor_copy(act_in[:, bass.ds(u * TOPK, TOPK)], dots[e][:]))

            choose(0, 0)
            per_choice = 0
            before = step[0]
            choose(1, 1)
            per_choice = step[0] - before
            dot_products(0, 0, 0)
            per_unit = step[0] - before
            done = 1
            for b, units in ((0, 7), (1, 7)):
                pairs = (units - 1) // 2 if b == 0 else 3
                start = step[0]
                with dve.Fori(0, pairs) as i:
                    step[0] = i * (2 * per_unit) + start
                    for e in range(2):
                        u = i * 2 + (done + e)
                        choose(u + 1, (done + e + 1) % 2)
                        dot_products(u, (done + e) % 2, b)
                step[0] = start + pairs * 2 * per_unit
                done += 2 * pairs
                if b == 0:
                    for bb in (0, 1):
                        choose(done + 1, (done + 1) % 2)
                        dot_products(done, done % 2, bb)
                        done += 1
            dot_products(done, done % 2, 1)

            units_v = lambda t: t.rearrange("p (u k) -> p u k", k=TOPK)
            s_all = units_v(picked[:, 2])
            top = s_all[:, :, 0:1].broadcast_to([P, UNITS, TOPK])
            dve.tensor_tensor(units_v(soft[:]), s_all, top, ALU.subtract).then_inc(soft_shifted, 1)
            dve.wait_ge(soft_exp, 1)
            st = stats[:, 108:124]
            link(dve.tensor_reduce(st, units_v(soft[:]), AX.X, ALU.add))
            link(dve.reciprocal(st, st))
            link(dve.tensor_tensor(units_v(soft[:]), units_v(soft[:]),
                                   st.rearrange("p (u o) -> p u o", o=1).broadcast_to([P, UNITS, TOPK]), ALU.mult))
            dve.wait_ge(peer_gelu, 1)
            dve.tensor_tensor(soft[:], soft[:], act_in[:], ALU.mult).then_inc(weights_ready, 1)
            dve.wait_ge(slots_turned, 1)
            dve.tensor_copy(kT_of[:, 0:2].rearrange("p a t -> p (a t)"), bank[:, 0]).then_inc(slotsT_ready, 1)
            dve.tensor_copy(kT_of[:, 2], bank[:, 1, 0:T]).then_inc(slotsT_ready, 1)
            dve.wait_ge(slotsT_ready, 2)

            def one_hots(e, token):
                for j in range(4):
                    ins = dve.tensor_scalar(one_i1[:, e, j, :], con("iota"), kT_of[:, 0, bass.ds(token + j, 1)],
                                            kT_of[:, 2, bass.ds(token + j, 1)], ALU.is_equal, ALU.mult)
                ins.then_inc(one_i1_ready, 1)
                for j in range(4):
                    ins = dve.tensor_scalar(one_i2[:, e, j, :], con("iota"), kT_of[:, 1, bass.ds(token + j, 1)],
                                            None, ALU.is_equal)
                ins.then_inc(one_i2_ready, 1)

            for e in range(2):
                one_hots(e, 4 * e)
            with dve.Fori(1, T // 8) as i:
                for e in range(2):
                    dve.wait_ge(spread_done, i * 2 + (e - 1))
                    one_hots(e, i * 8 + 4 * e)

            dve.wait_ge(spread_out, T // 4)

            def column(s, j):
                dve.tensor_copy(wcol[s][:], spread[:].rearrange("p t k -> p k t")[:, bass.ds(j, 1), :]
                                .rearrange("p o t -> p (o t)")).then_inc(wcol_ready, 1)

            for s in range(VRING):
                column(s, s)
            with dve.Fori(1, KEYS // VRING) as j:
                for s in range(VRING):
                    dve.wait_ge(v_used, j * VRING + (s + 1 - VRING))
                    column(s, j * VRING + s)
            dve.wait_ge(v_used, KEYS)
            for b in range(TB):
                for c in range(4):
                    xc = xs[:, b, c * 512:(c + 1) * 512]
                    dve.tensor_tensor(xc, bank[:, 4 * b + c], xc, ALU.add).then_inc(out_ready, 1)

        @block.gpsimd
        def _(pool):
            pool.memset(hid[:].rearrange("p k g n -> p (k g n)"), 0.0).then_inc(hid_zero, 1)
            pool.wait_ge(small_in_s, 32)
            w_s = par("sg_w").rearrange("p (h t) -> p h t", h=SG_HEADS)
            causal = con("causal").rearrange("p (o t) -> p o t", o=1).broadcast_to([P, SG_HEADS, P])
            pool.tensor_tensor(w_s, w_s, causal, ALU.mult).then_inc(sgw_ready, 1)
            pool.wait_ge(rows_ln, 32)
            for b in range(TB):
                v = proj[:, b, C_V:C_V + D_SG]
                pool.wait_ge(v_centred, b + 1)
                pool.tensor_tensor(v, v, lnG[:], ALU.mult).then_inc(pool_step, 1)
                pool.wait_ge(pool_step, b + 1)
                pool.tensor_tensor(v, v, lnB[:], ALU.add).then_inc(v_ready, 1)

            def carry(n):
                pool.wait_ge(carry_step, n)
                pool.tensor_tensor(carried[:, 0:1], carried[:, 1:2], carried[:, 1:2], ALU.add).then_inc(carry_step, 1)

            pool.memset(carried[:], 0.0).then_inc(carry_step, 1)

            def gather(u, e, n, first):
                pool.wait_ge(ids_ready, u + 1)
                carry(n)
                for k in range(TOPK):
                    if k % 4 == 0 and (not first or k >= RING):
                        pool.wait_ge(rows_used, u * TOPK + (k + 4 - RING))
                        n = n + 1
                        carry(n)
                    pool.indirect_dma_start(
                        out=ring[k % RING][:], out_offset=None, in_=peer_u,
                        in_offset=bass.IndirectOffsetOnAxis(ap=ids[e][:, k:k + 1], axis=0),
                    ).then_inc(row_in[k % RING], 16)

            pool.wait_ge(tiles_used, TILES)
            for u in range(2):
                gather(u, u, 1 + 3 * u, u == 0)
            with pool.Fori(1, UNITS // 2) as i:
                for e in range(2):
                    gather(i * 2 + e, e, i * 10 + (5 * e - 1), False)


def bucket_of(distance):
    if distance < BUCKETS // 2:
        return distance
    edges = (16, 21, 27, 35, 46, 59, 77, 99, 128, 166, 216)
    return BUCKETS // 2 - 1 + sum(distance >= e for e in edges)


def constants():
    import numpy as np

    c = np.zeros((P, CONST_N), np.float32)

    def put(name, a):
        c[:a.shape[0], CONST[name][0]:CONST[name][0] + a.shape[1]] = a

    put("eye", np.eye(P, dtype=np.float32))
    put("iota", np.tile(np.arange(P, dtype=np.float32), (P, 1)))
    put("causal", np.triu(np.ones((P, P), np.float32)))
    put("own", np.repeat(np.eye(REP, dtype=np.float32), 32, axis=0))
    put("seen", (np.arange(P) >= CMP_BLOCK - 1).astype(np.float32)[:, None])
    one = np.zeros((BUCKETS + 1, SPAN), np.float32)
    for m in range(SPAN):
        one[bucket_of(255 - m) if m <= 255 else BUCKETS, m] = 1.0
    put("bucket", one)
    return c


def kernel(x, attn_norm_g, w_in, q_norm_g, k_norm_g, cmp_pe_k, cmp_w1_k, cmp_w2_k, cmp_pe_v, cmp_w1_v, cmp_w2_v,
           rel_bias, sg_ln_g, sg_ln_b, sg_w, sg_b, out_norm_nsa, out_norm_sg, w_out, ffn_norm_g, peer_w_query,
           peer_sub_keys, peer_u, peer_v):
    import numpy as np
    import concourse.bacc as bacc
    from concourse.bass_utils import run_bass_kernel_spmd

    def groups(w):
        n = w.shape[1] // GROUP
        t = w.reshape(QUADS, 4, P, n, GROUP).transpose(3, 0, 2, 1, 4)
        return t.reshape(n * QUADS, P, 4 * GROUP)

    def cmp_tiles(w1):
        t = w1.reshape(2, 2, 2, 16, HD, P).transpose(0, 2, 1, 4, 3, 5)
        return t.reshape(4, P, 16 * P)

    w_in, w_out, w_query = (np.asarray(w) for w in (w_in, w_out, peer_w_query))
    q_end = D_NSA
    kv_end = q_end + 6 * D_KV
    g_end = kv_end + GATES
    u_end = g_end + D_SG
    main = np.concatenate([w_in[:, q_end:kv_end], w_in[:, :q_end], w_in[:, u_end:], w_in[:, g_end:u_end]], axis=1)
    tiles = np.concatenate([groups(main), cmp_tiles(np.asarray(cmp_w1_k)), cmp_tiles(np.asarray(cmp_w1_v)),
                            groups(w_out), groups(w_query)], axis=0)

    small = np.zeros((P, SMALL_N), np.float32)

    def put(name, a):
        small[:a.shape[0], SMALL[name][0]:SMALL[name][0] + a.shape[1]] = a

    put("attn_g", np.asarray(attn_norm_g).reshape(DC, P).T)
    put("out_g", np.concatenate([np.asarray(out_norm_nsa), np.asarray(out_norm_sg)]).reshape(DC, P).T)
    put("q_g", np.tile(np.asarray(q_norm_g), 2)[:, None])
    put("k_g", np.tile(np.asarray(k_norm_g), (1, 2)).T)
    put("sg_b", np.asarray(sg_b).T)
    put("rel", np.concatenate([np.asarray(rel_bias), np.full((1, HEADS), NEG, np.float32)], axis=0))
    w2 = np.stack([np.asarray(cmp_w2_k), np.asarray(cmp_w2_v)])
    put("w2", w2.transpose(2, 0, 1, 3).reshape(P, -1))
    pe = np.stack([np.asarray(cmp_pe_k), np.asarray(cmp_pe_v)])
    put("pe", pe.reshape(2, CMP_BLOCK, 2, 2, HD).transpose(3, 4, 0, 2, 1).reshape(P, -1))
    put("subkeys", np.asarray(peer_sub_keys).transpose(2, 0, 1).reshape(P, -1))
    put("sg_w", np.asarray(sg_w).transpose(2, 0, 1).reshape(P, -1))
    put("w_gate", w_in[:, kv_end:g_end].reshape(DC, P, GATES).transpose(1, 0, 2).reshape(P, -1))

    arrays = {
        "x": np.asarray(x).reshape(T, D), "tiles": tiles, "small": small, "const": constants(),
        "ln_g": np.asarray(sg_ln_g).reshape(-1), "ln_b": np.asarray(sg_ln_b).reshape(-1),
        "ffn_g": np.asarray(ffn_norm_g), "peer_u": np.asarray(peer_u), "peer_v": np.asarray(peer_v),
    }
    arrays = {f"in_{k}": np.ascontiguousarray(v) for k, v in arrays.items()}
    nc = bacc.Bacc("TRN2", target_bir_lowering=False, num_devices=1)
    args = [nc.dram_tensor(k, v.shape, mybir.dt.from_np(v.dtype), kind="ExternalInput").ap() for k, v in arrays.items()]
    bias_rows = nc.dram_tensor("bias_rows", (P, HEADS, SPAN), F32, kind="Internal").ap()
    out = nc.dram_tensor("out", (T, D), F32, kind="ExternalOutput").ap()
    peer_layer(nc, *args, bias_rows, out)
    r = run_bass_kernel_spmd(nc, [arrays], core_ids=[0])
    return r.results[0]["out"].reshape(1, T, D)
```

```python
from contextlib import ExitStack

import concourse.bass as bass
from concourse import mybir

ALU = mybir.AluOpType
ACT = mybir.ActivationFunctionType
F32 = mybir.dt.float32
F32R = mybir.dt.float32r
U32 = mybir.dt.uint32
AX = mybir.AxisListType

P = 128
D = 2048
T = 256
TB = T // P
DC = D // P
HEADS, KV, HD = 16, 4, 64
D_NSA, D_KV, D_SG = HEADS * HD, KV * HD, 1024
SG_HEADS = 8
CMP_STRIDE = 16
CMP_BLOCK = 32
NCMP = T // CMP_STRIDE - 1
BUCKETS = 32
REP = HEADS // KV
GATES = 3 * HEADS
PEER_HEADS, TOPK, KEYS = 8, 16, 128
EPS = 1e-6
NEG = -1e30

PART = 512
HALF = 2 * PART
G_IN = 9
G_OUT = D // PART
G_QUERY = PEER_HEADS * 2 * KEYS // PART
N_OUT = DC * G_IN
N_QUERY = N_OUT + DC * G_OUT
N_U = N_QUERY + DC * G_QUERY
N_V = N_U + 4 * KEYS
RAW = 4
SPLIT = 4
N_CMP = 2 * 2 * KV
CMP_RING = 3
UNITS = TB * PEER_HEADS
SOFT_AT = 44
EARLY = 48

C_KC, C_VC, C_KS, C_VS, C_KW, C_VW, C_Q, C_V, C_U = 0, 256, 512, 768, 1024, 1280, 1536, 2560, 3584
PROJ = 4608

SMALL = {}
_at = 0
for _name, _n in (("q_g", 1), ("k_g", 3), ("sg_b", SG_HEADS), ("rel", HEADS),
                  ("w2", 2 * KV * HD), ("pe", 2 * 2 * CMP_BLOCK), ("subkeys", 2 * KEYS),
                  ("sg_w", SG_HEADS * P), ("w_gate", DC * GATES)):
    SMALL[_name] = (_at, _n)
    _at += _n
SMALL_N = _at
SPAN = 384
CONST = {}
_at = 0
for _name, _n in (("eye", P), ("iota", P), ("causal", P), ("own", REP), ("seen", 1), ("bucket", SPAN)):
    CONST[_name] = (_at, _n)
    _at += _n
CONST_N = _at


def peer_layer(nc, x, tiles, cmp_tiles, u_tiles, peer_v, small_in, const_in, attn_g, out_g, ffn_g, ln_g, ln_b,
               bias_rows, resid_dram, out):
    with ExitStack() as ctx:
        base = 16512

        def sb(name, offset, shape, dt=F32):
            return nc.alloc_sbuf_tensor_at(name, shape, dt, offset=base + offset)

        def sem(name):
            return ctx.enter_context(nc.semaphore(name))

        K = 1024
        raw = [sb(f"raw{s}", s * 4 * K, [P, HALF]) for s in range(RAW)]
        hi = [sb(f"hi{s}", (16 + 2 * s) * K, [P, PART], F32R) for s in range(SPLIT)]
        lo = [sb(f"lo{s}", (24 + 2 * s) * K, [P, PART], F32R) for s in range(SPLIT)]
        consts = sb("consts", 32 * K, [P, CONST_N])
        stats = sb("stats", 35 * K + 256, [P, 128])
        A = 35 * K + 768
        picked = sb("picked", A, [P, 3, UNITS * TOPK])
        soft = sb("soft", A + 3 * K, [P, UNITS * TOPK])
        slotsT = sb("slotsT", A, [P, 3, T])
        wcol_hi = [sb(f"wcol_hi{e}", A + e * K, [P, T], F32R) for e in range(2)]
        wcol_lo = [sb(f"wcol_lo{e}", A + (2 + e) * K, [P, T], F32R) for e in range(2)]
        B = A + 4 * K
        cmp_w1 = [sb(f"cmp_w1_{s}", A + 4 * K * s, [P, HALF]) for s in range(CMP_RING)]
        sc = sb("sc", B, [P, 2, KEYS])
        sc_rest = sb("sc_rest", B + K, [P, 2, KEYS])
        cand = sb("cand", B + 2 * K, [P, TOPK, TOPK])
        cand_rest = sb("cand_rest", B + 3 * K, [P, TOPK * TOPK])
        hit = sb("hit", B + 4 * K, [P, 2, TOPK, TOPK])
        best = sb("best", B + 6 * K, [P, 2, TOPK])
        best_at = sb("best_at", B + 6 * K + 128, [P, 2, TOPK], U32)
        best_f = sb("best_f", B + 6 * K + 256, [P, 2, TOPK])
        pos = sb("pos", B + 6 * K + 384, [P, TOPK], U32)
        pos2 = sb("pos2", B + 6 * K + 448, [P, 2, TOPK], U32)
        pos_f = sb("pos_f", B + 6 * K + 576, [P, 2, TOPK])
        chosen = sb("chosen", B + 7 * K, [P, 3, TOPK])
        one_i1 = sb("one_i1", B, [P, 2, 4, P])
        one_i2 = sb("one_i2", B + 4 * K, [P, 2, 4, P])
        acted = sb("acted", B, [P, 2, T])
        C = B + 8 * K
        xT_hi = sb("xT_hi", C, [P, DC, T], F32R)
        xT_lo = sb("xT_lo", C + 16 * K, [P, DC, T], F32R)
        vc_own = sb("vc_own", C, [P, KV, REP, HD])
        kcT = sb("kcT", C + 4 * K, [P, KV, 32])
        pc = sb("pc", C + 5 * K, [P, HEADS, 32])
        pcT = sb("pcT", C + 7 * K, [P, KV, P])
        kcs = sb("kcs", C + 9 * K, [P, KV, HD])
        hid = sb("hid", C + 10 * K, [P, 2, KV, P])
        hid_rows = sb("hid_rows", C + 14 * K, [P, 2, KV * P])
        biased = sb("biased", C + 18 * K, [P, 2, 2, T])
        probs = sb("probs", C + 22 * K, [P, 2, 2, T])
        probsT = sb("probsT", C + 26 * K, [P, 2, 4, P])
        resid = sb("resid", C, [P, TB, D])
        E = C + 32 * K
        spread = sb("spread", E, [P, KEYS, T])
        xs = sb("xs", E, [P, TB, D])
        proj = sb("proj", E + 16 * K, [P, TB, PROJ])
        h0 = sb("h0", E + 16 * K, [P, TB, D])
        hn = sb("hn", E + 16 * K, [P, TB, D])
        bias = sb("bias", E + 52 * K, [P, HEADS, T])
        bias_rep = sb("bias_rep", E + 52 * K, [P, HEADS, SPAN])
        qT = sb("qT", E + 68 * K, [P, HEADS // 2, T])
        kT = sb("kT", E + 76 * K, [P, 2, KV, T])
        queryT = sb("queryT", E + 76 * K, [P, 2, 4, T])
        small = sb("small", E + 84 * K, [P, SMALL_N])
        gates = sb("gates", E + 95 * K, [P, TB, GATES])
        sums = sb("sums", E + 95 * K + 384, [P, TB, 2, HEADS])
        wcomb = sb("wcomb", E + 95 * K + 640, [P, 2 * 8])
        wg_hi = sb("wg_hi", E + 96 * K, [P, DC, GATES], F32R)
        wg_lo = sb("wg_lo", E + 99 * K, [P, DC, GATES], F32R)
        kv_pe = sb("kv_pe", E + 102 * K, [P, 2, 2, KV, T // 2])
        lnG = sb("lnG", E + 110 * K, [P, D_SG])
        lnB = sb("lnB", E + 114 * K, [P, D_SG])
        squares = sb("squares", E + 110 * K, [P, 1024])
        row_g = sb("row_g", E + 118 * K, [P, D])
        scratch = sb("scratch", E + 126 * K, [P, 512])
        scores = sb("scores", E + 112 * K, [P, UNITS, 2, KEYS])

        bank = ctx.enter_context(nc.psum_tensor("bank", [P, 8, 512], F32))

        def par(name, rows=P):
            a, n = SMALL[name]
            return small[0:rows, a:a + n]

        def con(name, rows=P):
            a, n = CONST[name]
            return consts[0:rows, a:a + n]

        eye = con("eye")

        x_in = sem("x_in")
        small_in_s = sem("small_in")
        rows_ln = sem("rows_ln")
        gain_in = sem("gain_in")
        raw_in = [sem(f"raw_in{s}") for s in range(RAW)]
        hi_ready = sem("hi_ready")
        lo_ready = sem("lo_ready")
        v_lo_ready = sem("v_lo_ready")
        parts_used = sem("parts_used")
        cmp_in = [sem(f"cmp_in{s}") for s in range(CMP_RING)]
        cmp_used = sem("cmp_used")
        xT_hi_part = sem("xT_hi_part")
        wg_hi_ready = sem("wg_hi_ready")
        wg_ready = sem("wg_ready")
        var_ready = sem("var_ready")
        root_ready = sem("root_ready")
        squares_ready = sem("squares_ready")
        rows_scaled = sem("rows_scaled")
        turned_x = sem("turned_x")
        xT_part = sem("xT_part")
        group_out_act = sem("group_out_act")
        group_out_dve = sem("group_out_dve")
        gates_done = sem("gates_done")
        gates_exp = sem("gates_exp")
        bias_rows_done = sem("bias_rows_done")
        bias_rows_out = sem("bias_rows_out")
        bias_stored = sem("bias_stored")
        bias_in = sem("bias_in")
        kn_ready = sem("kn_ready")
        qn_ready = sem("qn_ready")
        turned_kq = sem("turned_kq")
        kq_out = sem("kq_out")
        gelu_done = sem("gelu_done")
        v_centred = sem("v_centred")
        v_ready = sem("v_ready")
        sgw_ready = sem("sgw_ready")
        mixed_done = sem("mixed_done")
        sg_out = sem("sg_out")
        turned_kv = sem("turned_kv")
        kv_pe_ready = sem("kv_pe_ready")
        hid_acted = sem("hid_acted")
        hid_turned = sem("hid_turned")
        hid_zero = sem("hid_zero")
        hid_ready = sem("hid_ready")
        cmp_done = sem("cmp_done")
        kc_ready = sem("kc_ready")
        kc_turned = sem("kc_turned")
        kc_out = sem("kc_out")
        cmp_scored = sem("cmp_scored")
        cmp_shifted = sem("cmp_shifted")
        cmp_exp = sem("cmp_exp")
        cmp_weighed = sem("cmp_weighed")
        cmp_turned = sem("cmp_turned")
        cmp_out = sem("cmp_out")
        scored = sem("scored")
        biased_ready = sem("biased_ready")
        probs_ready = sem("probs_ready")
        probs_turned = sem("probs_turned")
        probsT_ready = sem("probsT_ready")
        valued = sem("valued")
        half_done = sem("half_done")
        half_out = sem("half_out")
        dve_step = sem("dve_step")
        choice_step = sem("choice_step")
        pool_step = sem("pool_step")
        query_out_act = sem("query_out_act")
        query_out_dve = sem("query_out_dve")
        keyed = sem("keyed")
        keyed_out_act = sem("keyed_out_act")
        keyed_out_dve = sem("keyed_out_dve")
        soft_shifted = sem("soft_shifted")
        soft_exp = sem("soft_exp")
        weights_ready = sem("weights_ready")
        slots_turned = sem("slots_turned")
        slotsT_ready = sem("slotsT_ready")
        one_i1_ready = sem("one_i1_ready")
        one_i2_ready = sem("one_i2_ready")
        spread_done = sem("spread_done")
        spread_weighed = sem("spread_weighed")
        spread_out = sem("spread_out")
        u_out = sem("u_out")
        u_weighed = sem("u_weighed")
        wcol_hi_ready = sem("wcol_hi_ready")
        wcol_ready = sem("wcol_ready")
        resid_stored = sem("resid_stored")
        resid_in = sem("resid_in")
        out_ready = sem("out_ready")
        out_stored = sem("out_stored")

        N_UNITS_ATT = TB * HEADS
        x_rows = x.rearrange("(b p) d -> p b d", p=P)
        out_rows = out.rearrange("(b p) d -> p b d", p=P)
        resid_rows = resid_dram.rearrange("(b p) d -> p b d", p=P)
        v_tiles = peer_v.rearrange("(p j) (h d) -> (j h) p d", j=KEYS, h=2)

        def tb_cols(b):
            return slice(b * P, (b + 1) * P)

        block = ctx.enter_context(nc.Block())

        @block.sync
        def _(sp):
            sp.dma_start(xs[:], x_rows).then_inc(x_in, 16)
            for s in range(RAW):
                sp.dma_start(raw[s][:], tiles[s]).then_inc(raw_in[s], 16)
            for s in range(CMP_RING):
                sp.dma_start(cmp_w1[s][:], cmp_tiles[s]).then_inc(cmp_in[s], 16)
            sp.wait_ge(bias_rows_out, HEADS)
            sp.dma_start(bias_rows.rearrange("p h m -> p (h m)"),
                         bias_rep[:].rearrange("p h m -> p (h m)")).then_inc(bias_stored, 16)
            sp.wait_ge(bias_stored, 16)
            sp.dma_start(bias[:], bass.AP(bias_rows.tensor, P - 1, [[HEADS * SPAN - 1, P], [SPAN, HEADS], [1, T]]))\
              .then_inc(bias_in, 16)
            def load(src, i, s, first):
                sp.wait_ge(lo_ready, i * (2 * RAW) + (first + 2 * (s + 1 - RAW)))
                sp.dma_start(raw[s][:], src[i * RAW + s]).then_inc(raw_in[s], 16)

            with sp.Fori(1, N_OUT // (2 * RAW) + 1) as i:
                for s in range(RAW):
                    load(tiles, i, s, 0)
            for k in range(CMP_RING, N_CMP):
                sp.wait_ge(cmp_used, k + 1 - CMP_RING)
                sp.dma_start(cmp_w1[k % CMP_RING][:], cmp_tiles[k]).then_inc(cmp_in[k % CMP_RING], 16)
            with sp.Fori(N_OUT // (2 * RAW) + 1, N_U // (2 * RAW)) as i:
                for s in range(RAW):
                    load(tiles, i, s, 0)
            with sp.Fori(0, 2 * KEYS // RAW) as i:
                for s in range(RAW):
                    load(u_tiles, i, s, N_U)
            for s in range(RAW):
                load(v_tiles, 0, s, N_V)
            sp.wait_ge(parts_used, N_V)
            sp.dma_start(resid[:], resid_rows).then_inc(resid_in, 16)
            with sp.Fori(1, 2 * KEYS // RAW) as i:
                for s in range(RAW):
                    sp.wait_ge(v_lo_ready, i * (2 * RAW) + 2 * (s + 1 - RAW))
                    sp.dma_start(raw[s][:], v_tiles[i * RAW + s]).then_inc(raw_in[s], 16)
            for b in range(TB):
                sp.wait_ge(out_ready, 4 * (b + 1))
                sp.dma_start(out_rows[:, b], resid[:, b]).then_inc(out_stored, 16)
            sp.wait_ge(out_stored, 16 * TB)

        @block.tensor
        def _(pe):
            def split_part(n):
                pe.wait_ge(lo_ready, n + 1)
                return hi[n % SPLIT][:], lo[n % SPLIT][:]

            def passes(out_, left, right, start, stop):
                pe.matmul(out_, left[0], right[0], start=start, stop=False, skip_group_check=True)
                pe.matmul(out_, left[0], right[1], start=False, stop=False, skip_group_check=True)
                return pe.matmul(out_, left[1], right[0], start=False, stop=stop, skip_group_check=True)

            def turn_rows(src, n, first_turn):
                for b in range(TB):
                    pe.wait_ge(rows_scaled, n + b + 1)
                    for k in range(DC // 4):
                        m = first_turn + b * (DC // 4) + k
                        if m >= 2:
                            pe.wait_ge(xT_part, m - 1)
                        for c in range(4):
                            mm = pe.transpose(bank[:, m % 2, c * P:(c + 1) * P], src(b, 4 * k + c), eye)
                        mm.then_inc(turned_x, 1)

            def product(G, k):
                w = split_part(DC * G + k)
                for b in range(TB):
                    mm = passes(bank[:, 4 + 2 * (G % 2) + b], [xT_hi[:, k, tb_cols(b)], xT_lo[:, k, tb_cols(b)]],
                                w, start=(k == 0), stop=(k == DC - 1))
                mm.then_inc(parts_used, 1)

            pe.wait_ge(small_in_s, 32)
            rel = par("rel", BUCKETS + 1)
            for h in range(HEADS):
                if h >= 2:
                    pe.wait_ge(bias_rows_out, h - 1)
                pe.matmul(bank[:, 2 + h % 2, 0:SPAN], rel[:, h:h + 1].broadcast_to([BUCKETS + 1, P]),
                          con("bucket", BUCKETS + 1), start=True, stop=True).then_inc(bias_rows_done, 1)

            turn_rows(lambda b, c: h0[:, b, c * P:(c + 1) * P], 0, 0)

            pe.wait_ge(xT_part, 8)
            for G in range(G_IN):
                if G >= 2:
                    pe.wait_ge(group_out_act, G - 1)
                    pe.wait_ge(group_out_dve, G - 1)
                for c in range(DC):
                    product(G, c)
            pe.wait_ge(wg_ready, 1)
            for b in range(TB):
                for c in range(DC):
                    mm = passes(bank[:, b, 0:GATES], [xT_hi[:, c, tb_cols(b)], xT_lo[:, c, tb_cols(b)]],
                                [wg_hi[:, c, :], wg_lo[:, c, :]], start=(c == 0), stop=(c == DC - 1))
                mm.then_inc(gates_done, 1)

            pe.wait_ge(kn_ready, 2)
            pe.wait_ge(bias_rows_out, HEADS)
            for b in range(TB):
                for r, c0 in enumerate((C_KS, C_KW)):
                    for gp in range(2):
                        mm = pe.transpose(bank[:, 2 + b, (2 * r + gp) * P:(2 * r + gp + 1) * P],
                                          proj[:, b, c0 + gp * P:c0 + (gp + 1) * P], eye)
                mm.then_inc(turned_kq, 1)
            pe.wait_ge(group_out_act, G_IN)
            pe.wait_ge(group_out_dve, G_IN)
            for b in range(TB):
                for k in range(4):
                    mm = pe.transpose(bank[:, 4 + b, tb_cols(k)], proj[:, b, k * P:(k + 1) * P], eye)
                mm.then_inc(turned_kv, 1)
            pe.wait_ge(qn_ready, 2)
            for b in range(TB):
                for half in range(2):
                    m = 2 * b + half
                    if m >= 2:
                        pe.wait_ge(kq_out, 8)
                    for k in range(4):
                        pr = 4 * half + k
                        mm = pe.transpose(bank[:, (6, 7, 2, 3)[m], tb_cols(k)],
                                          proj[:, b, C_Q + pr * P:C_Q + (pr + 1) * P], eye)
                    mm.then_inc(turned_kq, 1)

            pe.wait_ge(gates_exp, 2)
            pe.wait_ge(kv_pe_ready, 4)
            for kvg in range(2 * KV):
                kvi, g = divmod(kvg, KV)
                for ih in range(2):
                    k = 2 * kvg + ih
                    pe.wait_ge(cmp_in[k % CMP_RING], 16 * (k // CMP_RING + 1))
                    w = cmp_w1[k % CMP_RING]
                    for i in range(8):
                        a = 8 * ih + i
                        mm = pe.matmul(bank[0:NCMP, kvi, tb_cols(g)],
                                       kv_pe[:, ih, kvi, g, a:a + 8 * (NCMP - 1) + 1:8], w[:, i * P:(i + 1) * P],
                                       start=(ih == 0 and i == 0), stop=(ih == 1 and i == 7))
                    mm.then_inc(cmp_used, 1)
            pe.wait_ge(hid_acted, 2)
            for kvg in range(2 * KV):
                kvi, g = divmod(kvg, KV)
                mm = pe.transpose(bank[:, 0, kvg * 16:kvg * 16 + NCMP], hid_rows[0:NCMP, kvi, tb_cols(g)],
                                  eye[0:NCMP, 0:NCMP])
            mm.then_inc(hid_turned, 1)
            pe.wait_ge(hid_ready, 1)
            for kvi in range(2):
                for g in range(KV):
                    w2 = par("w2").rearrange("p (k g d) -> p k g d", k=2, g=KV)
                    mm = pe.matmul(bank[:, 4, (kvi * KV + g) * HD:(kvi * KV + g + 1) * HD], hid[:, kvi, g, :],
                                   w2[:, kvi, g, :], start=True, stop=True)
            mm.then_inc(cmp_done, 1)
            pe.wait_ge(kc_ready, 1)
            for gp in range(2):
                mm = pe.transpose(bank[:, 5, gp * 32:gp * 32 + 32],
                                  kcs[0:32, 2 * gp:2 * gp + 2, :].rearrange("p g d -> p (g d)"), eye[0:32, 0:32])
            mm.then_inc(kc_turned, 1)

            pe.wait_ge(v_ready, 2)
            pe.wait_ge(sgw_ready, 1)
            pe.wait_ge(kq_out, 12)
            for h in range(SG_HEADS):
                w_s = par("sg_w").rearrange("p (h t) -> p h t", h=SG_HEADS)
                pe.matmul(bank[:, (0, 1, 2, 3)[h // 2], (h % 2) * T:(h % 2 + 1) * T], w_s[:, h, :],
                          proj[:, :, C_V + h * P:C_V + (h + 1) * P], start=True, stop=True).then_inc(mixed_done, 1)

            pe.wait_ge(sg_out, SG_HEADS)
            pe.wait_ge(kc_out, 1)
            S0, PT0, O_SEL, O_WIN, O_CMP, CMP = 0, 2, 4, 5, 6, 7

            def score(u):
                b, h = divmod(u, HEADS)
                n = (b + 1) * P
                rows = slice(HD * (h % 2), HD * (h % 2) + HD)
                if u >= 2:
                    pe.wait_ge(biased_ready, u - 1)
                pe.matmul(bank[:, S0 + u % 2, 0:2 * n], qT[rows, h // 2, tb_cols(b)],
                          kT[rows, :, h // REP, 0:n], start=True, stop=True).then_inc(scored, 1)

            def turn_probs(u):
                b, h = divmod(u, HEADS)
                pe.wait_ge(probs_ready, 2 * (u + 1))
                if u >= 2:
                    pe.wait_ge(probsT_ready, u - 1)
                for r in range(2):
                    for s in range(b + 1):
                        mm = pe.transpose(bank[:, PT0 + u % 2, tb_cols(r * (b + 1) + s)],
                                          probs[:, u % 2, r, tb_cols(s)], eye)
                mm.then_inc(probs_turned, 1)

            def value(u):
                b, h = divmod(u, HEADS)
                half = u // 8
                pe.wait_ge(probsT_ready, u + 1)
                if h % 8 == 0:
                    if half >= 1:
                        pe.wait_ge(half_out, half)
                    if h == 0:
                        pe.wait_ge(cmp_out, b + 1)
                    for g in range(2):
                        gg = 2 * (half % 2) + g
                        pe.matmul(bank[:, O_CMP, g * T:(g + 1) * T], pcT[:, gg, :],
                                  vc_own[:, gg].rearrange("p r d -> p (r d)"), start=True, stop=True)
                for r, (o, c0) in enumerate(((O_SEL, C_VS), (O_WIN, C_VW))):
                    for s in range(b + 1):
                        v0 = c0 + (h // REP) * HD
                        mm = pe.matmul(bank[:, o, (h % 8) * HD:(h % 8 + 1) * HD],
                                       probsT[:, u % 2, r * (b + 1) + s, :], proj[:, s, v0:v0 + HD],
                                       start=(s == 0), stop=(s == b))
                mm.then_inc(valued, 1)

            for u in range(N_UNITS_ATT + 2):
                if u % HEADS == 0 and u < N_UNITS_ATT:
                    b = u // HEADS
                    if b >= 1:
                        pe.wait_ge(cmp_shifted, b)
                    for odd in range(2):
                        if odd:
                            pe.wait_ge(cmp_scored, 2 * b + 1)
                        rows = slice(HD * odd, HD * odd + HD)
                        for h in range(odd, HEADS, 2):
                            mm = pe.matmul(bank[:, CMP, h * 32:h * 32 + 16], qT[rows, h // 2, tb_cols(b)],
                                           kcT[rows, h // REP, 0:16], start=True, stop=True)
                        mm.then_inc(cmp_scored, 1)
                if u < N_UNITS_ATT:
                    score(u)
                if 1 <= u <= N_UNITS_ATT:
                    turn_probs(u - 1)
                if u % HEADS == 1 and u < N_UNITS_ATT:
                    b = u // HEADS
                    pe.wait_ge(cmp_weighed, b + 1)
                    for g in range(KV):
                        mm = pe.transpose(bank[:, CMP, tb_cols(g)],
                                          pc[:, 4 * g:4 * g + 4, :].rearrange("p h n -> p (h n)"), eye)
                    mm.then_inc(cmp_turned, 1)
                if u >= 2:
                    value(u - 2)

            mix_col = lambda c: (C_Q if c < 8 else C_U - 8 * P) + c * P
            turn_rows(lambda b, c: proj[:, b, mix_col(c):mix_col(c) + P], 2, 8)
            pe.wait_ge(xT_part, 16)
            pe.wait_ge(half_out, 4)
            for k in range(G_OUT):
                G = G_IN + k
                if k >= 2:
                    pe.wait_ge(group_out_dve, G - 1)
                for c in range(DC):
                    product(G, c)

            turn_rows(lambda b, c: hn[:, b, c * P:(c + 1) * P], 4, 16)
            pe.wait_ge(xT_part, 24)
            pe.wait_ge(group_out_dve, G_IN + G_OUT)
            subkeys = par("subkeys").rearrange("p (a k) -> p a k", a=2)

            def key_scores(k):
                pe.wait_ge(query_out_act, k + 1)
                pe.wait_ge(query_out_dve, k + 1)
                if k >= 1:
                    pe.wait_ge(keyed_out_act, k)
                    pe.wait_ge(keyed_out_dve, k)
                for b in range(TB):
                    for j in range(4):
                        mm = pe.matmul(bank[:, b, tb_cols(j)], queryT[:, k % 2, j, tb_cols(b)],
                                       subkeys[:, j % 2, :], start=True, stop=True)
                mm.then_inc(keyed, 1)

            for k in range(G_QUERY):
                if k >= 2:
                    pe.wait_ge(query_out_act, k - 1)
                    pe.wait_ge(query_out_dve, k - 1)
                for c in range(DC):
                    w = split_part(N_QUERY + DC * k + c)
                    for j in range(4):
                        mm = passes(bank[:, 4 + 2 * (k % 2) + j // 2, (j % 2) * T:(j % 2 + 1) * T],
                                    [v[:, tb_cols(j)] for v in w], [xT_hi[:, c, :], xT_lo[:, c, :]],
                                    start=(c == 0 and j % 2 == 0), stop=(c == DC - 1))
                    mm.then_inc(parts_used, 1)
                if k >= 1:
                    key_scores(k - 1)
            key_scores(G_QUERY - 1)

            def act_part(s, r):
                for c in range(4):
                    k = 4 * r + c
                    mm = passes(bank[:, 4 + s, 0:T], [v[r][:, tb_cols(c)] for v in (hi, lo)],
                                [xT_hi[:, k, :], xT_lo[:, k, :]], start=(k == 0), stop=(k == DC - 1))
                mm.then_inc(parts_used, 1)

            def act_tiles(first, last):
                with pe.Fori(first // 2, last // 2) as i:
                    for s in range(2):
                        pe.wait_ge(u_out, i * 2 + (s - 1))
                        for r in range(4):
                            pe.wait_ge(lo_ready, i * 8 + (N_U + 4 * s + r + 1))
                            act_part(s, r)

            for s in range(2):
                for r in range(4):
                    pe.wait_ge(lo_ready, N_U + 4 * s + r + 1)
                    act_part(s, r)
            act_tiles(2, EARLY)

            pe.wait_ge(weights_ready, 1)
            for a in range(3):
                for b in range(TB):
                    src = picked[:, a, tb_cols(b)] if a < 2 else soft[:, tb_cols(b)]
                    mm = pe.transpose(bank[:, a // 2, (a % 2) * T + b * P:(a % 2) * T + (b + 1) * P], src, eye)
            mm.then_inc(slots_turned, 1)

            def spread_four(e):
                for j in range(4):
                    mm = pe.matmul(bank[:, 2 + e, tb_cols(j)], one_i1[:, e, j, :], one_i2[:, e, j, :],
                                   start=True, stop=True)
                mm.then_inc(spread_done, 1)

            for e in range(2):
                pe.wait_ge(one_i1_ready, e + 1)
                pe.wait_ge(one_i2_ready, e + 1)
                spread_four(e)
            with pe.Fori(1, T // 8) as i:
                for e in range(2):
                    pe.wait_ge(one_i1_ready, i * 2 + (e + 1))
                    pe.wait_ge(one_i2_ready, i * 2 + (e + 1))
                    pe.wait_ge(spread_out, i * 2 + (e - 1))
                    spread_four(e)

            act_tiles(EARLY, KEYS)

            def experts(s, c, first, last):
                for b in range(TB):
                    mm = passes(bank[:, 4 * b + c], [wcol_hi[s][:, tb_cols(b)], wcol_lo[s][:, tb_cols(b)]],
                                [hi[c][:], lo[c][:]], start=first, stop=last)
                mm.then_inc(parts_used, 1)

            pe.wait_ge(u_out, KEYS)
            for s in range(2):
                pe.wait_ge(wcol_ready, s + 1)
                for c in range(4):
                    pe.wait_ge(v_lo_ready, 4 * s + c + 1)
                    experts(s, c, s == 0, False)
            with pe.Fori(1, KEYS // 2 - 1) as i:
                for s in range(2):
                    pe.wait_ge(wcol_ready, i * 2 + (s + 1))
                    for c in range(4):
                        pe.wait_ge(v_lo_ready, i * 8 + (4 * s + c + 1))
                        experts(s, c, False, False)
            for s in range(2):
                pe.wait_ge(wcol_ready, KEYS - 1 + s)
                for c in range(4):
                    pe.wait_ge(v_lo_ready, 4 * KEYS - 7 + 4 * s + c)
                    experts(s, c, False, s == 1)

        @block.scalar
        def _(act):
            act.dma_start(small[:], small_in).then_inc(small_in_s, 16)
            act.dma_start(consts[:], const_in).then_inc(small_in_s, 16)
            act.dma_start(row_g[:], attn_g.partition_broadcast(P)).then_inc(gain_in, 16)
            act.dma_start(lnG[:], ln_g.partition_broadcast(P)).then_inc(rows_ln, 16)
            act.dma_start(lnB[:], ln_b.partition_broadcast(P)).then_inc(rows_ln, 16)

            def round_part(n):
                act.wait_ge(raw_in[n // 2 % RAW], 16 * (n // (2 * RAW) + 1))
                if n >= SPLIT:
                    act.wait_ge(parts_used, n + 1 - SPLIT)
                act.copy(hi[n % SPLIT][:], raw[n // 2 % RAW][:, n % 2 * PART:(n % 2 + 1) * PART]).then_inc(hi_ready, 1)

            def round_dyn(first, i, k):
                s = k // 2 % RAW
                act.wait_ge(raw_in[s], i * 16 + 16 * ((first + k) // (2 * RAW) + 1))
                act.wait_ge(parts_used, i * 8 + (first + k + 1 - SPLIT))
                act.copy(hi[k % SPLIT][:], raw[s][:, k % 2 * PART:(k % 2 + 1) * PART]).then_inc(hi_ready, 1)

            def take_hi(m):
                b, k = divmod(m % 8, DC // 4)
                act.wait_ge(turned_x, m + 1)
                act.copy(xT_hi[:, 4 * k:4 * k + 4, tb_cols(b)], bank[:, m % 2].rearrange("p (c t) -> p c t", c=4))\
                   .then_inc(xT_hi_part, 1)

            roots = [0]

            def root(cols_):
                roots[0] += 1
                act.wait_ge(var_ready, roots[0])
                act.activation(stats[:, cols_], stats[:, cols_], ACT.Sqrt).then_inc(root_ready, 1)

            act.wait_ge(x_in, 16)
            for b in range(TB):
                act.activation(h0[:, b], xs[:, b], ACT.Square, accum_out=stats[:, b:b + 1]).then_inc(squares_ready, 1)
            root(slice(0, 2))
            for h in range(HEADS):
                act.wait_ge(bias_rows_done, h + 1)
                act.copy(bias_rep[:, h], bank[:, 2 + h % 2, 0:SPAN]).then_inc(bias_rows_out, 1)
            act.copy(wg_hi[:].rearrange("p c n -> p (c n)"), par("w_gate")).then_inc(wg_hi_ready, 1)
            for n in range(SPLIT):
                round_part(n)
            for m in range(8):
                take_hi(m)

            def gelu(k):
                g, b = divmod(k, 2)
                c0 = C_V + PART * g
                act.wait_ge(group_out_act, 6 + g)
                act.wait_ge(group_out_dve, 6 + g)
                act.activation(proj[:, b, c0:c0 + PART], proj[:, b, c0:c0 + PART], ACT.Gelu).then_inc(gelu_done, 1)

            for n in range(SPLIT, N_OUT + SPLIT):
                round_part(n)
                G, c = divmod(n, DC)
                if c == 2 and G >= 1:
                    act.wait_ge(parts_used, DC * G)
                    act.copy(proj[:, 0, (G - 1) * PART:G * PART], bank[:, 4 + 2 * ((G - 1) % 2)]).then_inc(group_out_act, 1)
                if G == 4 and c == 6:
                    root(slice(8, 24))
                if G == 6 and c == 6:
                    root(slice(24, 56))
                if G == 6 and c in (8, 10):
                    gelu((c - 8) // 2)
                if G == 7 and c in (4, 6):
                    gelu((c - 4) // 2 + 2)
                if G == 8 and c in (4, 6):
                    gelu((c - 4) // 2 + 4)
            for k in range(6, 8):
                gelu(k)
            root(slice(56, 72))
            for b in range(TB):
                act.wait_ge(gates_done, b + 1)
                act.activation(gates[:, b], bank[:, b, 0:GATES], ACT.Exp, scale=-1.0).then_inc(gates_exp, 1)
            for kvi in range(2):
                act.wait_ge(cmp_used, N_CMP // 2 * (kvi + 1))
                act.activation(hid_rows[0:NCMP, kvi], bank[0:NCMP, kvi], ACT.Gelu).then_inc(hid_acted, 1)
            root(slice(72, 76))

            def cmp_exps(b):
                act.wait_ge(cmp_shifted, b + 1)
                nv = 7 if b == 0 else NCMP
                act.activation(pc[:, :, 0:nv], pc[:, :, 0:nv], ACT.Exp).then_inc(cmp_exp, 1)

            def exps(u):
                b, h = divmod(u, HEADS)
                n = (b + 1) * P
                act.wait_ge(biased_ready, u + 1)
                if u >= 2:
                    act.wait_ge(probs_turned, u - 1)
                for r in range(2):
                    act.activation(probs[:, u % 2, r, 0:n], biased[:, u % 2, r, 0:n], ACT.Exp,
                                   bias=stats[:, 80 + 2 * (u % 2) + r:81 + 2 * (u % 2) + r],
                                   accum_out=sums[:, b, r, h:h + 1]).then_inc(probs_ready, 1)

            def probsT_copy(u):
                b, h = divmod(u, HEADS)
                act.wait_ge(probs_turned, u + 1)
                if u >= 2:
                    act.wait_ge(valued, u - 1)
                n = 2 * (b + 1)
                act.copy(probsT[:, u % 2, 0:n].rearrange("p a t -> p (a t)"), bank[:, 2 + u % 2, 0:n * P])\
                   .then_inc(probsT_ready, 1)

            for u in range(N_UNITS_ATT + 1):
                if u < N_UNITS_ATT:
                    if u % HEADS == 0:
                        cmp_exps(u // HEADS)
                    exps(u)
                if u >= 1:
                    probsT_copy(u - 1)

            act.wait_ge(rows_scaled, TB)
            act.dma_start(row_g[:], out_g.partition_broadcast(P)).then_inc(gain_in, 16)
            for b in range(TB):
                act.wait_ge(half_out, 2 * (b + 1))
                act.wait_ge(sg_out, SG_HEADS)
                for k, c0 in enumerate((C_Q, C_U)):
                    if b or k:
                        act.wait_ge(squares_ready, TB + 2 * b + k)
                    act.activation(squares[:], proj[:, b, c0:c0 + 1024], ACT.Square,
                                   accum_out=stats[:, 84 + 2 * b + k:85 + 2 * b + k]).then_inc(squares_ready, 1)
            root(slice(84, 88))
            for m in range(8, 16):
                take_hi(m)
            act.dma_start(row_g[:], ffn_g.partition_broadcast(P)).then_inc(gain_in, 16)
            for n in range(N_OUT + SPLIT, N_QUERY + SPLIT):
                round_part(n)
            act.wait_ge(group_out_dve, G_IN + G_OUT)
            act.dma_start(resid_rows, xs[:]).then_inc(resid_stored, 16)
            for b in range(TB):
                act.activation(hn[:, b], xs[:, b], ACT.Square, accum_out=stats[:, 88 + b:89 + b])\
                   .then_inc(squares_ready, 1)
            root(slice(88, 90))
            for m in range(16, 24):
                take_hi(m)

            def keyed_out(k):
                act.wait_ge(keyed, k + 1)
                act.copy(scores[:, 2 * k:2 * k + 2].rearrange("p u a k -> p (u a k)"), bank[:, 0])\
                   .then_inc(keyed_out_act, 1)

            for n in range(N_QUERY + SPLIT, N_U + SPLIT):
                round_part(n)
                k, c = divmod(n - N_QUERY, DC)
                if k >= 1 and c == 2:
                    act.wait_ge(parts_used, N_QUERY + DC * k)
                    if k >= 3:
                        act.wait_ge(keyed, k - 2)
                    act.copy(queryT[:, (k - 1) % 2, 0:2].rearrange("p j t -> p (j t)"), bank[:, 4 + 2 * ((k - 1) % 2)])\
                       .then_inc(query_out_act, 1)
                if k >= 2 and c == 3:
                    keyed_out(k - 2)
            keyed_out(G_QUERY - 1)

            act.wait_ge(resid_stored, 16)
            act.wait_ge(keyed_out_dve, G_QUERY)

            def tile_out(i, s, out_):
                for r in range(3):
                    round_dyn(N_U, i, 4 * s + 4 + r)
                act.wait_ge(parts_used, i * 8 + (N_U + 4 * s + 4))
                act.activation(out_, bank[:, 4 + s, 0:T], ACT.Gelu).then_inc(u_out, 1)
                round_dyn(N_U, i, 4 * s + 7)

            def early_tiles(first, last):
                with act.Fori(first // 2, last // 2) as i:
                    for s in range(2):
                        tile_out(i, s, spread[:, bass.ds(i * 2 + s, 1), :].rearrange("p o t -> p (o t)"))

            early_tiles(0, SOFT_AT)
            act.wait_ge(soft_shifted, 1)
            act.activation(soft[:], soft[:], ACT.Exp).then_inc(soft_exp, 1)
            early_tiles(SOFT_AT, EARLY)

            with act.Fori(0, T // 8) as i:
                for e in range(2):
                    act.wait_ge(spread_weighed, i * 2 + (e + 1))
                    src = bank[:, 2 + e].rearrange("p (t k) -> p k t", t=4)
                    act.copy(spread[:, EARLY:KEYS, bass.ds(i * 8 + 4 * e, 4)], src[:, EARLY:KEYS, :])\
                       .then_inc(spread_out, 1)

            act.wait_ge(spread_weighed, T // 4)
            for s in range(2):
                tile_out(EARLY // 2, s, acted[:, s, :])
            with act.Fori(EARLY // 2 + 1, KEYS // 2) as i:
                for s in range(2):
                    act.wait_ge(u_weighed, i * 2 + (s - 1 - EARLY))
                    tile_out(i, s, acted[:, s, :])

            act.wait_ge(u_weighed, KEYS - EARLY)
            for s in range(2):
                act.copy(wcol_hi[s][:], spread[:, s, :]).then_inc(wcol_hi_ready, 1)
            with act.Fori(0, KEYS // 2 - 1) as i:
                for s in range(2):
                    for c in range(4):
                        round_dyn(N_V, i, 4 * s + 4 + c)
                    act.copy(wcol_hi[s][:], spread[:, bass.ds(i * 2 + (s + 2), 1), :].rearrange("p o t -> p (o t)"))\
                       .then_inc(wcol_hi_ready, 1)
            for n in range(N_V + 4 * (KEYS - 1), N_V + 4 * KEYS):
                round_part(n)

        @block.vector
        def _(dve):
            step = [0]

            def link(ins):
                step[0] = step[0] + 1
                ins.then_inc(dve_step, 1)
                dve.wait_ge(dve_step, step[0])

            choice = [0]

            def link_choice(ins):
                choice[0] += 1
                ins.then_inc(choice_step, 1)
                dve.wait_ge(choice_step, choice[0])

            roots = [0]

            def rstd(c, count):
                roots[0] += 1
                dve.tensor_scalar(stats[:, c], stats[:, c], 1.0 / count, EPS, ALU.mult, ALU.add).then_inc(var_ready, 1)
                dve.wait_ge(root_ready, roots[0])
                link(dve.reciprocal(stats[:, c], stats[:, c]))

            dve.wait_ge(squares_ready, TB)
            rstd(slice(0, 2), D)
            for b in range(TB):
                if b == 0:
                    dve.wait_ge(gain_in, 16)
                dve.scalar_tensor_tensor(out=h0[:, b], in0=xs[:, b], scalar=stats[:, b:b + 1], in1=row_g[:],
                                         op0=ALU.mult, op1=ALU.mult).then_inc(rows_scaled, 1)

            def take_lo(n):
                for m in range(n, n + 8):
                    b, k = divmod(m % 8, DC // 4)
                    dve.wait_ge(xT_hi_part, m + 1)
                    at = (slice(None), slice(4 * k, 4 * k + 4), tb_cols(b))
                    dve.tensor_tensor(xT_lo[at], bank[:, m % 2].rearrange("p (c t) -> p c t", c=4),
                                      xT_hi[at].bitcast(F32), ALU.subtract).then_inc(xT_part, 1)

            take_lo(0)
            dve.wait_ge(wg_hi_ready, 1)
            dve.tensor_tensor(wg_lo[:].rearrange("p c n -> p (c n)"), par("w_gate"),
                              wg_hi[:].rearrange("p c n -> p (c n)").bitcast(F32), ALU.subtract).then_inc(wg_ready, 1)

            def group_out(G):
                dve.wait_ge(parts_used, DC * (G + 1))
                dve.tensor_copy(proj[:, 1, G * PART:(G + 1) * PART], bank[:, 5 + 2 * (G % 2)])\
                   .then_inc(group_out_dve, 1)

            for G in range(3):
                group_out(G)
            dve.wait_ge(group_out_act, 3)
            dve.wait_ge(group_out_dve, 3)
            k_both = lambda b: proj[:, b, C_KS:C_KS + 1024].rearrange("p (r n) -> p r n", r=2)[:, :, 0:D_KV]
            k_stat = lambda b: stats[:, 8 + 8 * b:16 + 8 * b]
            for b in range(TB):
                link(dve.tensor_tensor(scratch[:].rearrange("p (r n) -> p r n", r=2), k_both(b), k_both(b), ALU.mult))
                link(dve.tensor_reduce(k_stat(b), scratch[:].rearrange("p (g d) -> p g d", d=HD), AX.X, ALU.add))
            group_out(3)
            rstd(slice(8, 24), HD)
            for b in range(TB):
                for r in range(2):
                    v = proj[:, b, C_KS + 512 * r:C_KS + 512 * r + D_KV].rearrange("p (g d) -> p g d", d=HD)
                    s = stats[:, 8 + 8 * b + 4 * r:12 + 8 * b + 4 * r].rearrange("p (g o) -> p g o", o=1)
                    ins = dve.tensor_tensor(v, v, s.broadcast_to([P, KV, HD]), ALU.mult)
                ins.then_inc(kn_ready, 1)
            group_out(4)
            dve.wait_ge(group_out_act, 5)
            dve.wait_ge(group_out_dve, 5)
            for b in range(TB):
                for half in range(2):
                    q = proj[:, b, C_Q + 512 * half:C_Q + 512 * half + 512]
                    link(dve.tensor_tensor(scratch[:], q, q, ALU.mult))
                    a = 24 + 16 * b + 8 * half
                    link(dve.tensor_reduce(stats[:, a:a + 8], scratch[:].rearrange("p (g d) -> p g d", d=HD),
                                           AX.X, ALU.add))
            group_out(5)
            rstd(slice(24, 56), HD)
            for b in range(TB):
                v = proj[:, b, C_Q:C_Q + D_NSA].rearrange("p (h d) -> p h d", d=HD)
                s = stats[:, 24 + 16 * b:40 + 16 * b].rearrange("p (h o) -> p h o", o=1)
                dve.tensor_tensor(v, v, s.broadcast_to([P, HEADS, HD]), ALU.mult).then_inc(qn_ready, 1)
            group_out(6)
            dve.wait_ge(gelu_done, 4)
            for b in range(TB):
                v = proj[:, b, C_V:C_V + D_SG].rearrange("p (h c) -> p h c", c=P)
                mean = stats[:, 92 + 8 * b:100 + 8 * b]
                link(dve.tensor_reduce(mean, v, AX.X, ALU.add))
                link(dve.tensor_scalar(mean, mean, 1.0 / P, None, ALU.mult))
                link(dve.tensor_tensor(v, v, mean.rearrange("p (h o) -> p h o", o=1).broadcast_to([P, SG_HEADS, P]),
                                       ALU.subtract))
            group_out(7)
            for b in range(TB):
                for half in range(2):
                    v = proj[:, b, C_V + 512 * half:C_V + 512 * half + 512]
                    link(dve.tensor_tensor(scratch[:], v, v, ALU.mult))
                    a = 56 + 8 * b + 4 * half
                    link(dve.tensor_reduce(stats[:, a:a + 4], scratch[:].rearrange("p (h c) -> p h c", c=P),
                                           AX.X, ALU.add))
            group_out(8)
            rstd(slice(56, 72), P)
            for b in range(TB):
                v = proj[:, b, C_V:C_V + D_SG].rearrange("p (h c) -> p h c", c=P)
                s = stats[:, 56 + 8 * b:64 + 8 * b].rearrange("p (h o) -> p h o", o=1)
                dve.tensor_tensor(v, v, s.broadcast_to([P, SG_HEADS, P]), ALU.mult).then_inc(v_centred, 1)
            dve.wait_ge(gates_exp, TB)
            gates_all = gates[:].rearrange("p b n -> p (b n)")
            link(dve.tensor_scalar(gates_all, gates_all, 1.0, None, ALU.add))
            link(dve.reciprocal(gates_all, gates_all))
            g_cmp = gates[:, 0, 0:GATES:3]
            link(dve.tensor_scalar(g_cmp, g_cmp, con("seen"), None, ALU.mult))

            dve.wait_ge(bias_stored, 16)
            for b in range(TB):
                dve.wait_ge(turned_kq, b + 1)
                for src_half in range(2):
                    for dst_half in range(2):
                        sr, dr = slice(64 * src_half, 64 * src_half + 64), slice(64 * dst_half, 64 * dst_half + 64)
                        src = bank[sr, 2 + b].rearrange("p (r a t) -> p r a t", r=2, a=2)
                        gain = small[sr, SMALL["k_g"][0] + 1:SMALL["k_g"][0] + 3].rearrange("p (r a o) -> p r a o", a=1, o=1)
                        dst = kT[dr, :, src_half::2, tb_cols(b)]
                        dve.tensor_tensor(dst, src, gain.broadcast_to([64, 2, 2, P]), ALU.mult).then_inc(kq_out, 1)
            pe_code = par("pe").rearrange("p (k i) -> p k i", k=4)
            for b in range(TB):
                dve.wait_ge(turned_kv, b + 1)
                for ih in range(2):
                    for e in range(2):
                        rows = slice(HD * e, HD * e + HD)
                        for odd in range(2):
                            src = bank[rows, 4 + b].rearrange("p (k n i) -> p k n i", k=4, i=16)[:, :, :, odd::2]
                            dst = kv_pe[HD * odd:HD * odd + HD, ih].rearrange("p v g t -> p (v g) t")[:, e::2, :]
                            dst = dst[:, :, b * 64:(b + 1) * 64].rearrange("p k (n i) -> p k n i", i=8)
                            code = pe_code[rows, :, 16 * ih + odd:16 * ih + 16:2].rearrange("p k (o i) -> p k o i", o=1)
                            ins = dve.tensor_tensor(dst, src, code.broadcast_to([HD, 4, 8, 8]), ALU.add)
                    ins.then_inc(kv_pe_ready, 1)
            for m in range(4):
                b, half = divmod(m, 2)
                dve.wait_ge(turned_kq, 3 + m)
                src = bank[:, (6, 7, 2, 3)[m]].rearrange("p (a t) -> p a t", a=4)
                dve.tensor_scalar(qT[:, 4 * half:4 * half + 4, tb_cols(b)], src, par("q_g"), HD ** -0.5,
                                  ALU.mult, ALU.mult).then_inc(kq_out, 1)

            dve.wait_ge(hid_turned, 1)
            dve.wait_ge(hid_zero, 1)
            for kvi in range(2):
                src = bank[:, 0, kvi * 64:kvi * 64 + 64].rearrange("p (g o n) -> p g o n", g=KV, o=1)[:, :, :, 0:NCMP]
                dst = hid[:, kvi].rearrange("p g (r n) -> p g r n", n=32)[:, :, :, 0:NCMP]
                ins = dve.tensor_copy(dst, src.broadcast_to([P, KV, REP, NCMP]))
            ins.then_inc(hid_ready, 1)
            dve.wait_ge(cmp_done, 1)
            kc_src = bank[:, 4, 0:D_KV].rearrange("p (g d) -> p g d", d=HD)
            link(dve.tensor_copy(kcs[:], kc_src))
            own = con("own").rearrange("p (r o) -> p r o", o=1).broadcast_to([P, REP, HD])
            for g in range(KV):
                src = bank[:, 4, D_KV + g * HD:D_KV + (g + 1) * HD].rearrange("p (o d) -> p o d", o=1)
                ins = dve.tensor_tensor(vc_own[:, g], src.broadcast_to([P, REP, HD]), own, ALU.mult)
            link(ins)
            sq = scratch[:, 0:D_KV].rearrange("p (g d) -> p g d", d=HD)
            link(dve.tensor_tensor(sq, kcs[:], kcs[:], ALU.mult))
            link(dve.tensor_reduce(stats[:, 72:76], sq, AX.X, ALU.add))
            rstd(slice(72, 76), HD)
            s = stats[:, 72:76].rearrange("p (g o) -> p g o", o=1)
            dve.tensor_tensor(kcs[:], kcs[:], s.broadcast_to([P, KV, HD]), ALU.mult).then_inc(kc_ready, 1)
            dve.wait_ge(kc_turned, 1)
            k0 = SMALL["k_g"][0]
            for src_half in range(2):
                for dst_half in range(2):
                    sr, dr = slice(64 * src_half, 64 * src_half + 64), slice(64 * dst_half, 64 * dst_half + 64)
                    src = bank[sr, 5, 0:64].rearrange("p (a n) -> p a n", a=2)
                    ins = dve.tensor_scalar(kcT[dr, src_half::2, :], src, small[sr, k0:k0 + 1], None, ALU.mult)
            ins.then_inc(kc_out, 1)

            for h in range(SG_HEADS):
                dve.wait_ge(mixed_done, 2 * (h // 2) + 2)
                if h == 0:
                    dve.wait_ge(gelu_done, 8)
                src = bank[:, h // 2, (h % 2) * T:(h % 2 + 1) * T].rearrange("p (b c) -> p b c", b=TB)
                u = proj[:, :, C_U + h * P:C_U + (h + 1) * P]
                a = SMALL["sg_b"][0] + h
                dve.scalar_tensor_tensor(out=u, in0=src, scalar=small[:, a:a + 1], in1=u, op0=ALU.add,
                                         op1=ALU.mult).then_inc(sg_out, 1)

            dve.wait_ge(bias_in, 16)
            link(dve.memset(pc[:], 0.0))

            def cmp_softmax(b):
                nv = 7 if b == 0 else NCMP
                first = P + CMP_BLOCK - 1 if b == 0 else CMP_BLOCK - 1
                p = pc[:, :, 0:nv]
                st = stats[:, 108:124]
                st_o = st.rearrange("p (h o) -> p h o", o=1).broadcast_to([P, HEADS, nv])
                dve.wait_ge(cmp_scored, 2 * b + 2)
                if b:
                    dve.wait_ge(cmp_turned, b)
                src = bank[:, 7].rearrange("p (h n) -> p h n", n=32)[:, :, 0:nv]
                link(dve.tensor_tensor(p, src, bias[:, :, first:first + 16 * (nv - 1) + 1:16], ALU.add))
                link(dve.tensor_reduce(st, p, AX.X, ALU.max))
                dve.tensor_tensor(p, p, st_o, ALU.subtract).then_inc(cmp_shifted, 1)

            def cmp_weigh(b):
                nv = 7 if b == 0 else NCMP
                p = pc[:, :, 0:nv]
                st = stats[:, 108:124]
                st_o = st.rearrange("p (h o) -> p h o", o=1).broadcast_to([P, HEADS, nv])
                dve.wait_ge(cmp_exp, b + 1)
                link(dve.tensor_reduce(st, p, AX.X, ALU.add))
                link(dve.reciprocal(st, st))
                link(dve.tensor_tensor(st, st, gates[:, b, 0:GATES:3], ALU.mult))
                dve.tensor_tensor(p, p, st_o, ALU.mult).then_inc(cmp_weighed, 1)

            def cmp_take(b):
                dve.wait_ge(cmp_turned, b + 1)
                if b:
                    dve.wait_ge(valued, 9)
                dve.tensor_copy(pcT[:].rearrange("p g t -> p (g t)"), bank[:, 7]).then_inc(cmp_out, 1)

            def bias_scores(u):
                b, h = divmod(u, HEADS)
                n = (b + 1) * P
                dve.wait_ge(scored, u + 1)
                if u >= 2:
                    dve.wait_ge(probs_ready, 2 * (u - 1))
                src = bank[:, u % 2, 0:2 * n].rearrange("p (r s) -> p r s", r=2)
                bb = bias[:, h, T - n:T].rearrange("p (o s) -> p o s", o=1).broadcast_to([P, 2, n])
                dst = biased[:, u % 2, :, 0:n]
                link(dve.tensor_tensor(dst, src, bb, ALU.add))
                dve.tensor_reduce(stats[:, 80 + 2 * (u % 2):82 + 2 * (u % 2)], dst, AX.X, ALU.max,
                                  negate=True).then_inc(biased_ready, 1)

            def combine(half):
                b, k = divmod(half, 2)
                dve.wait_ge(valued, 8 * (half + 1))
                hs = slice(8 * k, 8 * k + 8)
                wt = wcomb[:].rearrange("p (r h) -> p r h", r=2)
                link(dve.reciprocal(wt, sums[:, b, :, hs]))
                gt = gates[:, b].rearrange("p (h r) -> p r h", r=3)[:, 1:3, hs]
                link(dve.tensor_tensor(wt, wt, gt, ALU.mult))
                o = proj[:, b, C_Q + 512 * k:C_Q + 512 * k + 512]
                for r, dst in enumerate((o, scratch[:])):
                    src = bank[:, 4 + r].rearrange("p (h d) -> p h d", d=HD)
                    ww = wt[:, r].rearrange("p (h o) -> p h o", o=1).broadcast_to([P, 8, HD])
                    link(dve.tensor_tensor(dst.rearrange("p (h d) -> p h d", d=HD), src, ww, ALU.mult))
                link(dve.tensor_tensor(o, o, scratch[:], ALU.add))
                dve.tensor_tensor(o, o, bank[:, 6], ALU.add).then_inc(half_out, 1)

            for u in range(N_UNITS_ATT):
                if u % HEADS == 0:
                    cmp_softmax(u // HEADS)
                bias_scores(u)
                if u % HEADS == 0:
                    cmp_weigh(u // HEADS)
                if u % HEADS == 1:
                    cmp_take(u // HEADS)
                if u % 8 == 1 and u > 8:
                    combine(u // 8 - 1)
            combine(3)

            dve.wait_ge(squares_ready, TB + 4)
            rstd(slice(84, 88), 1024)
            dve.wait_ge(gain_in, 32)
            for b in range(TB):
                for k, c0 in enumerate((C_Q, C_U)):
                    v = proj[:, b, c0:c0 + 1024]
                    ins = dve.scalar_tensor_tensor(out=v, in0=v, scalar=stats[:, 84 + 2 * b + k:85 + 2 * b + k],
                                                   in1=row_g[:, 1024 * k:1024 * (k + 1)], op0=ALU.mult, op1=ALU.mult)
                    if k == 0:
                        link(ins)
                ins.then_inc(rows_scaled, 1)
            take_lo(8)
            for k in range(G_OUT):
                G = G_IN + k
                dve.wait_ge(parts_used, DC * (G + 1))
                for b in range(TB):
                    xc = xs[:, b, k * PART:(k + 1) * PART]
                    ins = dve.tensor_tensor(xc, bank[:, 4 + 2 * (G % 2) + b], xc, ALU.add)
                    if b == 0:
                        link(ins)
                ins.then_inc(group_out_dve, 1)
            dve.wait_ge(squares_ready, TB + 4 + TB)
            rstd(slice(88, 90), D)
            dve.wait_ge(gain_in, 48)
            for b in range(TB):
                dve.scalar_tensor_tensor(out=hn[:, b], in0=xs[:, b], scalar=stats[:, 88 + b:89 + b], in1=row_g[:],
                                         op0=ALU.mult, op1=ALU.mult).then_inc(rows_scaled, 1)
            take_lo(16)
            for k in range(G_QUERY):
                dve.wait_ge(parts_used, N_QUERY + DC * (k + 1))
                if k >= 2:
                    dve.wait_ge(keyed, k - 1)
                dve.tensor_copy(queryT[:, k % 2, 2:4].rearrange("p j t -> p (j t)"), bank[:, 5 + 2 * (k % 2)])\
                   .then_inc(query_out_dve, 1)
                dve.wait_ge(keyed, k + 1)
                dve.tensor_copy(scores[:, 8 + 2 * k:10 + 2 * k].rearrange("p u a k -> p (u a k)"), bank[:, 1])\
                   .then_inc(keyed_out_dve, 1)

            dve.wait_ge(keyed_out_act, G_QUERY)
            dve.wait_ge(keyed_out_dve, G_QUERY)

            iota16 = con("iota")[:, 0:TOPK].rearrange("p (a m) -> p a m", a=1)

            def choose(u):
                link_choice(dve.tensor_copy(sc[:].rearrange("p a k -> p (a k)"),
                                     scores[:].rearrange("p u a k -> p (u a k)")[:, bass.ds(u * (2 * KEYS), 2 * KEYS)]))
                for a in range(2):
                    link_choice(dve.max(best[:, a, 0:8], sc[:, a]))
                    link_choice(dve.match_replace(sc_rest[:, a], best[:, a, 0:8], sc[:, a], -3.0e38))
                    link_choice(dve.max(best[:, a, 8:16], sc_rest[:, a]))
                    link_choice(dve.max_index(best_at[:, a, 0:8], best[:, a, 0:8], sc[:, a]))
                    link_choice(dve.max_index(best_at[:, a, 8:16], best[:, a, 8:16], sc_rest[:, a]))
                link_choice(dve.tensor_copy(best_f[:], best_at[:]))
                b1 = best[:, 0].rearrange("p (a o) -> p a o", o=1).broadcast_to([P, TOPK, TOPK])
                b2 = best[:, 1].rearrange("p (o b) -> p o b", o=1).broadcast_to([P, TOPK, TOPK])
                link_choice(dve.tensor_tensor(cand[:], b1, b2, ALU.add))
                flat = cand[:].rearrange("p a b -> p (a b)")
                link_choice(dve.max(chosen[:, 2, 0:8], flat))
                link_choice(dve.match_replace(cand_rest[:], chosen[:, 2, 0:8], flat, -3.0e38))
                link_choice(dve.max(chosen[:, 2, 8:16], cand_rest[:]))
                link_choice(dve.max_index(pos[:, 0:8], chosen[:, 2, 0:8], flat))
                link_choice(dve.max_index(pos[:, 8:16], chosen[:, 2, 8:16], cand_rest[:]))
                dve.tensor_scalar(pos2[:, 0], pos[:], 4, None, ALU.logical_shift_right)
                link_choice(dve.tensor_scalar(pos2[:, 1], pos[:], 15, None, ALU.bitwise_and))
                link_choice(dve.tensor_copy(pos_f[:], pos2[:]))
                for a in range(2):
                    at = pos_f[:, a].rearrange("p (j o) -> p j o", o=1).broadcast_to([P, TOPK, TOPK])
                    link_choice(dve.tensor_tensor(hit[:, a], at, iota16.broadcast_to([P, TOPK, TOPK]), ALU.is_equal))
                    val = best_f[:, a].rearrange("p (o m) -> p o m", o=1).broadcast_to([P, TOPK, TOPK])
                    link_choice(dve.tensor_tensor(hit[:, a], hit[:, a], val, ALU.mult))
                link_choice(dve.tensor_reduce(chosen[:, 0:2], hit[:], AX.X, ALU.add))
                dve.tensor_copy(picked[:, :, bass.ds(u * TOPK, TOPK)], chosen[:]).then_inc(dve_step, 1)
                dve.sem_clear(choice_step)
                choice[0] = 0

            before = step[0]
            with dve.Fori(0, UNITS) as u:
                choose(u)
                dve.wait_ge(dve_step, u + (before + 1))
            step[0] = before + UNITS

            units_v = lambda t: t.rearrange("p (u k) -> p u k", k=TOPK)
            s_all = units_v(picked[:, 2])
            top = s_all[:, :, 0:1].broadcast_to([P, UNITS, TOPK])
            dve.tensor_tensor(units_v(soft[:]), s_all, top, ALU.subtract).then_inc(soft_shifted, 1)
            dve.wait_ge(soft_exp, 1)
            st = stats[:, 108:124]
            link(dve.tensor_reduce(st, units_v(soft[:]), AX.X, ALU.add))
            link(dve.reciprocal(st, st))
            dve.tensor_tensor(units_v(soft[:]), units_v(soft[:]),
                              st.rearrange("p (u o) -> p u o", o=1).broadcast_to([P, UNITS, TOPK]), ALU.mult)\
               .then_inc(weights_ready, 1)
            dve.wait_ge(slots_turned, 1)
            dve.tensor_copy(slotsT[:, 0:2].rearrange("p a t -> p (a t)"), bank[:, 0]).then_inc(slotsT_ready, 1)
            dve.tensor_copy(slotsT[:, 2], bank[:, 1, 0:T]).then_inc(slotsT_ready, 1)
            dve.wait_ge(slotsT_ready, 2)

            def one_hots(e, token):
                for j in range(4):
                    ins = dve.tensor_scalar(one_i1[:, e, j, :], con("iota"), slotsT[:, 0, bass.ds(token + j, 1)],
                                            slotsT[:, 2, bass.ds(token + j, 1)], ALU.is_equal, ALU.mult)
                ins.then_inc(one_i1_ready, 1)
                for j in range(4):
                    ins = dve.tensor_scalar(one_i2[:, e, j, :], con("iota"), slotsT[:, 1, bass.ds(token + j, 1)],
                                            None, ALU.is_equal)
                ins.then_inc(one_i2_ready, 1)

            def weigh_early(g, e):
                dve.wait_ge(spread_done, g + 1)
                src = bank[:, 2 + e].rearrange("p (t k) -> p k t", t=4)
                at = spread[:, 0:EARLY, bass.ds(g * 4, 4)]
                dve.tensor_tensor(at, src[:, 0:EARLY, :], at, ALU.mult).then_inc(spread_weighed, 1)

            dve.wait_ge(u_out, EARLY)
            for e in range(2):
                one_hots(e, 4 * e)
            with dve.Fori(1, T // 8) as i:
                for e in range(2):
                    weigh_early(i * 2 + (e - 2), e)
                    one_hots(e, i * 8 + 4 * e)
            for e in range(2):
                weigh_early(T // 4 - 2 + e, e)

            dve.wait_ge(spread_out, T // 4)
            with dve.Fori(EARLY // 2, KEYS // 2) as i:
                for s in range(2):
                    dve.wait_ge(u_out, i * 2 + (s + 1))
                    at = spread[:, bass.ds(i * 2 + s, 1), :].rearrange("p o t -> p (o t)")
                    dve.tensor_tensor(at, at, acted[:, s, :], ALU.mult).then_inc(u_weighed, 1)

            def column_lo(s, j):
                dve.wait_ge(wcol_hi_ready, j + 1)
                at = spread[:, bass.ds(j, 1), :].rearrange("p o t -> p (o t)")
                dve.tensor_tensor(wcol_lo[s][:], at, wcol_hi[s][:].bitcast(F32), ALU.subtract).then_inc(wcol_ready, 1)

            def rest(i, s, c):
                dve.wait_ge(hi_ready, i * 8 + (N_V + 4 * s + c + 1))
                dve.tensor_tensor(lo[c][:], raw[2 * s + c // 2][:, c % 2 * PART:(c % 2 + 1) * PART],
                                  hi[c][:].bitcast(F32), ALU.subtract).then_inc(v_lo_ready, 1)

            column_lo(0, 0)
            with dve.Fori(0, KEYS // 2 - 1) as i:
                for s in range(2):
                    for c in range(4):
                        rest(i, s, c)
                    column_lo(1 - s, i * 2 + (s + 1))
            for s in range(2):
                for c in range(4):
                    rest(KEYS // 2 - 1, s, c)
                if s == 0:
                    column_lo(1, KEYS - 1)
            dve.wait_ge(parts_used, N_V + 4 * KEYS)
            dve.wait_ge(resid_in, 16)
            for b in range(TB):
                for c in range(4):
                    xc = resid[:, b, c * 512:(c + 1) * 512]
                    dve.tensor_tensor(xc, bank[:, 4 * b + c], xc, ALU.add).then_inc(out_ready, 1)

        @block.gpsimd
        def _(pool):
            pool.wait_ge(small_in_s, 32)
            w_s = par("sg_w").rearrange("p (h t) -> p h t", h=SG_HEADS)
            causal = con("causal").rearrange("p (o t) -> p o t", o=1).broadcast_to([P, SG_HEADS, P])
            pool.tensor_tensor(w_s, w_s, causal, ALU.mult).then_inc(sgw_ready, 1)

            def rest(i, k):
                pool.wait_ge(hi_ready, i * 8 + (k + 1))
                pool.tensor_tensor(lo[k % SPLIT][:], raw[k // 2][:, k % 2 * PART:(k % 2 + 1) * PART],
                                   hi[k % SPLIT][:].bitcast(F32), ALU.subtract).then_inc(lo_ready, 1)

            def rests(first, last):
                with pool.Fori(first // 8, last // 8) as i:
                    for k in range(8):
                        rest(i, k)

            rests(0, N_OUT)
            for k in range(4):
                rest(N_OUT // 8, k)
            pool.wait_ge(gates_done, TB)
            pool.memset(hid[:].rearrange("p k g n -> p (k g n)"), 0.0).then_inc(hid_zero, 1)
            pool.wait_ge(rows_ln, 32)
            for b in range(TB):
                v = proj[:, b, C_V:C_V + D_SG]
                pool.wait_ge(v_centred, b + 1)
                pool.tensor_tensor(v, v, lnG[:], ALU.mult).then_inc(pool_step, 1)
                pool.wait_ge(pool_step, b + 1)
                pool.tensor_tensor(v, v, lnB[:], ALU.add).then_inc(v_ready, 1)
            for k in range(4, 8):
                rest(N_OUT // 8, k)
            rests(N_OUT + 8, N_V)


def bucket_of(distance):
    if distance < BUCKETS // 2:
        return distance
    edges = (16, 21, 27, 35, 46, 59, 77, 99, 128, 166, 216)
    return BUCKETS // 2 - 1 + sum(distance >= e for e in edges)


def constants():
    import numpy as np

    c = np.zeros((P, CONST_N), np.float32)

    def put(name, a):
        c[:a.shape[0], CONST[name][0]:CONST[name][0] + a.shape[1]] = a

    put("eye", np.eye(P, dtype=np.float32))
    put("iota", np.tile(np.arange(P, dtype=np.float32), (P, 1)))
    put("causal", np.triu(np.ones((P, P), np.float32)))
    put("own", np.repeat(np.eye(REP, dtype=np.float32), 32, axis=0))
    put("seen", (np.arange(P) >= CMP_BLOCK - 1).astype(np.float32)[:, None])
    one = np.zeros((BUCKETS + 1, SPAN), np.float32)
    for m in range(SPAN):
        one[bucket_of(255 - m) if m <= 255 else BUCKETS, m] = 1.0
    put("bucket", one)
    return c


def kernel(x, attn_norm_g, w_in, q_norm_g, k_norm_g, cmp_pe_k, cmp_w1_k, cmp_w2_k, cmp_pe_v, cmp_w1_v, cmp_w2_v,
           rel_bias, sg_ln_g, sg_ln_b, sg_w, sg_b, out_norm_nsa, out_norm_sg, w_out, ffn_norm_g, peer_w_query,
           peer_sub_keys, peer_u, peer_v):
    import numpy as np
    import concourse.bacc as bacc
    from concourse.bass_utils import run_bass_kernel_spmd

    def halves(w):
        n = w.shape[1] // PART
        t = w.reshape(DC // 2, 2, P, n, PART).transpose(3, 0, 2, 1, 4)
        return t.reshape(n * DC // 2, P, HALF)

    def cmp_halves(w1):
        t = w1.reshape(KV, 2, 8, 2, HD, P).transpose(0, 1, 3, 4, 2, 5)
        return t.reshape(2 * KV, P, HALF)

    w_in, w_out, w_query = (np.asarray(w) for w in (w_in, w_out, peer_w_query))
    q_end = D_NSA
    kv_end = q_end + 6 * D_KV
    g_end = kv_end + GATES
    u_end = g_end + D_SG
    main = np.concatenate([w_in[:, q_end:kv_end], w_in[:, :q_end], w_in[:, u_end:], w_in[:, g_end:u_end]], axis=1)
    tiles = np.concatenate([halves(main), halves(w_out), halves(w_query)], axis=0)
    u_tiles = np.asarray(peer_u).reshape(KEYS, KEYS, 2, 8, P).transpose(1, 2, 4, 3, 0).reshape(2 * KEYS, P, HALF)

    small = np.zeros((P, SMALL_N), np.float32)

    def put(name, a):
        small[:a.shape[0], SMALL[name][0]:SMALL[name][0] + a.shape[1]] = a

    put("q_g", np.tile(np.asarray(q_norm_g), 2)[:, None])
    put("k_g", np.tile(np.asarray(k_norm_g), (1, 2)).T)
    put("sg_b", np.asarray(sg_b).T)
    put("rel", np.concatenate([np.asarray(rel_bias), np.full((1, HEADS), NEG, np.float32)], axis=0))
    w2 = np.stack([np.asarray(cmp_w2_k), np.asarray(cmp_w2_v)])
    put("w2", w2.transpose(2, 0, 1, 3).reshape(P, -1))
    pe = np.stack([np.asarray(cmp_pe_k), np.asarray(cmp_pe_v)])
    put("pe", pe.reshape(2, CMP_BLOCK, 2, 2, HD).transpose(3, 4, 0, 2, 1).reshape(P, -1))
    put("subkeys", np.asarray(peer_sub_keys).transpose(2, 0, 1).reshape(P, -1))
    put("sg_w", np.asarray(sg_w).transpose(2, 0, 1).reshape(P, -1))
    put("w_gate", w_in[:, kv_end:g_end].reshape(DC, P, GATES).transpose(1, 0, 2).reshape(P, -1))

    arrays = {
        "x": np.asarray(x).reshape(T, D), "tiles": tiles,
        "cmp_tiles": np.concatenate([cmp_halves(np.asarray(cmp_w1_k)), cmp_halves(np.asarray(cmp_w1_v))]),
        "u_tiles": u_tiles, "peer_v": np.asarray(peer_v), "small": small, "const": constants(),
        "attn_g": np.asarray(attn_norm_g), "out_g": np.concatenate([np.asarray(out_norm_nsa), np.asarray(out_norm_sg)]),
        "ffn_g": np.asarray(ffn_norm_g), "ln_g": np.asarray(sg_ln_g).reshape(-1), "ln_b": np.asarray(sg_ln_b).reshape(-1),
    }
    arrays = {f"in_{k}": np.ascontiguousarray(v) for k, v in arrays.items()}
    nc = bacc.Bacc("TRN2", target_bir_lowering=False, num_devices=1)
    args = [nc.dram_tensor(k, v.shape, mybir.dt.from_np(v.dtype), kind="ExternalInput").ap() for k, v in arrays.items()]
    bias_rows = nc.dram_tensor("bias_rows", (P, HEADS, SPAN), F32, kind="Internal").ap()
    resid_dram = nc.dram_tensor("resid_dram", (T, D), F32, kind="Internal").ap()
    out = nc.dram_tensor("out", (T, D), F32, kind="ExternalOutput").ap()
    peer_layer(nc, *args, bias_rows, resid_dram, out)
    r = run_bass_kernel_spmd(nc, [arrays], core_ids=[0])
    return r.results[0]["out"].reshape(1, T, D)
```

```python
from contextlib import ExitStack

import concourse.bass as bass
from concourse import mybir

ALU = mybir.AluOpType
ACT = mybir.ActivationFunctionType
F32 = mybir.dt.float32
F32R = mybir.dt.float32r
U32 = mybir.dt.uint32
AX = mybir.AxisListType

P = 128
D = 2048
T = 256
TB = T // P
DC = D // P
HEADS, KV, HD = 16, 4, 64
D_NSA, D_KV, D_SG = HEADS * HD, KV * HD, 1024
SG_HEADS = 8
CMP_STRIDE = 16
CMP_BLOCK = 32
NCMP = T // CMP_STRIDE - 1
BUCKETS = 32
REP = HEADS // KV
GATES = 3 * HEADS
PEER_HEADS, TOPK, KEYS = 8, 16, 128
EPS = 1e-6
NEG = -1e30

PART = 512
HALF = 2 * PART
G_IN = 9
G_OUT = D // PART
G_QUERY = PEER_HEADS * 2 * KEYS // PART
N_OUT = DC * G_IN
N_QUERY = N_OUT + DC * G_OUT
N_U = N_QUERY + DC * G_QUERY
N_V = N_U + 4 * KEYS
RAW = 4
SPLIT = 4
N_CMP = 2 * 2 * KV
CMP_RING = 3
UNITS = TB * PEER_HEADS
SOFT_AT = 44
EARLY = 48
HELD = 12
LATE = EARLY + HELD
N_LATE = N_U + 4 * LATE
SPREAD_LOOPS = 2
SPREAD_GROUPS = T // 4 // SPREAD_LOOPS
SPREAD_PARTS = 4 * HELD // SPREAD_LOOPS

C_KC, C_VC, C_KS, C_VS, C_KW, C_VW, C_Q, C_V, C_U = 0, 256, 512, 768, 1024, 1280, 1536, 2560, 3584
PROJ = 4608

SMALL = {}
_at = 0
for _name, _n in (("q_g", 1), ("k_g", 3), ("sg_b", SG_HEADS), ("rel", HEADS),
                  ("w2", 2 * KV * HD), ("pe", 2 * 2 * CMP_BLOCK), ("subkeys", 2 * KEYS),
                  ("sg_w", SG_HEADS * P), ("w_gate", DC * GATES)):
    SMALL[_name] = (_at, _n)
    _at += _n
SMALL_N = _at
SPAN = 384
CONST = {}
_at = 0
for _name, _n in (("eye", P), ("iota", P), ("causal", P), ("own", REP), ("seen", 1), ("bucket", SPAN)):
    CONST[_name] = (_at, _n)
    _at += _n
CONST_N = _at


def peer_layer(nc, x, tiles, cmp_tiles, u_tiles, peer_v, small_in, const_in, attn_g, out_g, ffn_g, ln_g, ln_b,
               bias_rows, resid_dram, out):
    with ExitStack() as ctx:
        base = 16512

        def sb(name, offset, shape, dt=F32):
            return nc.alloc_sbuf_tensor_at(name, shape, dt, offset=base + offset)

        def sem(name):
            return ctx.enter_context(nc.semaphore(name))

        K = 1024
        raw = [sb(f"raw{s}", s * 4 * K, [P, HALF]) for s in range(RAW)]
        hi = [sb(f"hi{s}", (16 + 2 * s) * K, [P, PART], F32R) for s in range(SPLIT)]
        lo = [sb(f"lo{s}", (24 + 2 * s) * K, [P, PART], F32R) for s in range(SPLIT)]
        consts = sb("consts", 32 * K, [P, CONST_N])
        stats = sb("stats", 35 * K + 256, [P, 128])
        A = 35 * K + 768
        picked = sb("picked", A, [P, 3, UNITS * TOPK])
        soft = sb("soft", A + 3 * K, [P, UNITS * TOPK])
        slotsT = sb("slotsT", A, [P, 3, T])
        wcol_hi = [sb(f"wcol_hi{e}", A + e * K, [P, T], F32R) for e in range(2)]
        wcol_lo = [sb(f"wcol_lo{e}", A + (2 + e) * K, [P, T], F32R) for e in range(2)]
        B = A + 4 * K
        cmp_w1 = [sb(f"cmp_w1_{s}", A + 4 * K * s, [P, HALF]) for s in range(CMP_RING)]
        sc = sb("sc", B, [P, 2, KEYS])
        sc_rest = sb("sc_rest", B + K, [P, 2, KEYS])
        cand = sb("cand", B + 2 * K, [P, TOPK, TOPK])
        cand_rest = sb("cand_rest", B + 3 * K, [P, TOPK * TOPK])
        hit = sb("hit", B + 4 * K, [P, 2, TOPK, TOPK])
        best = sb("best", B + 6 * K, [P, 2, TOPK])
        best_at = sb("best_at", B + 6 * K + 128, [P, 2, TOPK], U32)
        best_f = sb("best_f", B + 6 * K + 256, [P, 2, TOPK])
        pos = sb("pos", B + 6 * K + 384, [P, TOPK], U32)
        pos2 = sb("pos2", B + 6 * K + 448, [P, 2, TOPK], U32)
        pos_f = sb("pos_f", B + 6 * K + 576, [P, 2, TOPK])
        chosen = sb("chosen", B + 7 * K, [P, 3, TOPK])
        one_i1 = sb("one_i1", B, [P, 2, 4, P])
        one_i2 = sb("one_i2", B + 4 * K, [P, 2, 4, P])
        acted = sb("acted", B, [P, 2, T])
        C = B + 8 * K
        xT_hi = sb("xT_hi", C, [P, DC, T], F32R)
        xT_lo = sb("xT_lo", C + 16 * K, [P, DC, T], F32R)
        vc_own = sb("vc_own", C, [P, KV, REP, HD])
        kcT = sb("kcT", C + 4 * K, [P, KV, 32])
        pc = sb("pc", C + 5 * K, [P, HEADS, 32])
        pcT = sb("pcT", C + 7 * K, [P, KV, P])
        kcs = sb("kcs", C + 9 * K, [P, KV, HD])
        oT = sb("oT", C + 10 * K, [P, 2, 4, P])
        biased = sb("biased", C + 18 * K, [P, 2, 2, T])
        probs = sb("probs", C + 22 * K, [P, 2, 2, T])
        probsT = sb("probsT", C + 26 * K, [P, 2, 4, P])
        resid = sb("resid", C, [P, TB, D])
        E = C + 32 * K
        spread = sb("spread", E, [P, KEYS, T])
        xs = sb("xs", E, [P, TB, D])
        proj = sb("proj", E + 16 * K, [P, TB, PROJ])
        h0 = sb("h0", E + 16 * K, [P, TB, D])
        hn = sb("hn", E + 16 * K, [P, TB, D])
        bias = sb("bias", E + 52 * K, [P, HEADS, T])
        qT = sb("qT", E + 68 * K, [P, HEADS // 2, T])
        kT = sb("kT", E + 76 * K, [P, 2, KV, T])
        queryT = sb("queryT", E + 76 * K, [P, 2, 4, T])
        small = sb("small", E + 84 * K, [P, SMALL_N])
        gates = sb("gates", E + 95 * K, [P, TB, GATES])
        sums = sb("sums", E + 95 * K + 384, [P, TB, 2, HEADS])
        branch_w = sb("branch_w", E + 95 * K + 640, [P, 2, 2])
        wg_hi = sb("wg_hi", E + 96 * K, [P, DC, GATES], F32R)
        wg_lo = sb("wg_lo", E + 99 * K, [P, DC, GATES], F32R)
        kv_pe = sb("kv_pe", E + 102 * K, [P, 2, 2, KV, T // 2])
        gatesT = sb("gatesT", E + 102 * K, [P, T])
        lnG = sb("lnG", E + 110 * K, [P, D_SG])
        lnB = sb("lnB", E + 114 * K, [P, D_SG])
        squares = sb("squares", E + 110 * K, [P, 1024])
        row_g = sb("row_g", E + 118 * K, [P, D])
        hid_rows = sb("hid_rows", E + 118 * K, [P, 2, KV * P])
        hid = sb("hid", E + 122 * K, [P, 2, KV, P])
        bias_heads = sb("bias_heads", E + 126 * K, [P, SPAN])
        scratch = sb("scratch", E + 126 * K, [P, 512])
        scores = sb("scores", E + 112 * K, [P, UNITS, 2, KEYS])

        bank = ctx.enter_context(nc.psum_tensor("bank", [P, 8, 512], F32))

        def par(name, rows=P):
            a, n = SMALL[name]
            return small[0:rows, a:a + n]

        def con(name, rows=P):
            a, n = CONST[name]
            return consts[0:rows, a:a + n]

        eye = con("eye")

        x_in = [sem(f"x_in{b}") for b in range(TB)]
        small_in_s = sem("small_in")
        const_in_s = sem("const_in")
        rows_ln = sem("rows_ln")
        gain_in = sem("gain_in")
        raw_in = [sem(f"raw_in{s}") for s in range(RAW)]
        hi_ready = sem("hi_ready")
        lo_ready = sem("lo_ready")
        late_lo_ready = sem("late_lo_ready")
        parts_used = sem("parts_used")
        cmp_in = [sem(f"cmp_in{s}") for s in range(CMP_RING)]
        cmp_used = sem("cmp_used")
        xT_hi_part = sem("xT_hi_part")
        wg_hi_ready = sem("wg_hi_ready")
        wg_ready = sem("wg_ready")
        var_ready = sem("var_ready")
        root_ready = sem("root_ready")
        squares_ready = sem("squares_ready")
        norm_ready = sem("norm_ready")
        rows_scaled = sem("rows_scaled")
        rows_normed = sem("rows_normed")
        rows_scaled_pool = sem("rows_scaled_pool")
        turned_x = sem("turned_x")
        xT_part = sem("xT_part")
        group_out_act = sem("group_out_act")
        group_out_dve = sem("group_out_dve")
        gates_done = sem("gates_done")
        gates_copied = sem("gates_copied")
        gates_turned = sem("gates_turned")
        gates_exp = sem("gates_exp")
        bias_rows_done = sem("bias_rows_done")
        bias_rows_out = sem("bias_rows_out")
        bias_stored = sem("bias_stored")
        bias_in = sem("bias_in")
        kn_ready = sem("kn_ready")
        qn_ready = sem("qn_ready")
        turned_kq = sem("turned_kq")
        kq_out = sem("kq_out")
        gelu_done = sem("gelu_done")
        v_ready = sem("v_ready")
        sgw_ready = sem("sgw_ready")
        mixed_done = sem("mixed_done")
        sg_out = sem("sg_out")
        turned_kv = sem("turned_kv")
        kv_pe_ready = sem("kv_pe_ready")
        hid_acted = sem("hid_acted")
        hid_turned = sem("hid_turned")
        hid_zero = sem("hid_zero")
        hid_ready = sem("hid_ready")
        cmp_done = sem("cmp_done")
        kc_ready = sem("kc_ready")
        kc_turned = sem("kc_turned")
        kc_out = sem("kc_out")
        cmp_scored = sem("cmp_scored")
        cmp_shifted = sem("cmp_shifted")
        cmp_exp = sem("cmp_exp")
        cmp_weighed = sem("cmp_weighed")
        cmp_turned = sem("cmp_turned")
        cmp_out = sem("cmp_out")
        scored = sem("scored")
        biased_ready = sem("biased_ready")
        probs_ready = sem("probs_ready")
        probs_scaled = sem("probs_scaled")
        probs_turned = sem("probs_turned")
        probsT_ready = sem("probsT_ready")
        valued = sem("valued")
        oT_out = sem("oT_out")
        half_turned = sem("half_turned")
        half_out = sem("half_out")
        dve_step = sem("dve_step")
        choice_step = sem("choice_step")
        query_out_act = sem("query_out_act")
        query_out_dve = sem("query_out_dve")
        keyed = sem("keyed")
        keyed_out_act = sem("keyed_out_act")
        keyed_out_dve = sem("keyed_out_dve")
        soft_shifted = sem("soft_shifted")
        soft_exp = sem("soft_exp")
        weights_ready = sem("weights_ready")
        slots_turned = sem("slots_turned")
        one_i1_ready = sem("one_i1_ready")
        one_i2_ready = sem("one_i2_ready")
        spread_done = sem("spread_done")
        spread_weighed = sem("spread_weighed")
        spread_free = sem("spread_free")
        u_out = sem("u_out")
        u_weighed = sem("u_weighed")
        wcol_hi_ready = sem("wcol_hi_ready")
        wcol_ready = sem("wcol_ready")
        resid_stored = sem("resid_stored")
        resid_in = sem("resid_in")
        out_ready = sem("out_ready")
        out_stored = sem("out_stored")

        N_UNITS_ATT = TB * HEADS
        x_rows = x.rearrange("(b p) d -> p b d", p=P)
        out_rows = out.rearrange("(b p) d -> p b d", p=P)
        resid_rows = resid_dram.rearrange("(b p) d -> p b d", p=P)
        v_tiles = peer_v.rearrange("(p j) (h d) -> (j h) p d", j=KEYS, h=2)

        def tb_cols(b):
            return slice(b * P, (b + 1) * P)

        block = ctx.enter_context(nc.Block())

        @block.sync
        def _(sp):
            sp.dma_start(xs[:, 0], x_rows[:, 0]).then_inc(x_in[0], 16)
            sp.dma_start(row_g[:], attn_g.partition_broadcast(P)).then_inc(gain_in, 16)
            for s in range(RAW):
                sp.dma_start(raw[s][:], tiles[s]).then_inc(raw_in[s], 16)
            for s in range(CMP_RING):
                sp.dma_start(cmp_w1[s][:], cmp_tiles[s]).then_inc(cmp_in[s], 16)
            def load(src, i, s, split, before):
                sp.wait_ge(split, before + 2 * (s + 1 - RAW))
                sp.dma_start(raw[s][:], src[i * RAW + s]).then_inc(raw_in[s], 16)

            def loads(src, first, last, split, before):
                with sp.Fori(first, last) as i:
                    for s in range(RAW):
                        load(src, i, s, split, i * (2 * RAW) + before)

            loads(tiles, 1, N_OUT // (2 * RAW) - 1, lo_ready, 0)
            for k in range(CMP_RING, N_CMP):
                sp.wait_ge(cmp_used, k + 1 - CMP_RING)
                sp.dma_start(cmp_w1[k % CMP_RING][:], cmp_tiles[k]).then_inc(cmp_in[k % CMP_RING], 16)
            loads(tiles, N_OUT // (2 * RAW) - 1, N_U // (2 * RAW), lo_ready, 0)
            loads(u_tiles, 0, LATE // 2 + 1, lo_ready, N_U)
            loads(u_tiles, LATE // 2 + 1, KEYS // 2, late_lo_ready, N_U - N_LATE)
            for s in range(RAW):
                load(v_tiles, 0, s, late_lo_ready, N_V - N_LATE)
            sp.wait_ge(parts_used, N_V)
            sp.dma_start(resid[:], resid_rows).then_inc(resid_in, 16)
            loads(v_tiles, 1, KEYS // 2, late_lo_ready, N_V - N_LATE)
            for c in range(4):
                for b in range(TB):
                    at = slice(c * 512, (c + 1) * 512)
                    sp.wait_ge(out_ready, 2 * c + b + 1)
                    sp.dma_start(out_rows[:, b, at], resid[:, b, at]).then_inc(out_stored, 16)
            sp.wait_ge(out_stored, 16 * 4 * TB)

        @block.tensor
        def _(pe):
            def split_part(n):
                pe.wait_ge(lo_ready, n + 1)
                return hi[n % SPLIT][:], lo[n % SPLIT][:]

            def passes(out_, left, right, start, stop):
                pe.matmul(out_, left[0], right[0], start=start, stop=False, skip_group_check=True)
                pe.matmul(out_, left[0], right[1], start=False, stop=False, skip_group_check=True)
                return pe.matmul(out_, left[1], right[0], start=False, stop=stop, skip_group_check=True)

            def turn_rows(src, first, scaled):
                for m in range(first, first + 2 * DC // 4):
                    b, k = divmod(m - first, DC // 4)
                    pe.wait_ge(scaled[b][0], scaled[b][1] + k + 1)
                    if m >= 4:
                        pe.wait_ge(xT_part, m - 3)
                    for c in range(4):
                        mm = pe.transpose(bank[:, m % 4, c * P:(c + 1) * P], src(b, 4 * k + c), eye)
                    mm.then_inc(turned_x, 1)

            def product(G, k):
                w = split_part(DC * G + k)
                for b in range(TB):
                    mm = passes(bank[:, 4 + 2 * (G % 2) + b], [xT_hi[:, k, tb_cols(b)], xT_lo[:, k, tb_cols(b)]],
                                w, start=(k == 0), stop=(k == DC - 1))
                mm.then_inc(parts_used, 1)

            pe.wait_ge(const_in_s, 16)
            turn_rows(lambda b, c: h0[:, b, c * P:(c + 1) * P], 0,
                      ((rows_scaled, 0), (rows_scaled_pool, 0)))

            pe.wait_ge(small_in_s, 16)
            rel = par("rel", BUCKETS + 1)
            pe.matmul(bank[0:HEADS, 7, 0:SPAN], rel, con("bucket", BUCKETS + 1), start=True, stop=True)\
              .then_inc(bias_rows_done, 1)

            def turn_compressed():
                pe.wait_ge(group_out_act, 1)
                pe.wait_ge(group_out_dve, 1)
                for b in range(TB):
                    for k in range(4):
                        mm = pe.transpose(bank[:, b, tb_cols(k)], proj[:, b, k * P:(k + 1) * P], eye)
                    mm.then_inc(turned_kv, 1)

            def turn_keys():
                pe.wait_ge(kn_ready, 2)
                pe.wait_ge(bias_rows_out, 1)
                for b in range(TB):
                    for r, c0 in enumerate((C_KS, C_KW)):
                        for gp in range(2):
                            mm = pe.transpose(bank[:, 2 + b, (2 * r + gp) * P:(2 * r + gp + 1) * P],
                                              proj[:, b, c0 + gp * P:c0 + (gp + 1) * P], eye)
                    mm.then_inc(turned_kq, 1)

            def turn_queries():
                pe.wait_ge(qn_ready, 2)
                pe.wait_ge(kv_pe_ready, 4)
                pe.wait_ge(kq_out, 8)
                for m in range(4):
                    b, half = divmod(m, 2)
                    for k in range(4):
                        c0 = C_Q + (4 * half + k) * P
                        mm = pe.transpose(bank[:, m, tb_cols(k)], proj[:, b, c0:c0 + P], eye)
                    mm.then_inc(turned_kq, 1)

            def compress():
                pe.wait_ge(kq_out, 10)
                for kvg in range(2 * KV):
                    kvi, g = divmod(kvg, KV)
                    for ih in range(2):
                        k = 2 * kvg + ih
                        pe.wait_ge(cmp_in[k % CMP_RING], 16 * (k // CMP_RING + 1))
                        w = cmp_w1[k % CMP_RING]
                        for i in range(8):
                            a = 8 * ih + i
                            mm = pe.matmul(bank[0:NCMP, kvi, tb_cols(g)],
                                           kv_pe[:, ih, kvi, g, a:a + 8 * (NCMP - 1) + 1:8], w[:, i * P:(i + 1) * P],
                                           start=(ih == 0 and i == 0), stop=(ih == 1 and i == 7))
                        mm.then_inc(cmp_used, 1)

            pe.wait_ge(xT_part, 8)
            for G in range(G_IN):
                if G >= 2:
                    pe.wait_ge(group_out_act, G - 1)
                    pe.wait_ge(group_out_dve, G - 1)
                for c in range(DC):
                    product(G, c)
                if G == 1:
                    turn_compressed()
                if G == 4:
                    turn_keys()
                if G == 6:
                    turn_queries()
                if G == 7:
                    compress()
            pe.wait_ge(hid_acted, 2)
            for kvg in range(2 * KV):
                kvi, g = divmod(kvg, KV)
                mm = pe.transpose(bank[:, 0, kvg * 16:kvg * 16 + NCMP], hid_rows[0:NCMP, kvi, tb_cols(g)],
                                  eye[0:NCMP, 0:NCMP])
            mm.then_inc(hid_turned, 1)
            pe.wait_ge(kq_out, 12)
            pe.wait_ge(wg_ready, 1)
            for c in range(DC):
                mm = passes(bank[0:GATES, 2, 0:T], [wg_hi[:, c, :], wg_lo[:, c, :]], [xT_hi[:, c, :], xT_lo[:, c, :]],
                            start=(c == 0), stop=(c == DC - 1))
            mm.then_inc(gates_done, 1)
            pe.wait_ge(hid_ready, 1)
            w2 = par("w2").rearrange("p (k g d) -> p k g d", k=2, g=KV)
            for kvi in range(2):
                for g in range(KV):
                    mm = pe.matmul(bank[:, 1, (kvi * KV + g) * HD:(kvi * KV + g + 1) * HD], hid[:, kvi, g, :],
                                   w2[:, kvi, g, :], start=True, stop=True)
            mm.then_inc(cmp_done, 1)
            pe.wait_ge(v_ready, 2)
            pe.wait_ge(sgw_ready, 1)
            pe.wait_ge(group_out_act, G_IN)
            pe.wait_ge(group_out_dve, G_IN)
            w_s = par("sg_w").rearrange("p (h t) -> p h t", h=SG_HEADS)
            for h in range(SG_HEADS):
                pe.matmul(bank[:, 4 + h // 2, (h % 2) * T:(h % 2 + 1) * T], w_s[:, h, :],
                          proj[:, :, C_V + h * P:C_V + (h + 1) * P], start=True, stop=True).then_inc(mixed_done, 1)
            pe.wait_ge(kc_ready, 1)
            for gp in range(2):
                mm = pe.transpose(bank[:, 0, gp * 32:gp * 32 + 32],
                                  kcs[0:32, 2 * gp:2 * gp + 2, :].rearrange("p g d -> p (g d)"), eye[0:32, 0:32])
            mm.then_inc(kc_turned, 1)

            pe.wait_ge(gates_copied, 1)
            for b in range(TB):
                mm = pe.transpose(bank[:, 3, b * GATES:(b + 1) * GATES], gatesT[0:GATES, tb_cols(b)],
                                  eye[0:GATES, 0:GATES])
            mm.then_inc(gates_turned, 1)
            pe.wait_ge(sg_out, SG_HEADS)
            pe.wait_ge(kc_out, 1)
            pe.wait_ge(gates_exp, 1)
            S0, PT0, O0, BACK, CMP = 0, 2, 4, 6, 7

            def score(u):
                b, h = divmod(u, HEADS)
                n = (b + 1) * P
                rows = slice(HD * (h % 2), HD * (h % 2) + HD)
                if u >= 2:
                    pe.wait_ge(biased_ready, u - 1)
                pe.matmul(bank[:, S0 + u % 2, 0:2 * n], qT[rows, h // 2, tb_cols(b)],
                          kT[rows, :, h // REP, 0:n], start=True, stop=True).then_inc(scored, 1)

            def turn_probs(u):
                b, h = divmod(u, HEADS)
                pe.wait_ge(probs_scaled, 2 * (u + 1))
                if u >= 2:
                    pe.wait_ge(probsT_ready, u - 1)
                for r in range(2):
                    for s in range(b + 1):
                        mm = pe.transpose(bank[:, PT0 + u % 2, tb_cols(r * (b + 1) + s)],
                                          probs[:, u % 2, r, tb_cols(s)], eye)
                mm.then_inc(probs_turned, 1)

            def value(u):
                b, h = divmod(u, HEADS)
                half = u // 8
                pe.wait_ge(probsT_ready, u + 1)
                if h == 0:
                    pe.wait_ge(cmp_out, b + 1)
                if h % 8 == 0 and half >= 2:
                    pe.wait_ge(oT_out, half - 1)
                o = bank[HD * (h % 2):HD * (h % 2) + HD, O0 + half % 2, tb_cols(h % 8 // 2)]
                g, r = divmod(h, REP)
                for k, c0 in enumerate((C_VS, C_VW)):
                    for s in range(b + 1):
                        pe.matmul(o, proj[:, s, c0 + g * HD:c0 + (g + 1) * HD], probsT[:, u % 2, k * (b + 1) + s, :],
                                  start=(k == 0 and s == 0), stop=False)
                pe.matmul(o, vc_own[:, g, r, :], pcT[:, g, :], start=False, stop=True).then_inc(valued, 1)

            def turn_back(half):
                pe.wait_ge(oT_out, half + 1)
                if half >= 1:
                    pe.wait_ge(half_out, half)
                for k in range(4):
                    mm = pe.transpose(bank[:, BACK, tb_cols(k)], oT[:, half % 2, k, :], eye)
                mm.then_inc(half_turned, 1)

            for u in range(N_UNITS_ATT + 3):
                if u % HEADS == 0 and u < N_UNITS_ATT:
                    b = u // HEADS
                    if b >= 1:
                        pe.wait_ge(cmp_shifted, b)
                    for pr in range(HEADS // 2):
                        mm = pe.matmul(bank[:, CMP, pr * 32:pr * 32 + 32], qT[:, pr, tb_cols(b)],
                                       kcT[:, pr // (REP // 2), :], start=True, stop=True)
                    mm.then_inc(cmp_scored, 1)
                if u < N_UNITS_ATT:
                    score(u)
                if 2 <= u < N_UNITS_ATT + 2:
                    turn_probs(u - 2)
                if u % HEADS == 1 and u < N_UNITS_ATT:
                    b = u // HEADS
                    pe.wait_ge(cmp_weighed, b + 1)
                    for g in range(KV):
                        mm = pe.transpose(bank[:, CMP, tb_cols(g)],
                                          pc[:, 4 * g:4 * g + 4, :].rearrange("p h n -> p (h n)"), eye)
                    mm.then_inc(cmp_turned, 1)
                if u >= 3:
                    value(u - 3)
                if u % 8 == 4 and u > 8:
                    turn_back(u // 8 - 1)
            turn_back(3)

            mix_col = lambda c: (C_Q if c < 8 else C_U - 8 * P) + c * P
            turn_rows(lambda b, c: proj[:, b, mix_col(c):mix_col(c) + P], 8,
                      ((rows_scaled, 4), (rows_scaled, 8)))
            pe.wait_ge(xT_part, 16)
            pe.wait_ge(half_out, 4)
            for k in range(G_OUT):
                G = G_IN + k
                if k >= 2:
                    pe.wait_ge(group_out_dve, G - 1)
                for c in range(DC):
                    product(G, c)

            turn_rows(lambda b, c: hn[:, b, c * P:(c + 1) * P], 16,
                      ((rows_scaled, 12), (rows_scaled_pool, 4)))
            pe.wait_ge(xT_part, 24)
            pe.wait_ge(group_out_dve, G_IN + G_OUT)
            subkeys = par("subkeys").rearrange("p (a k) -> p a k", a=2)

            def key_scores(k):
                pe.wait_ge(query_out_act, k + 1)
                pe.wait_ge(query_out_dve, k + 1)
                if k >= 1:
                    pe.wait_ge(keyed_out_act, k)
                    pe.wait_ge(keyed_out_dve, k)
                for b in range(TB):
                    for j in range(4):
                        mm = pe.matmul(bank[:, b, tb_cols(j)], queryT[:, k % 2, j, tb_cols(b)],
                                       subkeys[:, j % 2, :], start=True, stop=True)
                mm.then_inc(keyed, 1)

            for k in range(G_QUERY):
                if k >= 2:
                    pe.wait_ge(query_out_act, k - 1)
                    pe.wait_ge(query_out_dve, k - 1)
                for c in range(DC):
                    w = split_part(N_QUERY + DC * k + c)
                    for j in range(4):
                        mm = passes(bank[:, 4 + 2 * (k % 2) + j // 2, (j % 2) * T:(j % 2 + 1) * T],
                                    [v[:, tb_cols(j)] for v in w], [xT_hi[:, c, :], xT_lo[:, c, :]],
                                    start=(c == 0 and j % 2 == 0), stop=(c == DC - 1))
                    mm.then_inc(parts_used, 1)
                if k >= 1:
                    key_scores(k - 1)
            key_scores(G_QUERY - 1)

            def act_part(out_, r):
                for c in range(4):
                    k = 4 * r + c
                    mm = passes(out_, [v[r][:, tb_cols(c)] for v in (hi, lo)],
                                [xT_hi[:, k, :], xT_lo[:, k, :]], start=(k == 0), stop=(k == DC - 1))
                mm.then_inc(parts_used, 1)

            def act_tiles(bank0, first, last, split, before):
                with pe.Fori(first // 2, last // 2) as i:
                    for s in range(2):
                        pe.wait_ge(u_out, i * 2 + (s - 1))
                        for r in range(4):
                            pe.wait_ge(split, i * 8 + (N_U - before + 4 * s + r + 1))
                            act_part(bank[:, bank0 + s, 0:T], r)

            for s in range(2):
                for r in range(4):
                    pe.wait_ge(lo_ready, N_U + 4 * s + r + 1)
                    act_part(bank[:, 4 + s, 0:T], r)
            act_tiles(4, 2, EARLY, lo_ready, 0)

            pe.wait_ge(weights_ready, 1)
            for a in range(3):
                for b in range(TB):
                    src = picked[:, a, tb_cols(b)] if a < 2 else soft[:, tb_cols(b)]
                    mm = pe.transpose(bank[:, a // 2, (a % 2) * T + b * P:(a % 2) * T + (b + 1) * P], src, eye)
            mm.then_inc(slots_turned, 1)

            pe.wait_ge(u_out, EARLY)
            held = bank[:, 2:8].rearrange("p a b -> p (a b)")
            with pe.Fori(0, SPREAD_LOOPS) as i:
                for g in range(SPREAD_GROUPS):
                    e = g % 2
                    pe.wait_ge(one_i1_ready, i * SPREAD_GROUPS + (g + 1))
                    pe.wait_ge(one_i2_ready, i * SPREAD_GROUPS + (g + 1))
                    pe.wait_ge(spread_free, i * SPREAD_GROUPS + (g + 1))
                    for j in range(4):
                        mm = pe.matmul(bank[:, e, tb_cols(j)], one_i1[:, e, j, :], one_i2[:, e, j, :],
                                       start=True, stop=True)
                    mm.then_inc(spread_done, 1)
                    if g % 4 == 3:
                        continue
                    part = g - g // 4
                    pe.wait_ge(lo_ready, i * SPREAD_PARTS + (N_U + 4 * EARLY + part + 1))
                    act_part(held[:, bass.ds(i * (SPREAD_PARTS // 4 * T) + part // 4 * T, T)], part % 4)

            pe.wait_ge(spread_free, T // 4 + 2)
            for s in range(2):
                for r in range(4):
                    pe.wait_ge(late_lo_ready, 4 * s + r + 1)
                    act_part(bank[:, s, 0:T], r)
            act_tiles(0, LATE + 2, KEYS, late_lo_ready, N_LATE)

            def experts(s, c, first, last):
                for b in range(TB):
                    mm = passes(bank[:, 4 * b + c], [wcol_hi[s][:, tb_cols(b)], wcol_lo[s][:, tb_cols(b)]],
                                [hi[c][:], lo[c][:]], start=first, stop=last)
                mm.then_inc(parts_used, 1)

            pe.wait_ge(u_out, KEYS)
            for s in range(2):
                pe.wait_ge(wcol_ready, s + 1)
                for c in range(4):
                    pe.wait_ge(late_lo_ready, N_V - N_LATE + 4 * s + c + 1)
                    experts(s, c, s == 0, False)
            with pe.Fori(1, KEYS // 2 - 1) as i:
                for s in range(2):
                    pe.wait_ge(wcol_ready, i * 2 + (s + 1))
                    for c in range(4):
                        pe.wait_ge(late_lo_ready, i * 8 + (N_V - N_LATE + 4 * s + c + 1))
                        experts(s, c, False, False)
            for s in range(2):
                pe.wait_ge(wcol_ready, KEYS - 1 + s)
                for c in range(4):
                    pe.wait_ge(late_lo_ready, N_V - N_LATE + 4 * KEYS - 7 + 4 * s + c)
                    experts(s, c, False, s == 1)

        @block.scalar
        def _(act):
            act.dma_start(xs[:, 1], x_rows[:, 1]).then_inc(x_in[1], 16)
            act.dma_start(consts[:], const_in).then_inc(const_in_s, 16)
            act.dma_start(small[:], small_in).then_inc(small_in_s, 16)

            def round_part(n):
                act.wait_ge(raw_in[n // 2 % RAW], 16 * (n // (2 * RAW) + 1))
                if n >= SPLIT:
                    act.wait_ge(parts_used, n + 1 - SPLIT)
                act.copy(hi[n % SPLIT][:], raw[n // 2 % RAW][:, n % 2 * PART:(n % 2 + 1) * PART]).then_inc(hi_ready, 1)

            def round_at(n, i, stride):
                s = n // 2 % RAW
                act.wait_ge(raw_in[s], i * (16 * (stride // (2 * RAW))) + 16 * (n // (2 * RAW) + 1))
                act.wait_ge(parts_used, i * stride + (n + 1 - SPLIT))
                act.copy(hi[n % SPLIT][:], raw[s][:, n % 2 * PART:(n % 2 + 1) * PART]).then_inc(hi_ready, 1)

            def take_hi(m):
                b, k = divmod(m % 8, DC // 4)
                act.wait_ge(turned_x, m + 1)
                act.copy(xT_hi[:, 4 * k:4 * k + 4, tb_cols(b)], bank[:, m % 4].rearrange("p (c t) -> p c t", c=4))\
                   .then_inc(xT_hi_part, 1)

            roots = [0]

            def root(cols_):
                roots[0] += 1
                act.wait_ge(var_ready, roots[0])
                act.activation(stats[:, cols_], stats[:, cols_], ACT.Sqrt).then_inc(root_ready, 1)

            for b in range(TB):
                act.wait_ge(x_in[b], 16)
                act.activation(h0[:, b], xs[:, b], ACT.Square, accum_out=stats[:, b:b + 1]).then_inc(squares_ready, 1)
                root(slice(b, b + 1))

            def norm_second(dst, n, stat):
                act.wait_ge(norm_ready, n)
                for k in range(4):
                    at = slice(k * 512, (k + 1) * 512)
                    act.activation(dst[:, 1, at], xs[:, 1, at], ACT.Copy, scale=stats[:, stat:stat + 1])\
                       .then_inc(rows_normed, 1)

            norm_second(h0, 2, 1)
            act.dma_start(lnG[:], ln_g.partition_broadcast(P)).then_inc(rows_ln, 16)
            act.dma_start(lnB[:], ln_b.partition_broadcast(P)).then_inc(rows_ln, 16)
            for b in range(TB):
                for m in range(4 * b, 4 * b + 4):
                    take_hi(m)
                for n in range(2 * b, 2 * b + 2):
                    round_part(n)
            act.wait_ge(bias_rows_done, 1)
            act.copy(bias_heads[0:HEADS, :], bank[0:HEADS, 7, 0:SPAN]).then_inc(bias_rows_out, 1)
            act.copy(wg_hi[:].rearrange("p c n -> p (c n)"), par("w_gate")).then_inc(wg_hi_ready, 1)

            def gelu(k):
                g, b = divmod(k, 2)
                c0 = C_V + PART * g
                act.wait_ge(group_out_act, 6 + g)
                act.wait_ge(group_out_dve, 6 + g)
                act.activation(proj[:, b, c0:c0 + PART], proj[:, b, c0:c0 + PART], ACT.Gelu).then_inc(gelu_done, 1)

            for n in range(SPLIT, N_OUT + SPLIT):
                round_part(n)
                G, c = divmod(n, DC)
                if c == 2 and G >= 1:
                    act.wait_ge(parts_used, DC * G)
                    act.copy(proj[:, 0, (G - 1) * PART:G * PART], bank[:, 4 + 2 * ((G - 1) % 2)])\
                       .then_inc(group_out_act, 1)
                if G == 1 and c == 0:
                    act.wait_ge(bias_rows_out, 1)
                    act.dma_start(bias_rows, bias_heads[0:HEADS, :]).then_inc(bias_stored, 16)
                if G == 2 and c == 0:
                    act.wait_ge(bias_stored, 16)
                    act.dma_start(bias[:], bass.AP(bias_rows.tensor, 0, [[1, P], [SPAN, HEADS], [1, T]]))\
                       .then_inc(bias_in, 16)
                if G == 4 and c == 6:
                    root(slice(8, 24))
                if G == 6 and c == 6:
                    root(slice(24, 56))
                if G == 6 and c in (8, 10):
                    gelu((c - 8) // 2)
                if G == 7 and c in (4, 6):
                    gelu((c - 4) // 2 + 2)
                if G == 8 and c == 3:
                    for kvi in range(2):
                        act.wait_ge(cmp_used, N_CMP // 2 * (kvi + 1))
                        act.activation(hid_rows[0:NCMP, kvi], bank[0:NCMP, kvi], ACT.Gelu).then_inc(hid_acted, 1)
                if G == 8 and c in (6, 8):
                    gelu((c - 6) // 2 + 4)
                if G == 8 and c == 11:
                    root(slice(56, 72))
            for k in range(6, 8):
                gelu(k)
            act.wait_ge(gates_done, 1)
            act.copy(gatesT[0:GATES, :], bank[0:GATES, 2, 0:T]).then_inc(gates_copied, 1)
            root(slice(72, 76))
            act.wait_ge(gates_turned, 1)
            act.activation(gates[:].rearrange("p b n -> p (b n)"), bank[:, 3, 0:TB * GATES], ACT.Exp, scale=-1.0)\
               .then_inc(gates_exp, 1)

            act.wait_ge(cmp_done, 1)
            act.dma_start(row_g[:], out_g.partition_broadcast(P)).then_inc(gain_in, 16)

            def mean_square(b, c0, col):
                act.wait_ge(squares_ready, squared[0])
                squared[0] += 1
                act.activation(squares[:], proj[:, b, c0:c0 + 1024], ACT.Square, accum_out=stats[:, col:col + 1])\
                   .then_inc(squares_ready, 1)

            squared = [TB]
            act.wait_ge(sg_out, SG_HEADS)
            for b in range(TB):
                mean_square(b, C_U, 84 + b)
            root(slice(84, 86))

            def cmp_exps(b):
                act.wait_ge(cmp_shifted, b + 1)
                nv = 7 if b == 0 else NCMP
                act.activation(pc[:, :, 0:nv], pc[:, :, 0:nv], ACT.Exp).then_inc(cmp_exp, 1)

            def exps(u):
                b, h = divmod(u, HEADS)
                n = (b + 1) * P
                act.wait_ge(biased_ready, u + 1)
                if u >= 2:
                    act.wait_ge(probs_turned, u - 1)
                for r in range(2):
                    act.activation(probs[:, u % 2, r, 0:n], biased[:, u % 2, r, 0:n], ACT.Exp,
                                   bias=stats[:, 80 + 2 * (u % 2) + r:81 + 2 * (u % 2) + r],
                                   accum_out=sums[:, b, r, h:h + 1]).then_inc(probs_ready, 1)

            def probsT_copy(u):
                b, h = divmod(u, HEADS)
                act.wait_ge(probs_turned, u + 1)
                if u >= 2:
                    act.wait_ge(valued, u - 1)
                n = 2 * (b + 1)
                act.copy(probsT[:, u % 2, 0:n].rearrange("p a t -> p (a t)"), bank[:, 2 + u % 2, 0:n * P])\
                   .then_inc(probsT_ready, 1)

            def oT_copy(half):
                act.wait_ge(valued, 8 * (half + 1))
                if half >= 2:
                    act.wait_ge(half_turned, half - 1)
                act.copy(oT[:, half % 2].rearrange("p k t -> p (k t)"), bank[:, 4 + half % 2]).then_inc(oT_out, 1)

            for u in range(N_UNITS_ATT + 2):
                if u < N_UNITS_ATT:
                    if u % HEADS == 0:
                        cmp_exps(u // HEADS)
                    exps(u)
                if u >= 2:
                    probsT_copy(u - 2)
                if u % 8 == 3 and u > 8:
                    oT_copy(u // 8 - 1)
                if u == HEADS + 7:
                    act.wait_ge(half_out, 2)
                    mean_square(0, C_Q, 86)
                if u == HEADS + 9:
                    root(slice(86, 87))

            oT_copy(3)
            act.wait_ge(half_out, 4)
            mean_square(1, C_Q, 87)
            root(slice(87, 88))
            for m in range(8, 16):
                take_hi(m)
            act.dma_start(row_g[:], ffn_g.partition_broadcast(P)).then_inc(gain_in, 16)

            def residual_squares(k):
                act.wait_ge(group_out_dve, G_IN + k + 1)
                for b in range(TB):
                    at = slice(k * PART, (k + 1) * PART)
                    a = 92 + 4 * b + k
                    act.activation(hn[:, b, at], xs[:, b, at], ACT.Square, accum_out=stats[:, a:a + 1])\
                       .then_inc(squares_ready, 1)

            for n in range(N_OUT + SPLIT, N_QUERY + SPLIT):
                round_part(n)
                k, c = divmod(n - N_OUT, DC)
                if k >= 1 and c == 5:
                    residual_squares(k - 1)
            residual_squares(G_OUT - 1)
            act.dma_start(resid_rows, xs[:]).then_inc(resid_stored, 16)
            root(slice(88, 90))
            norm_second(hn, 3, 89)
            for m in range(16, 24):
                take_hi(m)

            def keyed_out(k):
                act.wait_ge(keyed, k + 1)
                act.copy(scores[:, 2 * k:2 * k + 2].rearrange("p u a k -> p (u a k)"), bank[:, 0])\
                   .then_inc(keyed_out_act, 1)

            for n in range(N_QUERY + SPLIT, N_U + SPLIT):
                round_part(n)
                k, c = divmod(n - N_QUERY, DC)
                if k >= 1 and c == 2:
                    act.wait_ge(parts_used, N_QUERY + DC * k)
                    if k >= 3:
                        act.wait_ge(keyed, k - 2)
                    act.copy(queryT[:, (k - 1) % 2, 0:2].rearrange("p j t -> p (j t)"), bank[:, 4 + 2 * ((k - 1) % 2)])\
                       .then_inc(query_out_act, 1)
                if k >= 2 and c == 3:
                    keyed_out(k - 2)
            keyed_out(G_QUERY - 1)

            act.wait_ge(resid_stored, 16)
            act.wait_ge(keyed_out_dve, G_QUERY)

            def tile_out(i, s, bank0, out_):
                for r in range(3):
                    round_at(N_U + 4 * s + 4 + r, i, 8)
                act.wait_ge(parts_used, i * 8 + (N_U + 4 * s + 4))
                act.activation(out_, bank[:, bank0 + s, 0:T], ACT.Gelu).then_inc(u_out, 1)
                round_at(N_U + 4 * s + 7, i, 8)

            def early_tiles(first, last):
                with act.Fori(first // 2, last // 2) as i:
                    for s in range(2):
                        tile_out(i, s, 4, spread[:, bass.ds(i * 2 + s, 1), :].rearrange("p o t -> p (o t)"))

            early_tiles(0, SOFT_AT)
            act.wait_ge(soft_shifted, 1)
            act.activation(soft[:], soft[:], ACT.Exp).then_inc(soft_exp, 1)
            early_tiles(SOFT_AT, EARLY)

            with act.Fori(0, SPREAD_LOOPS) as i:
                for g in range(SPREAD_GROUPS):
                    act.wait_ge(spread_weighed, i * SPREAD_GROUPS + (g + 1))
                    src = bank[:, g % 2].rearrange("p (t k) -> p k t", t=4)
                    act.copy(spread[:, EARLY:KEYS, bass.ds(i * (4 * SPREAD_GROUPS) + 4 * g, 4)], src[:, EARLY:KEYS, :])\
                       .then_inc(spread_free, 1)
                    if g % 4 != 3:
                        round_at(N_U + 4 * (EARLY + 1) + g - g // 4, i, SPREAD_PARTS)

            act.wait_ge(spread_weighed, T // 4)
            for t in range(HELD):
                act.wait_ge(parts_used, N_U + 4 * (EARLY + t + 1))
                if t >= 2:
                    act.wait_ge(u_weighed, t - 1)
                act.activation(acted[:, t % 2, :], bank[:, 2 + t // 2, t % 2 * T:(t % 2 + 1) * T], ACT.Gelu)\
                   .then_inc(u_out, 1)
                if t in (3, 6, 9):
                    round_part(N_LATE + 4 + t // 3 - 1)
            act.wait_ge(parts_used, N_LATE + 4)
            act.wait_ge(u_weighed, HELD - 1)
            act.activation(acted[:, 0, :], bank[:, 0, 0:T], ACT.Gelu).then_inc(u_out, 1)
            round_part(N_LATE + 7)
            act.wait_ge(u_weighed, HELD)
            tile_out(LATE // 2, 1, 0, acted[:, 1, :])
            with act.Fori(LATE // 2 + 1, KEYS // 2) as i:
                for s in range(2):
                    act.wait_ge(u_weighed, i * 2 + (s - 1 - EARLY))
                    tile_out(i, s, 0, acted[:, s, :])

            act.wait_ge(u_weighed, KEYS - EARLY)
            for s in range(2):
                act.copy(wcol_hi[s][:], spread[:, s, :]).then_inc(wcol_hi_ready, 1)
            with act.Fori(0, KEYS // 2 - 1) as i:
                for s in range(2):
                    for c in range(4):
                        round_at(N_V + 4 * s + 4 + c, i, 8)
                    act.copy(wcol_hi[s][:], spread[:, bass.ds(i * 2 + (s + 2), 1), :].rearrange("p o t -> p (o t)"))\
                       .then_inc(wcol_hi_ready, 1)
            for n in range(N_V + 4 * (KEYS - 1), N_V + 4 * KEYS):
                round_part(n)

        @block.vector
        def _(dve):
            step = [0]

            def link(ins):
                step[0] = step[0] + 1
                ins.then_inc(dve_step, 1)
                dve.wait_ge(dve_step, step[0])

            choice = [0]

            def link_choice(ins):
                choice[0] += 1
                ins.then_inc(choice_step, 1)
                dve.wait_ge(choice_step, choice[0])

            roots = [0]

            def variance(c, count):
                roots[0] += 1
                dve.tensor_scalar(stats[:, c], stats[:, c], 1.0 / count, EPS, ALU.mult, ALU.add).then_inc(var_ready, 1)

            def rstd(c, count=None):
                if count:
                    variance(c, count)
                dve.wait_ge(root_ready, roots[0])
                link(dve.reciprocal(stats[:, c], stats[:, c]))

            for b in range(TB):
                dve.wait_ge(squares_ready, b + 1)
                variance(slice(b, b + 1), D)
                dve.wait_ge(root_ready, roots[0])
                dve.reciprocal(stats[:, b:b + 1], stats[:, b:b + 1]).then_inc(norm_ready, 1)
                if b == 0:
                    dve.wait_ge(norm_ready, 1)
                    dve.wait_ge(gain_in, 16)
                    for k in range(4):
                        at = slice(k * 512, (k + 1) * 512)
                        dve.scalar_tensor_tensor(out=h0[:, 0, at], in0=xs[:, 0, at], scalar=stats[:, 0:1],
                                                 in1=row_g[:, at], op0=ALU.mult, op1=ALU.mult).then_inc(rows_scaled, 1)

            def take_lo(n):
                for m in range(n, n + 8):
                    b, k = divmod(m % 8, DC // 4)
                    dve.wait_ge(xT_hi_part, m + 1)
                    at = (slice(None), slice(4 * k, 4 * k + 4), tb_cols(b))
                    dve.tensor_tensor(xT_lo[at], bank[:, m % 4].rearrange("p (c t) -> p c t", c=4),
                                      xT_hi[at].bitcast(F32), ALU.subtract).then_inc(xT_part, 1)

            take_lo(0)
            dve.wait_ge(wg_hi_ready, 1)
            dve.tensor_tensor(wg_lo[:].rearrange("p c n -> p (c n)"), par("w_gate"),
                              wg_hi[:].rearrange("p c n -> p (c n)").bitcast(F32), ALU.subtract).then_inc(wg_ready, 1)

            def group_out(G):
                dve.wait_ge(parts_used, DC * (G + 1))
                dve.tensor_copy(proj[:, 1, G * PART:(G + 1) * PART], bank[:, 5 + 2 * (G % 2)])\
                   .then_inc(group_out_dve, 1)

            group_out(0)
            group_out(1)
            pe_code = par("pe").rearrange("p (k i) -> p k i", k=4)
            for b in range(TB):
                dve.wait_ge(turned_kv, b + 1)
                for ih in range(2):
                    for e in range(2):
                        rows = slice(HD * e, HD * e + HD)
                        for odd in range(2):
                            src = bank[rows, b].rearrange("p (k n i) -> p k n i", k=4, i=16)[:, :, :, odd::2]
                            dst = kv_pe[HD * odd:HD * odd + HD, ih].rearrange("p v g t -> p (v g) t")[:, e::2, :]
                            dst = dst[:, :, b * 64:(b + 1) * 64].rearrange("p k (n i) -> p k n i", i=8)
                            code = pe_code[rows, :, 16 * ih + odd:16 * ih + 16:2].rearrange("p k (o i) -> p k o i", o=1)
                            ins = dve.tensor_tensor(dst, src, code.broadcast_to([HD, 4, 8, 8]), ALU.add)
                    ins.then_inc(kv_pe_ready, 1)
            group_out(2)
            dve.wait_ge(group_out_act, 3)
            dve.wait_ge(group_out_dve, 3)
            dve.wait_ge(bias_stored, 16)
            k_both = lambda b: proj[:, b, C_KS:C_KS + 1024].rearrange("p (r n) -> p r n", r=2)[:, :, 0:D_KV]
            k_stat = lambda b: stats[:, 8 + 8 * b:16 + 8 * b]
            for b in range(TB):
                link(dve.tensor_tensor(scratch[:].rearrange("p (r n) -> p r n", r=2), k_both(b), k_both(b), ALU.mult))
                link(dve.tensor_reduce(k_stat(b), scratch[:].rearrange("p (g d) -> p g d", d=HD), AX.X, ALU.add))
            group_out(3)
            rstd(slice(8, 24), HD)
            for b in range(TB):
                for r in range(2):
                    v = proj[:, b, C_KS + 512 * r:C_KS + 512 * r + D_KV].rearrange("p (g d) -> p g d", d=HD)
                    s = stats[:, 8 + 8 * b + 4 * r:12 + 8 * b + 4 * r].rearrange("p (g o) -> p g o", o=1)
                    ins = dve.tensor_tensor(v, v, s.broadcast_to([P, KV, HD]), ALU.mult)
                ins.then_inc(kn_ready, 1)
            group_out(4)
            dve.wait_ge(group_out_act, 5)
            dve.wait_ge(group_out_dve, 5)
            for b in range(TB):
                for half in range(2):
                    q = proj[:, b, C_Q + 512 * half:C_Q + 512 * half + 512]
                    link(dve.tensor_tensor(scratch[:], q, q, ALU.mult))
                    a = 24 + 16 * b + 8 * half
                    link(dve.tensor_reduce(stats[:, a:a + 8], scratch[:].rearrange("p (g d) -> p g d", d=HD),
                                           AX.X, ALU.add))
            for b in range(TB):
                dve.wait_ge(turned_kq, b + 1)
                for src_half in range(2):
                    for dst_half in range(2):
                        sr, dr = slice(64 * src_half, 64 * src_half + 64), slice(64 * dst_half, 64 * dst_half + 64)
                        src = bank[sr, 2 + b].rearrange("p (r a t) -> p r a t", r=2, a=2)
                        g0 = SMALL["k_g"][0] + 1
                        gain = small[sr, g0:g0 + 2].rearrange("p (r a o) -> p r a o", a=1, o=1)
                        dst = kT[dr, :, src_half::2, tb_cols(b)]
                        dve.tensor_tensor(dst, src, gain.broadcast_to([64, 2, 2, P]), ALU.mult).then_inc(kq_out, 1)
            group_out(5)
            rstd(slice(24, 56), HD)
            for b in range(TB):
                v = proj[:, b, C_Q:C_Q + D_NSA].rearrange("p (h d) -> p h d", d=HD)
                s = stats[:, 24 + 16 * b:40 + 16 * b].rearrange("p (h o) -> p h o", o=1)
                dve.tensor_tensor(v, v, s.broadcast_to([P, HEADS, HD]), ALU.mult).then_inc(qn_ready, 1)
            group_out(6)
            for m in range(4):
                b, half = divmod(m, 2)
                dve.wait_ge(turned_kq, 3 + m)
                src = bank[:, m].rearrange("p (a t) -> p a t", a=4)
                dve.tensor_scalar(qT[:, 4 * half:4 * half + 4, tb_cols(b)], src, par("q_g"), HD ** -0.5,
                                  ALU.mult, ALU.mult).then_inc(kq_out, 1)

            dve.wait_ge(gelu_done, 4)
            for b in range(TB):
                v = proj[:, b, C_V:C_V + D_SG].rearrange("p (h c) -> p h c", c=P)
                mean = stats[:, 92 + 8 * b:100 + 8 * b]
                link(dve.tensor_reduce(mean, v, AX.X, ALU.add))
                link(dve.tensor_scalar(mean, mean, 1.0 / P, None, ALU.mult))
                link(dve.tensor_tensor(v, v, mean.rearrange("p (h o) -> p h o", o=1).broadcast_to([P, SG_HEADS, P]),
                                       ALU.subtract))
            group_out(7)
            for b in range(TB):
                for half in range(2):
                    v = proj[:, b, C_V + 512 * half:C_V + 512 * half + 512]
                    link(dve.tensor_tensor(scratch[:], v, v, ALU.mult))
                    a = 56 + 8 * b + 4 * half
                    link(dve.tensor_reduce(stats[:, a:a + 4], scratch[:].rearrange("p (h c) -> p h c", c=P),
                                           AX.X, ALU.add))
            rstd(slice(56, 72), P)
            dve.wait_ge(rows_ln, 32)
            for b in range(TB):
                v = proj[:, b, C_V:C_V + D_SG]
                vh = v.rearrange("p (h c) -> p h c", c=P)
                s = stats[:, 56 + 8 * b:64 + 8 * b].rearrange("p (h o) -> p h o", o=1)
                link(dve.tensor_tensor(vh, vh, s.broadcast_to([P, SG_HEADS, P]), ALU.mult))
                link(dve.tensor_tensor(v, v, lnG[:], ALU.mult))
                dve.tensor_tensor(v, v, lnB[:], ALU.add).then_inc(v_ready, 1)
            group_out(8)

            dve.wait_ge(hid_turned, 1)
            dve.wait_ge(hid_zero, 1)
            for kvi in range(2):
                src = bank[:, 0, kvi * 64:kvi * 64 + 64].rearrange("p (g o n) -> p g o n", g=KV, o=1)[:, :, :, 0:NCMP]
                dst = hid[:, kvi].rearrange("p g (r n) -> p g r n", n=32)[:, :, :, 0:NCMP]
                ins = dve.tensor_copy(dst, src.broadcast_to([P, KV, REP, NCMP]))
            ins.then_inc(hid_ready, 1)
            dve.wait_ge(gates_done, 1)
            link(dve.memset(kcT[:], 0.0))
            link(dve.memset(pc[:], 0.0))
            dve.wait_ge(cmp_done, 1)
            kc_src = bank[:, 1, 0:D_KV].rearrange("p (g d) -> p g d", d=HD)
            link(dve.tensor_copy(kcs[:], kc_src))
            own = con("own").rearrange("p (r o) -> p r o", o=1).broadcast_to([P, REP, HD])
            for g in range(KV):
                src = bank[:, 1, D_KV + g * HD:D_KV + (g + 1) * HD].rearrange("p (o d) -> p o d", o=1)
                ins = dve.tensor_tensor(vc_own[:, g], src.broadcast_to([P, REP, HD]), own, ALU.mult)
            link(ins)
            sq = scratch[:, 0:D_KV].rearrange("p (g d) -> p g d", d=HD)
            link(dve.tensor_tensor(sq, kcs[:], kcs[:], ALU.mult))
            link(dve.tensor_reduce(stats[:, 72:76], sq, AX.X, ALU.add))
            variance(slice(72, 76), HD)
            for h in range(SG_HEADS):
                dve.wait_ge(mixed_done, 2 * (h // 2) + 2)
                if h == 0:
                    dve.wait_ge(gelu_done, 8)
                src = bank[:, 4 + h // 2, (h % 2) * T:(h % 2 + 1) * T].rearrange("p (b c) -> p b c", b=TB)
                u = proj[:, :, C_U + h * P:C_U + (h + 1) * P]
                a = SMALL["sg_b"][0] + h
                dve.scalar_tensor_tensor(out=u, in0=src, scalar=small[:, a:a + 1], in1=u, op0=ALU.add,
                                         op1=ALU.mult).then_inc(sg_out, 1)

            rstd(slice(72, 76))
            s = stats[:, 72:76].rearrange("p (g o) -> p g o", o=1)
            dve.tensor_tensor(kcs[:], kcs[:], s.broadcast_to([P, KV, HD]), ALU.mult).then_inc(kc_ready, 1)
            dve.wait_ge(kc_turned, 1)
            k0 = SMALL["k_g"][0]
            for src_half in range(2):
                for dst_half in range(2):
                    sr, dr = slice(64 * src_half, 64 * src_half + 64), slice(64 * dst_half, 64 * dst_half + 64)
                    src = bank[sr, 0, 0:64].rearrange("p (a n) -> p a n", a=2)[:, :, 0:16]
                    cols = slice(16 * dst_half, 16 * dst_half + 16)
                    ins = dve.tensor_scalar(kcT[dr, src_half::2, cols], src, small[sr, k0:k0 + 1], None, ALU.mult)
            ins.then_inc(kc_out, 1)
            dve.wait_ge(gates_exp, 1)
            gates_all = gates[:].rearrange("p b n -> p (b n)")
            link(dve.tensor_scalar(gates_all, gates_all, 1.0, None, ALU.add))
            link(dve.reciprocal(gates_all, gates_all))
            g_cmp = gates[:, 0, 0:GATES:3]
            link(dve.tensor_scalar(g_cmp, g_cmp, con("seen"), None, ALU.mult))


            dve.wait_ge(squares_ready, TB + 2)
            variance(slice(84, 86), 1024)

            def scale_mix(b, c0, stat, k):
                v = proj[:, b, c0 + 512 * k:c0 + 512 * (k + 1)]
                g0 = (1024 if c0 == C_U else 0) + 512 * k
                return dve.scalar_tensor_tensor(out=v, in0=v, scalar=stats[:, stat:stat + 1], in1=row_g[:, g0:g0 + 512],
                                                op0=ALU.mult, op1=ALU.mult)

            dve.wait_ge(bias_in, 16)

            def cmp_softmax(b):
                nv = 7 if b == 0 else NCMP
                p = pc[:, :, 0:nv]
                st = stats[:, 108:124]
                st_o = st.rearrange("p (h o) -> p h o", o=1).broadcast_to([P, HEADS, nv])
                dve.wait_ge(cmp_scored, b + 1)
                if b:
                    dve.wait_ge(cmp_turned, b)
                src = bank[:, 7, 0:HEADS * 16].rearrange("p (h n) -> p h n", n=16)[:, :, 0:nv]
                link(dve.tensor_tensor(p, src, bias[:, :, 16 * (nv - 1)::-16], ALU.add))
                link(dve.tensor_reduce(st, p, AX.X, ALU.max))
                dve.tensor_tensor(p, p, st_o, ALU.subtract).then_inc(cmp_shifted, 1)

            def cmp_weigh(b):
                nv = 7 if b == 0 else NCMP
                p = pc[:, :, 0:nv]
                st = stats[:, 108:124]
                st_o = st.rearrange("p (h o) -> p h o", o=1).broadcast_to([P, HEADS, nv])
                dve.wait_ge(cmp_exp, b + 1)
                link(dve.tensor_reduce(st, p, AX.X, ALU.add))
                link(dve.reciprocal(st, st))
                link(dve.tensor_tensor(st, st, gates[:, b, 0:GATES:3], ALU.mult))
                dve.tensor_tensor(p, p, st_o, ALU.mult).then_inc(cmp_weighed, 1)

            def cmp_take(b):
                dve.wait_ge(cmp_turned, b + 1)
                if b:
                    dve.wait_ge(valued, HEADS)
                dve.tensor_copy(pcT[:].rearrange("p g t -> p (g t)"), bank[:, 7]).then_inc(cmp_out, 1)

            def bias_scores(u):
                b, h = divmod(u, HEADS)
                n = (b + 1) * P
                dve.wait_ge(scored, u + 1)
                if u >= 2:
                    dve.wait_ge(probs_ready, 2 * (u - 1))
                src = bank[:, u % 2, 0:2 * n].rearrange("p (r s) -> p r s", r=2)
                bb = bias[:, h, n - 1::-1].rearrange("p (o s) -> p o s", o=1).broadcast_to([P, 2, n])
                dst = biased[:, u % 2, :, 0:n]
                link(dve.tensor_tensor(dst, src, bb, ALU.add))
                dve.tensor_reduce(stats[:, 80 + 2 * (u % 2):82 + 2 * (u % 2)], dst, AX.X, ALU.max,
                                  negate=True).then_inc(biased_ready, 1)

            def scale_probs(u):
                b, h = divmod(u, HEADS)
                dve.wait_ge(probs_ready, 2 * (u + 1))
                w = branch_w[:, u % 2]
                link(dve.reciprocal(w, sums[:, b, :, h]))
                link(dve.tensor_tensor(w, w, gates[:, b, 3 * h + 1:3 * h + 3], ALU.mult))
                for r in range(2):
                    p = probs[:, u % 2, r, 0:(b + 1) * P]
                    dve.tensor_scalar(p, p, w[:, r:r + 1], None, ALU.mult).then_inc(probs_scaled, 1)

            def take_back(half):
                b, k = divmod(half, 2)
                dve.wait_ge(half_turned, half + 1)
                dve.tensor_copy(proj[:, b, C_Q + 512 * k:C_Q + 512 * k + 512], bank[:, 6]).then_inc(half_out, 1)

            for u in range(N_UNITS_ATT):
                if u % HEADS == 0:
                    cmp_softmax(u // HEADS)
                bias_scores(u)
                if u >= 1:
                    scale_probs(u - 1)
                if u % HEADS == 0:
                    cmp_weigh(u // HEADS)
                if u % HEADS == 2:
                    cmp_take(u // HEADS)
                if u % 8 == 5 and u > 8:
                    take_back(u // 8 - 1)
                if u == 5:
                    rstd(slice(84, 86))
                    dve.wait_ge(gain_in, 32)
                    for b in range(TB):
                        for k in range(2):
                            link(scale_mix(b, C_U, 84 + b, k))
                if u == HEADS + 8:
                    dve.wait_ge(squares_ready, TB + 3)
                    variance(slice(86, 87), 1024)
                if u == HEADS + 10:
                    rstd(slice(86, 87))
                    for k in range(2):
                        scale_mix(0, C_Q, 86, k).then_inc(rows_scaled, 2)
            scale_probs(N_UNITS_ATT - 1)
            take_back(3)

            dve.wait_ge(squares_ready, TB + 4)
            rstd(slice(87, 88), 1024)
            for k in range(2):
                scale_mix(1, C_Q, 87, k).then_inc(rows_scaled, 1 + 2 * k)
            take_lo(8)
            for k in range(G_OUT):
                G = G_IN + k
                dve.wait_ge(parts_used, DC * (G + 1))
                for b in range(TB):
                    xc = xs[:, b, k * PART:(k + 1) * PART]
                    ins = dve.tensor_tensor(xc, bank[:, 4 + 2 * (G % 2) + b], xc, ALU.add)
                    if b == 0:
                        link(ins)
                ins.then_inc(group_out_dve, 1)
            dve.wait_ge(squares_ready, TB + 4 + TB * G_OUT)
            link(dve.tensor_reduce(stats[:, 88:90], stats[:, 92:100].rearrange("p (b k) -> p b k", b=TB),
                                   AX.X, ALU.add))
            variance(slice(88, 90), D)
            dve.wait_ge(root_ready, roots[0])
            dve.reciprocal(stats[:, 88:90], stats[:, 88:90]).then_inc(norm_ready, 1)
            dve.wait_ge(norm_ready, 3)
            dve.wait_ge(gain_in, 48)
            for k in range(4):
                at = slice(k * 512, (k + 1) * 512)
                dve.scalar_tensor_tensor(out=hn[:, 0, at], in0=xs[:, 0, at], scalar=stats[:, 88:89],
                                         in1=row_g[:, at], op0=ALU.mult, op1=ALU.mult).then_inc(rows_scaled, 1)
            take_lo(16)
            for k in range(G_QUERY):
                dve.wait_ge(parts_used, N_QUERY + DC * (k + 1))
                if k >= 2:
                    dve.wait_ge(keyed, k - 1)
                dve.tensor_copy(queryT[:, k % 2, 2:4].rearrange("p j t -> p (j t)"), bank[:, 5 + 2 * (k % 2)])\
                   .then_inc(query_out_dve, 1)
                dve.wait_ge(keyed, k + 1)
                dve.tensor_copy(scores[:, 8 + 2 * k:10 + 2 * k].rearrange("p u a k -> p (u a k)"), bank[:, 1])\
                   .then_inc(keyed_out_dve, 1)

            dve.wait_ge(keyed_out_act, G_QUERY)
            dve.wait_ge(keyed_out_dve, G_QUERY)

            iota16 = con("iota")[:, 0:TOPK].rearrange("p (a m) -> p a m", a=1)

            def choose(u):
                link_choice(dve.tensor_copy(sc[:].rearrange("p a k -> p (a k)"),
                                     scores[:].rearrange("p u a k -> p (u a k)")[:, bass.ds(u * (2 * KEYS), 2 * KEYS)]))
                for a in range(2):
                    link_choice(dve.max(best[:, a, 0:8], sc[:, a]))
                    link_choice(dve.match_replace(sc_rest[:, a], best[:, a, 0:8], sc[:, a], -3.0e38))
                    link_choice(dve.max(best[:, a, 8:16], sc_rest[:, a]))
                    link_choice(dve.max_index(best_at[:, a, 0:8], best[:, a, 0:8], sc[:, a]))
                    link_choice(dve.max_index(best_at[:, a, 8:16], best[:, a, 8:16], sc_rest[:, a]))
                link_choice(dve.tensor_copy(best_f[:], best_at[:]))
                b1 = best[:, 0].rearrange("p (a o) -> p a o", o=1).broadcast_to([P, TOPK, TOPK])
                b2 = best[:, 1].rearrange("p (o b) -> p o b", o=1).broadcast_to([P, TOPK, TOPK])
                link_choice(dve.tensor_tensor(cand[:], b1, b2, ALU.add))
                flat = cand[:].rearrange("p a b -> p (a b)")
                link_choice(dve.max(chosen[:, 2, 0:8], flat))
                link_choice(dve.match_replace(cand_rest[:], chosen[:, 2, 0:8], flat, -3.0e38))
                link_choice(dve.max(chosen[:, 2, 8:16], cand_rest[:]))
                link_choice(dve.max_index(pos[:, 0:8], chosen[:, 2, 0:8], flat))
                link_choice(dve.max_index(pos[:, 8:16], chosen[:, 2, 8:16], cand_rest[:]))
                dve.tensor_scalar(pos2[:, 0], pos[:], 4, None, ALU.logical_shift_right)
                link_choice(dve.tensor_scalar(pos2[:, 1], pos[:], 15, None, ALU.bitwise_and))
                link_choice(dve.tensor_copy(pos_f[:], pos2[:]))
                for a in range(2):
                    at = pos_f[:, a].rearrange("p (j o) -> p j o", o=1).broadcast_to([P, TOPK, TOPK])
                    link_choice(dve.tensor_tensor(hit[:, a], at, iota16.broadcast_to([P, TOPK, TOPK]), ALU.is_equal))
                    val = best_f[:, a].rearrange("p (o m) -> p o m", o=1).broadcast_to([P, TOPK, TOPK])
                    link_choice(dve.tensor_tensor(hit[:, a], hit[:, a], val, ALU.mult))
                link_choice(dve.tensor_reduce(chosen[:, 0:2], hit[:], AX.X, ALU.add))
                dve.tensor_copy(picked[:, :, bass.ds(u * TOPK, TOPK)], chosen[:]).then_inc(dve_step, 1)
                dve.sem_clear(choice_step)
                choice[0] = 0

            before = step[0]
            with dve.Fori(0, UNITS) as u:
                choose(u)
                dve.wait_ge(dve_step, u + (before + 1))
            step[0] = before + UNITS

            units_v = lambda t: t.rearrange("p (u k) -> p u k", k=TOPK)
            s_all = units_v(picked[:, 2])
            top = s_all[:, :, 0:1].broadcast_to([P, UNITS, TOPK])
            dve.tensor_tensor(units_v(soft[:]), s_all, top, ALU.subtract).then_inc(soft_shifted, 1)
            dve.wait_ge(soft_exp, 1)
            st = stats[:, 108:124]
            link(dve.tensor_reduce(st, units_v(soft[:]), AX.X, ALU.add))
            link(dve.reciprocal(st, st))
            dve.tensor_tensor(units_v(soft[:]), units_v(soft[:]),
                              st.rearrange("p (u o) -> p u o", o=1).broadcast_to([P, UNITS, TOPK]), ALU.mult)\
               .then_inc(weights_ready, 1)
            dve.wait_ge(slots_turned, 1)
            dve.tensor_copy(slotsT[:, 0:2].rearrange("p a t -> p (a t)"), bank[:, 0]).then_inc(spread_free, 1)
            dve.tensor_copy(slotsT[:, 2], bank[:, 1, 0:T]).then_inc(spread_free, 1)
            dve.wait_ge(spread_free, 2)

            def one_hots(e, token):
                for j in range(4):
                    ins = dve.tensor_scalar(one_i1[:, e, j, :], con("iota"), slotsT[:, 0, bass.ds(token + j, 1)],
                                            slotsT[:, 2, bass.ds(token + j, 1)], ALU.is_equal, ALU.mult)
                ins.then_inc(one_i1_ready, 1)
                at = slotsT[:, 1, bass.ds(token, 4)].rearrange("p (j o) -> p j o", o=1).broadcast_to([P, 4, P])
                keys = con("iota").rearrange("p (o k) -> p o k", o=1).broadcast_to([P, 4, P])
                ins = dve.tensor_tensor(one_i2[:, e], at, keys, ALU.is_equal)
                ins.then_inc(one_i2_ready, 1)

            def weigh_early(g, e):
                dve.wait_ge(spread_done, g + 1)
                src = bank[:, e].rearrange("p (t k) -> p k t", t=4)
                at = spread[:, 0:EARLY, bass.ds(g * 4, 4)]
                dve.tensor_tensor(at, src[:, 0:EARLY, :], at, ALU.mult).then_inc(spread_weighed, 1)

            dve.wait_ge(u_out, EARLY)
            for e in range(2):
                one_hots(e, 4 * e)
            with dve.Fori(1, T // 8) as i:
                for e in range(2):
                    weigh_early(i * 2 + (e - 2), e)
                    one_hots(e, i * 8 + 4 * e)
            for e in range(2):
                weigh_early(T // 4 - 2 + e, e)

            def rest_at(n, i):
                dve.wait_ge(hi_ready, i * 8 + (n + 1))
                dve.tensor_tensor(lo[n % SPLIT][:], raw[n // 2 % RAW][:, n % 2 * PART:(n % 2 + 1) * PART],
                                  hi[n % SPLIT][:].bitcast(F32), ALU.subtract).then_inc(late_lo_ready, 1)

            def weigh(j, s):
                dve.wait_ge(u_out, j + 1)
                at = spread[:, bass.ds(j, 1), :].rearrange("p o t -> p (o t)")
                dve.tensor_tensor(at, at, acted[:, s, :], ALU.mult).then_inc(u_weighed, 1)

            for r in range(4):
                rest_at(N_LATE + r, 0)
            dve.wait_ge(spread_free, T // 4 + 2)
            for t in range(HELD):
                weigh(EARLY + t, t % 2)
                if t in (3, 6, 9):
                    rest_at(N_LATE + 4 + t // 3 - 1, 0)
            weigh(LATE, 0)
            rest_at(N_LATE + 7, 0)

            def late_tile(i, s):
                for r in range(3):
                    rest_at(N_U + 4 * s + 4 + r, i)
                weigh(i * 2 + s, s)
                rest_at(N_U + 4 * s + 7, i)

            late_tile(LATE // 2, 1)
            with dve.Fori(LATE // 2 + 1, KEYS // 2) as i:
                for s in range(2):
                    late_tile(i, s)

            def column_lo(s, j):
                dve.wait_ge(wcol_hi_ready, j + 1)
                at = spread[:, bass.ds(j, 1), :].rearrange("p o t -> p (o t)")
                dve.tensor_tensor(wcol_lo[s][:], at, wcol_hi[s][:].bitcast(F32), ALU.subtract).then_inc(wcol_ready, 1)

            for s in range(2):
                column_lo(s, s)
            with dve.Fori(0, KEYS // 2 - 1) as i:
                for s in range(2):
                    for c in range(4):
                        rest_at(N_V + 4 * s + 4 + c, i)
                    column_lo(s, i * 2 + (s + 2))
            for c in range(4):
                rest_at(N_V + 4 * (KEYS - 1) + c, 0)
            dve.wait_ge(resid_in, 16)
            for c in range(4):
                dve.wait_ge(parts_used, N_V + 4 * (KEYS - 1) + c + 1)
                for b in range(TB):
                    xc = resid[:, b, c * 512:(c + 1) * 512]
                    dve.tensor_tensor(xc, bank[:, 4 * b + c], xc, ALU.add).then_inc(out_ready, 1)

        @block.gpsimd
        def _(pool):
            def gain_second(dst, n):
                for k in range(4):
                    at = slice(k * 512, (k + 1) * 512)
                    pool.wait_ge(rows_normed, 4 * (n - 1) + k + 1)
                    pool.tensor_tensor(dst[:, 1, at], dst[:, 1, at], row_g[:, at], ALU.mult).then_inc(rows_scaled_pool, 1)

            pool.wait_ge(gain_in, 16)
            gain_second(h0, 1)
            pool.wait_ge(small_in_s, 16)
            pool.wait_ge(const_in_s, 16)
            w_s = par("sg_w").rearrange("p (h t) -> p h t", h=SG_HEADS)
            causal = con("causal").rearrange("p (o t) -> p o t", o=1).broadcast_to([P, SG_HEADS, P])
            pool.tensor_tensor(w_s, w_s, causal, ALU.mult).then_inc(sgw_ready, 1)

            pool.wait_ge(rows_scaled, 4)
            pool.wait_ge(rows_scaled_pool, 4)
            pool.memset(hid[:].rearrange("p k g n -> p (k g n)"), 0.0).then_inc(hid_zero, 1)

            def rest(i, k):
                pool.wait_ge(hi_ready, i * 8 + (k + 1))
                pool.tensor_tensor(lo[k % SPLIT][:], raw[k // 2][:, k % 2 * PART:(k % 2 + 1) * PART],
                                   hi[k % SPLIT][:].bitcast(F32), ALU.subtract).then_inc(lo_ready, 1)

            def rests(first, last):
                with pool.Fori(first // 8, last // 8) as i:
                    for k in range(8):
                        rest(i, k)

            rests(0, N_QUERY)
            for k in range(4):
                rest(N_QUERY // 8, k)
            pool.wait_ge(gain_in, 48)
            gain_second(hn, 2)
            for k in range(4, 8):
                rest(N_QUERY // 8, k)
            rests(N_QUERY + 8, N_LATE)


def bucket_of(distance):
    if distance < BUCKETS // 2:
        return distance
    edges = (16, 21, 27, 35, 46, 59, 77, 99, 128, 166, 216)
    return BUCKETS // 2 - 1 + sum(distance >= e for e in edges)


def constants():
    import numpy as np

    c = np.zeros((P, CONST_N), np.float32)

    def put(name, a):
        c[:a.shape[0], CONST[name][0]:CONST[name][0] + a.shape[1]] = a

    put("eye", np.eye(P, dtype=np.float32))
    put("iota", np.tile(np.arange(P, dtype=np.float32), (P, 1)))
    put("causal", np.triu(np.ones((P, P), np.float32)))
    put("own", np.repeat(np.eye(REP, dtype=np.float32), 32, axis=0))
    put("seen", (np.arange(P) >= CMP_BLOCK - 1).astype(np.float32)[:, None])
    one = np.zeros((BUCKETS + 1, SPAN), np.float32)
    for m in range(SPAN):
        one[bucket_of(m - (P - 1)) if m >= P - 1 else BUCKETS, m] = 1.0
    put("bucket", one)
    return c


def kernel(x, attn_norm_g, w_in, q_norm_g, k_norm_g, cmp_pe_k, cmp_w1_k, cmp_w2_k, cmp_pe_v, cmp_w1_v, cmp_w2_v,
           rel_bias, sg_ln_g, sg_ln_b, sg_w, sg_b, out_norm_nsa, out_norm_sg, w_out, ffn_norm_g, peer_w_query,
           peer_sub_keys, peer_u, peer_v):
    import numpy as np
    import concourse.bacc as bacc
    from concourse.bass_utils import run_bass_kernel_spmd

    def halves(w):
        n = w.shape[1] // PART
        t = w.reshape(DC // 2, 2, P, n, PART).transpose(3, 0, 2, 1, 4)
        return t.reshape(n * DC // 2, P, HALF)

    def cmp_halves(w1):
        t = w1.reshape(KV, 2, 8, 2, HD, P).transpose(0, 1, 3, 4, 2, 5)
        return t.reshape(2 * KV, P, HALF)

    w_in, w_out, w_query = (np.asarray(w) for w in (w_in, w_out, peer_w_query))
    q_end = D_NSA
    kv_end = q_end + 6 * D_KV
    g_end = kv_end + GATES
    u_end = g_end + D_SG
    main = np.concatenate([w_in[:, q_end:kv_end], w_in[:, :q_end], w_in[:, u_end:], w_in[:, g_end:u_end]], axis=1)
    tiles = np.concatenate([halves(main), halves(w_out), halves(w_query)], axis=0)
    u_tiles = np.asarray(peer_u).reshape(KEYS, KEYS, 2, 8, P).transpose(1, 2, 4, 3, 0).reshape(2 * KEYS, P, HALF)

    small = np.zeros((P, SMALL_N), np.float32)

    def put(name, a):
        small[:a.shape[0], SMALL[name][0]:SMALL[name][0] + a.shape[1]] = a

    put("q_g", np.tile(np.asarray(q_norm_g), 2)[:, None])
    put("k_g", np.tile(np.asarray(k_norm_g), (1, 2)).T)
    put("sg_b", np.asarray(sg_b).T)
    put("rel", np.concatenate([np.asarray(rel_bias), np.full((1, HEADS), NEG, np.float32)], axis=0))
    w2 = np.stack([np.asarray(cmp_w2_k), np.asarray(cmp_w2_v)])
    put("w2", w2.transpose(2, 0, 1, 3).reshape(P, -1))
    pe = np.stack([np.asarray(cmp_pe_k), np.asarray(cmp_pe_v)])
    put("pe", pe.reshape(2, CMP_BLOCK, 2, 2, HD).transpose(3, 4, 0, 2, 1).reshape(P, -1))
    put("subkeys", np.asarray(peer_sub_keys).transpose(2, 0, 1).reshape(P, -1))
    put("sg_w", np.asarray(sg_w).transpose(2, 0, 1).reshape(P, -1))
    put("w_gate", w_in[:, kv_end:g_end].reshape(DC, P, GATES).transpose(1, 0, 2).reshape(P, -1))

    arrays = {
        "x": np.asarray(x).reshape(T, D), "tiles": tiles,
        "cmp_tiles": np.concatenate([cmp_halves(np.asarray(cmp_w1_k)), cmp_halves(np.asarray(cmp_w1_v))]),
        "u_tiles": u_tiles, "peer_v": np.asarray(peer_v), "small": small, "const": constants(),
        "attn_g": np.asarray(attn_norm_g), "out_g": np.concatenate([np.asarray(out_norm_nsa), np.asarray(out_norm_sg)]),
        "ffn_g": np.asarray(ffn_norm_g),
        "ln_g": np.asarray(sg_ln_g).reshape(-1), "ln_b": np.asarray(sg_ln_b).reshape(-1),
    }
    arrays = {f"in_{k}": np.ascontiguousarray(v) for k, v in arrays.items()}
    nc = bacc.Bacc("TRN2", target_bir_lowering=False, num_devices=1)
    args = [nc.dram_tensor(k, v.shape, mybir.dt.from_np(v.dtype), kind="ExternalInput").ap() for k, v in arrays.items()]
    bias_rows = nc.dram_tensor("bias_rows", (HEADS, SPAN), F32, kind="Internal").ap()
    resid_dram = nc.dram_tensor("resid_dram", (T, D), F32, kind="Internal").ap()
    out = nc.dram_tensor("out", (T, D), F32, kind="ExternalOutput").ap()
    peer_layer(nc, *args, bias_rows, resid_dram, out)
    r = run_bass_kernel_spmd(nc, [arrays], core_ids=[0])
    return r.results[0]["out"].reshape(1, T, D)
```
